# Optimizing a Trainium2 kernel written in Bass

```python
import jax, jax.numpy as jnp
from jax import lax
import numpy as np

D_MODEL = 1024
BATCH = 1
SEQ = 128
DEPTH = 2
DEC_BATCH = 1
DEC_SEQ = 256
PAST_LEN = 128

GRID_W = 64
N_HEADS = 8
QK_NOPE = 64
QK_ROPE = 32
QK_DIM = QK_NOPE + QK_ROPE
V_DIM = 64
Q_LORA = 384
KV_LORA = 256
ROPE_THETA = 10000.0
Q_BLOCK = 128
LRU_WIDTH = 1024
LRU_BLOCKS = 8
LRU_BW = LRU_WIDTH // LRU_BLOCKS
CONV_W = 4
LRU_C = 8.0
FF_HIDDEN = -(-8 * D_MODEL // (3 * 256)) * 256
N_MOD = 6
EPS = 1e-6
OFF_KV = Q_LORA
OFF_KR = OFF_KV + KV_LORA
OFF_LX = OFF_KR + QK_ROPE
OFF_LG = OFF_LX + LRU_WIDTH
OFF_MG = OFF_LG + LRU_WIDTH
IN_COLS = OFF_MG + 2 * D_MODEL

kernel_name = "hybrid_mla_rglru_diffusion_step"

def rms_norm(x, g):
    xf = x.astype(jnp.float32)
    y = xf * lax.rsqrt(jnp.mean(xf * xf, axis=-1, keepdims=True) + EPS)
    return (y * g.astype(jnp.float32)).astype(x.dtype)

def axial_rope_tables(n_tokens):
    rows = n_tokens // GRID_W
    row = jnp.repeat(jnp.arange(rows, dtype=jnp.float32), GRID_W)
    col = jnp.tile(jnp.arange(GRID_W, dtype=jnp.float32), rows)
    n_freq = QK_ROPE // 4
    inv = ROPE_THETA ** (-jnp.arange(n_freq, dtype=jnp.float32) / n_freq)
    ang = jnp.concatenate([row[:, None] * inv, col[:, None] * inv], axis=-1)
    return jnp.cos(ang), jnp.sin(ang)

def apply_rope(x, cos, sin):
    half = QK_ROPE // 2
    x1 = x[..., :half].astype(jnp.float32)
    x2 = x[..., half:].astype(jnp.float32)
    return jnp.concatenate([x1 * cos - x2 * sin, x1 * sin + x2 * cos], axis=-1).astype(x.dtype)

def attend(q, k, v):
    b, lq, h, dk = q.shape
    nb = lq // Q_BLOCK
    qb = jnp.swapaxes(q.reshape(b, nb, Q_BLOCK, h, dk), 0, 1)
    scale = dk ** -0.5

    def block(qi):
        s = jnp.einsum("bqhd,bkhd->bhqk", qi, k, preferred_element_type=jnp.float32) * scale
        p = jax.nn.softmax(s, axis=-1).astype(v.dtype)
        return jnp.einsum("bhqk,bkhd->bqhd", p, v)

    o = lax.map(block, qb)
    return jnp.swapaxes(o, 0, 1).reshape(b, lq, h * v.shape[-1])

def centred_conv(x, w, b):
    L = x.shape[1]
    xp = jnp.pad(x, ((0, 0), (CONV_W // 2, CONV_W - 1 - CONV_W // 2), (0, 0)))
    out = b
    for t in range(CONV_W):
        out = out + xp[:, t:t + L] * w[t]
    return out

def block_diag(x, w, b):
    bsz, L, _ = x.shape
    y = jnp.einsum("blnd,nde->blne", x.reshape(bsz, L, LRU_BLOCKS, LRU_BW), w)
    return y.reshape(bsz, L, LRU_WIDTH) + b

def rg_lru_direction(x, w_rg, b_rg, w_ig, b_ig, lam, h0, reverse):
    r = jax.nn.sigmoid(block_diag(x, w_rg, b_rg).astype(jnp.float32))
    i = jax.nn.sigmoid(block_diag(x, w_ig, b_ig).astype(jnp.float32))
    log_a = -LRU_C * jax.nn.softplus(-lam.astype(jnp.float32)) * r
    a = jnp.exp(log_a)
    u = jnp.sqrt(-jnp.expm1(2.0 * log_a)) * i * x.astype(jnp.float32)

    def step(h, au):
        a_t, u_t = au
        h = a_t * h + u_t
        return h, h

    h_last, hs = lax.scan(step, h0.astype(jnp.float32),
                          (jnp.swapaxes(a, 0, 1), jnp.swapaxes(u, 0, 1)), reverse=reverse)
    return jnp.swapaxes(hs, 0, 1), h_last

def mixer(h, p, latent, ckv_ctx, krope_ctx, hf0, hb0):
    b, L, _ = h.shape
    proj = h @ p["w_in"]
    q_lat = proj[..., :OFF_KV]
    kv_lat = proj[..., OFF_KV:OFF_KR]
    k_rope = proj[..., OFF_KR:OFF_LX]
    lru_x = proj[..., OFF_LX:OFF_LG]
    lru_gate = proj[..., OFF_LG:OFF_MG]
    merge = proj[..., OFF_MG:]
    q = (rms_norm(q_lat, p["g_q"]) @ p["w_q_up"]).reshape(b, L, N_HEADS, QK_DIM)
    q_nope, q_rope = q[..., :QK_NOPE], q[..., QK_NOPE:]
    ckv = rms_norm(kv_lat, p["g_kv"])
    if latent:
        cos, sin = axial_rope_tables(L)
        q_rope = apply_rope(q_rope, cos[:, None, :], sin[:, None, :])
        k_rope = apply_rope(k_rope, cos, sin)
        ckv_keys = jnp.concatenate([ckv, ckv_ctx.astype(ckv.dtype)], axis=1)
        krope_keys = jnp.concatenate([k_rope, krope_ctx.astype(k_rope.dtype)], axis=1)
    else:
        ckv_keys, krope_keys = ckv, k_rope
    lk = ckv_keys.shape[1]
    kv = (ckv_keys @ p["w_kv_up"]).reshape(b, lk, N_HEADS, QK_NOPE + V_DIM)
    k = jnp.concatenate([kv[..., :QK_NOPE],
                         jnp.broadcast_to(krope_keys[:, :, None, :], (b, lk, N_HEADS, QK_ROPE))], axis=-1)
    v = kv[..., QK_NOPE:]
    q = jnp.concatenate([q_nope, q_rope], axis=-1)
    y_mla = attend(q, k, v) @ p["w_o_mla"]
    xc = centred_conv(lru_x, p["conv_w"], p["conv_b"])
    hf_seq, hf = rg_lru_direction(xc, p["w_rg"][0], p["b_rg"][0], p["w_ig"][0], p["b_ig"][0],
                                  p["lru_lambda"][0], hf0, False)
    hb_seq, hb = rg_lru_direction(xc, p["w_rg"][1], p["b_rg"][1], p["w_ig"][1], p["b_ig"][1],
                                  p["lru_lambda"][1], hb0, True)
    y_lru = ((hf_seq + hb_seq).astype(h.dtype) * jax.nn.gelu(lru_gate)) @ p["w_o_lru"]
    gates = jax.nn.sigmoid(merge.astype(jnp.float32)).astype(h.dtype)
    y = (gates[..., :D_MODEL] * y_mla + gates[..., D_MODEL:] * y_lru) @ p["w_out"]
    return y, ckv, k_rope, hf, hb

def swiglu(h, p):
    gu = h @ p["w_ffn_in"]
    return (jax.nn.silu(gu[..., :FF_HIDDEN]) * gu[..., FF_HIDDEN:]) @ p["w_ffn_out"]

def layer(x, mod, p, latent, ckv_ctx, krope_ctx, hf0, hb0):
    sh1, sc1, g1, sh2, sc2, g2 = jnp.split(mod, N_MOD, axis=-1)
    h = rms_norm(x, p["g_pre_mix"]) * (1.0 + sc1) + sh1
    y, ckv, krope, hf, hb = mixer(h, p, latent, ckv_ctx, krope_ctx, hf0, hb0)
    x = x + g1 * rms_norm(y, p["g_post_mix"])
    h = rms_norm(x, p["g_pre_ffn"]) * (1.0 + sc2) + sh2
    x = x + g2 * rms_norm(swiglu(h, p), p["g_post_ffn"])
    return x, ckv, krope, hf, hb

def setup_inputs(seed: int = 0) -> dict:
    key = jax.random.key(seed)
    ks = jax.random.split(key, 40)

    def nrm(k, shape, scale):
        return jax.random.normal(k, shape, jnp.float32) * scale

    a0 = jax.random.uniform(ks[30], (DEPTH, 2, LRU_WIDTH), jnp.float32, 0.9, 0.999)
    s0 = a0 ** (1.0 / LRU_C)
    lam = jnp.log(s0) - jnp.log1p(-s0)
    return {
        "x_prompt": nrm(ks[0], (BATCH, SEQ, D_MODEL), 1.0),
        "x_sample": nrm(ks[1], (DEC_BATCH, DEC_SEQ, D_MODEL), 1.0),
        "cache_ckv": nrm(ks[2], (DEC_BATCH, DEPTH, PAST_LEN, KV_LORA), 1.0),
        "cache_krope": nrm(ks[3], (DEC_BATCH, DEPTH, PAST_LEN, QK_ROPE), 1.0),
        "state_lru_fwd": nrm(ks[4], (DEC_BATCH, DEPTH, LRU_WIDTH), 0.5),
        "state_lru_bwd": nrm(ks[5], (DEC_BATCH, DEPTH, LRU_WIDTH), 0.5),
        "c": nrm(ks[6], (DEC_BATCH, D_MODEL), 1.0),
        "c_ctx": nrm(ks[7], (D_MODEL,), 1.0),
        "w_mod": nrm(ks[8], (DEPTH, D_MODEL, N_MOD * D_MODEL), 0.5 * D_MODEL ** -0.5),
        "b_mod": nrm(ks[9], (DEPTH, N_MOD * D_MODEL), 0.1),
        "g_pre_mix": 1.0 + nrm(ks[10], (DEPTH, D_MODEL), 0.05),
        "g_post_mix": 1.0 + nrm(ks[11], (DEPTH, D_MODEL), 0.05),
        "g_pre_ffn": 1.0 + nrm(ks[12], (DEPTH, D_MODEL), 0.05),
        "g_post_ffn": 1.0 + nrm(ks[13], (DEPTH, D_MODEL), 0.05),
        "w_in": nrm(ks[14], (DEPTH, D_MODEL, IN_COLS), D_MODEL ** -0.5),
        "g_q": 1.0 + nrm(ks[15], (DEPTH, Q_LORA), 0.05),
        "w_q_up": nrm(ks[16], (DEPTH, Q_LORA, N_HEADS * QK_DIM), Q_LORA ** -0.5),
        "g_kv": 1.0 + nrm(ks[17], (DEPTH, KV_LORA), 0.05),
        "w_kv_up": nrm(ks[18], (DEPTH, KV_LORA, N_HEADS * (QK_NOPE + V_DIM)), KV_LORA ** -0.5),
        "w_o_mla": nrm(ks[19], (DEPTH, N_HEADS * V_DIM, D_MODEL), (N_HEADS * V_DIM) ** -0.5),
        "conv_w": nrm(ks[20], (DEPTH, CONV_W, LRU_WIDTH), CONV_W ** -0.5),
        "conv_b": nrm(ks[21], (DEPTH, LRU_WIDTH), 0.02),
        "w_rg": nrm(ks[22], (DEPTH, 2, LRU_BLOCKS, LRU_BW, LRU_BW), LRU_BW ** -0.5),
        "b_rg": nrm(ks[23], (DEPTH, 2, LRU_WIDTH), 0.1),
        "w_ig": nrm(ks[24], (DEPTH, 2, LRU_BLOCKS, LRU_BW, LRU_BW), LRU_BW ** -0.5),
        "b_ig": nrm(ks[25], (DEPTH, 2, LRU_WIDTH), 0.1),
        "lru_lambda": lam,
        "w_o_lru": nrm(ks[26], (DEPTH, LRU_WIDTH, D_MODEL), LRU_WIDTH ** -0.5),
        "w_out": nrm(ks[27], (DEPTH, D_MODEL, D_MODEL), D_MODEL ** -0.5),
        "w_ffn_in": nrm(ks[28], (DEPTH, D_MODEL, 2 * FF_HIDDEN), D_MODEL ** -0.5),
        "w_ffn_out": nrm(ks[29], (DEPTH, FF_HIDDEN, D_MODEL), FF_HIDDEN ** -0.5),
    }

def reference(x_prompt, x_sample, cache_ckv, cache_krope, state_lru_fwd, state_lru_bwd, c, c_ctx,
              w_mod, b_mod, g_pre_mix, g_post_mix, g_pre_ffn, g_post_ffn, w_in, g_q, w_q_up, g_kv,
              w_kv_up, w_o_mla, conv_w, conv_b, w_rg, b_rg, w_ig, b_ig, lru_lambda, w_o_lru, w_out,
              w_ffn_in, w_ffn_out):
    def params(l):
        return {"g_pre_mix": g_pre_mix[l], "g_post_mix": g_post_mix[l], "g_pre_ffn": g_pre_ffn[l],
                "g_post_ffn": g_post_ffn[l], "w_in": w_in[l], "g_q": g_q[l], "w_q_up": w_q_up[l],
                "g_kv": g_kv[l], "w_kv_up": w_kv_up[l], "w_o_mla": w_o_mla[l], "conv_w": conv_w[l],
                "conv_b": conv_b[l], "w_rg": w_rg[l], "b_rg": b_rg[l], "w_ig": w_ig[l], "b_ig": b_ig[l],
                "lru_lambda": lru_lambda[l], "w_o_lru": w_o_lru[l], "w_out": w_out[l],
                "w_ffn_in": w_ffn_in[l], "w_ffn_out": w_ffn_out[l]}

    x = x_prompt
    bp = x_prompt.shape[0]
    zeros_state = jnp.zeros((bp, LRU_WIDTH), jnp.float32)
    ckvs, kropes, hfs, hbs = [], [], [], []
    for l in range(DEPTH):
        mod_ctx = jax.nn.silu(c_ctx) @ w_mod[l] + b_mod[l]
        x, ckv, krope, hf, hb = layer(x, mod_ctx, params(l), False, None, None, zeros_state, zeros_state)
        ckvs.append(ckv)
        kropes.append(krope)
        hfs.append(hf)
        hbs.append(hb)
    y_prompt = x
    new_ckv = jnp.stack(ckvs, axis=1).astype(x_prompt.dtype)
    new_krope = jnp.stack(kropes, axis=1).astype(x_prompt.dtype)
    new_lru_fwd = jnp.stack(hfs, axis=1).astype(x_prompt.dtype)
    new_lru_bwd = jnp.stack(hbs, axis=1).astype(x_prompt.dtype)

    x = x_sample
    for l in range(DEPTH):
        mod_lat = (jax.nn.silu(c) @ w_mod[l] + b_mod[l])[:, None, :]
        x, _, _, _, _ = layer(x, mod_lat, params(l), True, cache_ckv[:, l], cache_krope[:, l],
                              state_lru_fwd[:, l], state_lru_bwd[:, l])
    y_sample = x
    return (y_prompt, y_sample, new_ckv, new_krope, new_lru_fwd, new_lru_bwd)


_drawn_inputs = setup_inputs


def setup_inputs(seed=0):
    import zlib

    import numpy as np

    out = dict(_drawn_inputs(seed))
    spreads = {}
    factors = {'cache_ckv': 4.0, 'cache_krope': 7.963, 'g_post_ffn': 2.8, 'g_q': 8.0, 'b_rg': 3.504}
    for name, (base, spread) in spreads.items():
        noise = np.random.default_rng([zlib.crc32(name.encode()), seed]).standard_normal(out[name].shape)
        drawn = base * np.exp(spread * noise) if base else spread * noise
        out[name] = __import__('jax').numpy.asarray(drawn.astype(out[name].dtype))
    for name, factor in factors.items():
        out[name] = (out[name] * factor).astype(out[name].dtype)
    return out
```

```python
from contextlib import ExitStack

import numpy as np

import concourse.bass as bass
from concourse import mybir

P = 128
D = 1024
DEPTH = 2
PAST = 128
HEADS = 8
NOPE, ROPE, VD = 64, 32, 64
QK = NOPE + ROPE
QL, KVL = 384, 256
LRU = 1024
FF = 2816
NMOD = 6
GRID_W = 64
EPS = 1e-6
TP, TS = 128, 256
T = TP + TS
TK = T + PAST
C = D // P
FC = FF // P
QC, KC = QL // P, KVL // P
OFF_KV = QL
OFF_KR = OFF_KV + KVL
OFF_LX = OFF_KR + ROPE
OFF_LG = OFF_LX + LRU
OFF_MG = OFF_LG + LRU
SCALE = float(QK) ** -0.5
TINY = 1e-30

F = mybir.dt.float32
FR = mybir.dt.float32r
ALU = mybir.AluOpType
ACT = mybir.ActivationFunctionType
AX = mybir.AxisListType

GROUPS = ((0, slice(0, TP)), (1, slice(TP, T)))

ROWS_A = {}
ROWS_B = {}
for _rows, _names in ((ROWS_A, (("b_mod", NMOD * C), ("g_pre_mix", C), ("g_post_mix", C), ("g_pre_ffn", C),
                                ("g_post_ffn", C), ("conv_w", 4 * C), ("conv_b", C))),
                      (ROWS_B, (("b_rg", 2 * C), ("b_ig", 2 * C), ("lru_lambda", 2 * C), ("state_lru_fwd", C),
                                ("state_lru_bwd", C), ("g_q", QC), ("g_kv", KC)))):
    _at = 0
    for _n, _k in _names:
        _rows[_n] = (_at, _k)
        _at += _k
NA = sum(k for _, k in ROWS_A.values())
NB = sum(k for _, k in ROWS_B.values())


class Load:

    def __init__(self, job, kc, cols, split, parts):
        self.job, self.kc, self.cols, self.split, self.parts = job, kc, cols, split, parts


def plan_loads():
    loads = []

    def rows(job, name, k0, kc, c0, cols, split=True):
        loads.append(Load(job, kc, cols, split, [("rows", name, k0, kc, c0, cols, 0)]))

    def w(job, name, c0, cols=512, chunks=(4, 4)):
        k0 = 0
        for kc in chunks:
            rows(job, name, k0, kc, c0, cols)
            k0 += kc

    def mod(job, ranges):
        for r in ranges:
            for k0 in (0, 4):
                rows(job, "w_mod", k0, 4, r * 512, 512, split=False)

    def gates(b):
        loads.append(Load(f"gates{b}", 4, 512, True,
                          [("gate", name, d, 4 * b, (2 * i + d) * 512) for i, name in enumerate(("w_rg", "w_ig"))
                           for d in range(2)]))

    w("lx0", "w_in", OFF_LX)
    mod("mod01", range(4))
    w("lx1", "w_in", OFF_LX + 512)
    gates(0)
    w("gg0", "w_in", OFF_LG)
    w("gg1", "w_in", OFF_LG + 512)
    gates(1)
    w("qk", "w_in", 0)
    w("kr", "w_in", 512, 160)
    w("m2a", "w_in", OFF_MG + D)
    w("m2b", "w_in", OFF_MG + D + 512)
    w("m1a", "w_in", OFF_MG)
    w("m1b", "w_in", OFF_MG + 512)
    w("qn0", "w_q_up", 0, 4 * QK, (3,))
    w("qn1", "w_q_up", 4 * QK, 4 * QK, (3,))
    w("kv", "w_kv_up", 0, 1024, (1, 1))
    w("ol0", "w_o_lru", 0)
    w("ol1", "w_o_lru", 512)
    w("om0", "w_o_mla", 0, chunks=(4,))
    w("om1", "w_o_mla", 512, chunks=(4,))
    w("wo0", "w_out", 0)
    mod("mod2", (4, 5))
    w("wo1", "w_out", 512)
    for j in range(FC // 2):
        for k0 in (0, 4):
            loads.append(Load(f"fi{j}", 4, 512, True,
                              [("rows", "w_ffn_in", k0, 4, j * 256, 256, 0),
                               ("rows", "w_ffn_in", k0, 4, FF + j * 256, 256, 256)]))
        if j == 0:
            mod("mod34", (6, 7, 8, 9))
        if j == 6:
            mod("mod5", (10, 11))
    w("fo0", "w_ffn_out", 0, chunks=(4, 3, 3, 3, 3, 3, 3))
    w("fo1", "w_ffn_out", 512, chunks=(4, 3, 3, 3, 3, 3, 3))
    return loads


LOADS = plan_loads()
RAW = 2
SPL = 3
SPLIT = [n for n, x in enumerate(LOADS) if x.split]
SIDX = {n: i for i, n in enumerate(SPLIT)}
assert len(LOADS) % RAW == 0 and len(SPLIT) % SPL == 0, (len(LOADS), len(SPLIT))


def of_job(job):
    return [n for n, x in enumerate(LOADS) if x.job == job]


def pieces(load, dst, src):
    size = load.kc * load.cols
    if load.job[:2] not in ("qn", "kv"):
        return [(dst[:, 0:size], src[:, 0:size])]
    first, head = NOPE, QK if load.job[:2] == "qn" else NOPE + VD
    h = load.cols // head
    d = dst[:, 0:size].rearrange("p (k n) -> p k n", n=load.cols)
    s = src[:, 0:size].rearrange("p (k h e) -> p k h e", k=load.kc, h=h)
    return [(d[:, :, 0:h * first].rearrange("p k (h e) -> p k h e", h=h), s[:, :, :, 0:first]),
            (d[:, :, h * first:].rearrange("p k (h e) -> p k h e", h=h), s[:, :, :, first:])]


class Steps:

    def __init__(self, sem, labels, total):
        self.sem, self.known, self.total = sem, labels, total
        self.count, self.labels = 0, {}

    def step(self, *label, by=1):
        self.count += by
        if label:
            assert label not in self.labels, label
            self.labels[label] = self.count
        return self.sem, by

    def value(self, *label):
        return self.known[label] if self.known else 1

    def also(self, *label):
        self.labels[label] = self.count


def program(nc, A, plan):
    new_plan = {}
    with ExitStack() as ctx:
        def sb(name, shape, dt=F):
            return ctx.enter_context(nc.sbuf_tensor(name, shape, dt))

        def sem(name):
            return ctx.enter_context(nc.semaphore(name))

        def steps(name):
            labels, total = plan.get(name, ({}, 1))
            s = Steps(sem(name), labels, total)
            new_plan[name] = s
            return s

        raw = [sb(f"raw{s}", [P, 2048]) for s in range(RAW)]
        wh = [sb(f"weight_high{s}", [P, 2048], FR) for s in range(SPL)]
        wl = [sb(f"weight_low{s}", [P, 2048], FR) for s in range(SPL)]
        x = sb("x", [P, C, T])
        hh = sb("act_high", [P, C, T], FR)
        hl = sb("act_low", [P, C, T], FR)
        REGION = 2 * FC * T * 4
        arena_at = -(-nc.sbuf_base // 32) * 32
        sb("arena", [P, REGION // 4])
        ybuf = sb("ybuf", [P, C, T])
        qkv = sb("qkv", [P, 6, T])
        ident = sb("ident", [P, P])
        ones = sb("ones", [P, P])
        rot = sb("rot", [P, P])
        rep = sb("rep", [P, P])
        reprot = sb("reprot", [P, P])
        cos = sb("cos", [P, TS])
        sin = sb("sin", [P, TS])
        rows_a = sb("rows_a", [NA, P])
        rows_b = sb("rows_b", [NB, P])
        cache_c = sb("cache_c", [P, KVL])
        cache_k = sb("cache_k", [P, 4, ROPE])
        par = sb("par", [P, NA + NB])
        mod = sb("mod", [P, NMOD * C, 2])
        scale1 = sb("scale1", [P, C, 2])
        scale2 = sb("scale2", [P, C, 2])
        gain1 = sb("gain1", [P, C, 2])
        gain2 = sb("gain2", [P, C, 2])
        cs = sb("cs", [P, 2, C])
        lam = [sb(f"lam{i}", [P, 2 * C]) for i in range(6)]
        decay, ndecay = lam[4], lam[5]
        hst = sb("hst", [P, 2, C])
        epsc = sb("epsc", [P, 4])
        sq = [sb(f"sq{i}", [P, T]) for i in range(4)]
        t = [sb(f"t{i}", [P, T]) for i in range(2)]
        rstd = sb("rstd", [P, T])
        negmax = sb("negmax", [P, 2])
        psums = sb("psums", [P, 2])
        prec = sb("prec", [P, 2])

        def region(name, at, shape, dt=F):
            return nc.alloc_sbuf_tensor_at(name, shape, dt, offset=arena_at + at)

        TB = T * 4
        hidh = region("hid_high", 0, [P, FC, T], FR)
        hidl = region("hid_low", FC * TB, [P, FC, T], FR)
        xc = region("xc", 0, [P, C, T])
        xch = region("xc_high", C * TB, [P, 2, T], FR)
        xcl = region("xc_low", (C + 2) * TB, [P, 2, T], FR)
        r_ = region("lru_r", 12 * TB, [P, 2, 4, T])
        i_ = region("lru_i", 20 * TB, [P, 2, 4, T])
        tau = region("lru_tau", 28 * TB, [P, 2, 4, T])
        lruh = region("lru_h", 36 * TB, [P, C, T])
        m2 = region("merge_lru", 12 * TB, [P, C, T])
        m1 = region("merge_mla", 20 * TB, [P, C, T])
        qnh = region("qn_high", 0, [P, QC, T], FR)
        qnl = region("qn_low", QC * TB, [P, QC, T], FR)
        ch = region("ckv_high", 2 * QC * TB, [P, KC, TK], FR)
        cl = region("ckv_low", 2 * QC * TB + KC * TK * 4, [P, KC, TK], FR)
        oh = region("o_high", 0, [P, 4, T], FR)
        ol = region("o_low", 4 * TB, [P, 4, T], FR)
        kt = region("k_nope", 28 * TB, [P, 4, TK])
        kr = region("k_rope", 28 * TB + 4 * TK * 4, [P, TK])
        vv = region("v", 36 * TB, [P, 4, HEADS * VD])
        out_c = region("out_ckv", 36 * TB + 8192, [P, KVL])
        out_k = region("out_krope", 36 * TB + 8192 + 1024, [P, ROPE])
        out_h = region("out_state", 36 * TB + 8192 + 1152, [2 * C, P])
        qt = qkv[:, 0:4, :]
        qr = qkv[:, 4:6, :]

        ps = [ctx.enter_context(nc.psum_tensor(f"bank{i}", [P, 512], F)) for i in range(8)]

        tensor_done = steps("tensor_done")
        scalar_done = steps("scalar_done")
        vector_done = steps("vector_done")
        gpsimd_done = steps("gpsimd_done")
        raw_full = [steps(f"raw_full{s}") for s in range(RAW)]
        rows_full = steps("rows_full")
        cache_full = steps("cache_full")
        stored = steps("stored")
        PE, AC, VE, GP = tensor_done, scalar_done, vector_done, gpsimd_done
        sync_passed = sem("sync_passed")
        start_load = sem("start_load")
        start_pe = sem("start_pe")
        start_ve = sem("start_ve")
        start_ac = sem("start_ac")
        start_gp = sem("start_gp")
        end_pe = sem("end_pe")
        end_ve = sem("end_ve")
        end_store = sem("end_store")

        def in_layer(l):
            def at(s, *label, prev=False):
                return s.sem, l * s.total + s.value(*label) + (0 if prev else s.total)
            return at

        def last(l, s):
            return s.sem, l * s.total + s.count + s.total

        def par_col(name, i):
            rows, off = (ROWS_A, 0) if name in ROWS_A else (ROWS_B, NA)
            return par[:, off + rows[name][0] + i:off + rows[name][0] + i + 1]

        def par_cols(name):
            rows, off = (ROWS_A, 0) if name in ROWS_A else (ROWS_B, NA)
            return par[:, off + rows[name][0]:off + rows[name][0] + rows[name][1]]

        jobs = [("par", [(VE, "par", 1)]), ("mod01", [(VE, "mod", 3)]), ("st_pre1", [(AC, "rs", "pre1")]),
                ("lx0", [(VE, "conv", 3)]), ("lx1", [(VE, "conv", 7)])]
        jobs += [(f"gate{n}", [(AC, "gate", n)]) for n in range(4)]
        jobs += [("gg0", [(AC, "gelu", 3)]), ("gg1", [(AC, "gelu", 7)])]
        jobs += [(f"gate{n}", [(AC, "gate", n)]) for n in range(4, 8)]
        jobs += [("qk", [(AC, "qkv", 3)]), ("kr", [(AC, "qkv", 5)]), ("m2a", [(AC, "m2", 3)]),
                 ("st_qkv", [(AC, "rs", "kv")]), ("m2b", [(AC, "m2", 7)]), ("krot", [(VE, "krot")]),
                 ("m1a", [(AC, "m1", 3)]), ("cache", [(VE, "cache")]), ("m1b", [(AC, "m1", 7)]),
                 ("outs", [(AC, "outs")]),
                 ("qn0", [(AC, "qn", 2)]), ("qn1", [(AC, "qn", 5)]), ("kn", [(AC, "kn", 3)]), ("vv", [(AC, "vv", 3)]),
                 ("qrot", [(VE, "qrot")]),
                 ("ol0", [(VE, "mix_lru", 3)]), ("ol1", [(VE, "mix_lru", 7)]),
                 ("attnA", [(AC, "pt", 23)]), ("attnB", [(VE, "o_low", 3)]),
                 ("om0", [(VE, "mix", 3)]), ("om1", [(VE, "mix", 7)]), ("mod2", [(VE, "mod", 5)]),
                 ("wo0", [(AC, "ysq", "post1", 3)]), ("wo1", [(AC, "ysq", "post1", 7)]), ("st_post1", [(AC, "rs", "post1")]),
                 ("mod34", [(VE, "mod", 9)]), ("st_pre2", [(AC, "rs", "pre2")])]
        for j in range(FC // 2):
            if j == 6:
                jobs.append(("mod5", [(VE, "mod", 11)]))
            jobs.append((f"fi{j}", [(AC, "silu", 2 * j + 1), (VE, "hid", 2 * j + 1)]))
        jobs += [("fo0", [(AC, "ysq", "post2", 3)]), ("fo1", [(AC, "ysq", "post2", 7)]), ("st_post2", [(AC, "rs", "post2")])]
        names = [n for n, _ in jobs]
        if len(jobs) % 2:
            jobs.insert(names.index("attnA"), ("none", []))
            names = [n for n, _ in jobs]
        assert names.index("attnA") % 2 == 0 or True
        set_of = {n: i % 2 for i, (n, _) in enumerate(jobs)}

        def bank(job, b):
            return ps[4 * set_of[job] + b]

        def reads_before(job):
            i = names.index(job)
            k = i - 2
            while not jobs[k][1]:
                k -= 2
            return [(r, k < 0) for r in jobs[k][1]]

        block = ctx.enter_context(nc.Block())

        @block.sync
        def _(sp):
            consts = ((ident, "ident"), (rot, "rot"), (rep, "rep"), (reprot, "reprot"), (cos, "cos"), (sin, "sin"))
            for buf, name in consts:
                sp.dma_start(buf[:, :], A[name]).then_inc(start_load, 16)
            sp.dma_start(rows_b[0:C, :], A["c_ctx"].rearrange("(n p) -> n p", p=P)).then_inc(start_load, 16)
            sp.dma_start(rows_b[C:2 * C, :], A["c"].rearrange("b (n p) -> (b n) p", p=P)).then_inc(start_load, 16)
            tok = ybuf[:, :, :].rearrange("p c t -> p (c t)").rearrange("p (a d) -> p a d", d=D)
            sp.dma_start(tok[:, 0, :], A["x_prompt"].rearrange("b t d -> (b t) d")).then_inc(start_load, 16)
            sp.dma_start(tok[:, 1:3, :], A["x_sample"].rearrange("b (a p) d -> p (b a) d", p=P)).then_inc(start_load, 16)

            with sp.Fori(0, DEPTH) as l:
                at = in_layer(l)

                def vector_rows():
                    sp.wait_ge(*at(PE, "par", 1, prev=True))
                    sp.sem_inc(sync_passed, 1)
                    sp.wait_ge(start_pe, 2)
                    for dst, rows in ((rows_a, ROWS_A), (rows_b, ROWS_B)):
                        for name, (r0, k) in rows.items():
                            src = A[name]
                            if name.startswith("state"):
                                src = src[0:1, bass.ds(l, 1), :].rearrange("b a (n p) -> (b a n) p", p=P)
                            elif len(src.shape) == 3:
                                src = src[bass.ds(l, 1), :, :].rearrange("a w (n p) -> (a w n) p", p=P)
                            else:
                                src = src[bass.ds(l, 1), :].rearrange("a (n p) -> (a n) p", p=P)
                            sp.dma_start(dst[r0:r0 + k, :], src).then_inc(*rows_full.step(by=16))
                    rows_full.also("all")

                def cache_rows():
                    sp.wait_ge(*at(PE, "cache", prev=True))
                    sp.sem_inc(sync_passed, 1)
                    sp.dma_start(cache_c[:, :], A["cache_ckv"][0:1, bass.ds(l, 1), :, :].rearrange("b a t d -> (b a t) d")
                                 ).then_inc(*cache_full.step(by=16))
                    for q in range(4):
                        sp.dma_start(cache_k[:, q, :], A["cache_krope"][0:1, bass.ds(l, 1), :, :].rearrange(
                            "b a t d -> (b a t) d")).then_inc(*cache_full.step(by=16))
                    cache_full.also("all")

                def stores():
                    sp.wait_ge(*at(AC, "outs"))
                    sp.sem_inc(sync_passed, 1)
                    sp.dma_start(A["new_ckv"][0:1, bass.ds(l, 1), :, :].rearrange("b a t d -> (b a t) d"), out_c[:, :]
                                 ).then_inc(*stored.step(by=16))
                    sp.dma_start(A["new_krope"][0:1, bass.ds(l, 1), :, :].rearrange("b a t d -> (b a t) d"), out_k[:, :]
                                 ).then_inc(*stored.step(by=16))
                    for d, name in enumerate(("new_lru_fwd", "new_lru_bwd")):
                        sp.dma_start(A[name][0:1, bass.ds(l, 1), :].rearrange("b a (n p) -> (b a n) p", p=P),
                                     out_h[C * d:C * d + C, :]).then_inc(*stored.step(by=16))
                    stored.also("all")

                for n, load in enumerate(LOADS):
                    if n == 2:
                        vector_rows()
                    if n == of_job("gg0")[0]:
                        cache_rows()
                    if n == of_job("fi2")[0]:
                        stores()
                    m = (n - RAW) % len(LOADS)
                    if LOADS[m].split:
                        sp.wait_ge(*at(GP, "low", m, prev=n < RAW))
                        sp.sem_inc(sync_passed, 1)
                    else:
                        sp.wait_ge(*at(PE, "used", m, prev=n < RAW))
                        sp.sem_inc(sync_passed, 1)
                    full = raw_full[n % RAW]
                    for part in load.parts:
                        if part[0] == "rows":
                            _, name, k0, kc, c0, cols, o = part
                            dst = raw[n % RAW][:, 0:load.kc * load.cols].rearrange("p (k n) -> p k n", n=load.cols)
                            src = A[name][bass.ds(l, 1), k0 * P:(k0 + kc) * P, c0:c0 + cols]
                            sp.dma_start(dst[:, :, o:o + cols], src.rearrange("a (k p) n -> p (a k) n", p=P)
                                         ).then_inc(*full.step(by=16))
                        else:
                            _, name, d, n0, o = part
                            dst = raw[n % RAW][:, o:o + 512].rearrange("p (n e) -> p n e", e=P)
                            src = A[name][bass.ds(l, 1), d, n0:n0 + 4, :, :]
                            sp.dma_start(dst, src.rearrange("a n k e -> k (a n) e")).then_inc(*full.step(by=16))
                    full.also("load", n)

            sp.wait_ge(end_ve, 6)
            tok = ybuf[:, :, :].rearrange("p c t -> p (c t)").rearrange("p (a d) -> p a d", d=D)
            sp.dma_start(A["y_prompt"].rearrange("b t d -> (b t) d"), tok[:, 0, :]).then_inc(end_store, 16)
            sp.dma_start(A["y_sample"].rearrange("b (a p) d -> p (b a) d", p=P), tok[:, 1:3, :]).then_inc(end_store, 16)
            sp.wait_ge(end_store, 32)
            sp.wait_ge(stored.sem, DEPTH * stored.total + stored.total)

        @block.gpsimd
        def _(gp):
            nc.gpsimd.memset(ones[:, :], 1.0).then_inc(start_gp, 1)
            nc.gpsimd.memset(epsc[:, 0:1], EPS).then_inc(start_gp, 1)
            nc.gpsimd.memset(epsc[:, 1:2], TINY).then_inc(start_gp, 1)
            nc.gpsimd.memset(epsc[:, 2:3], float(0.5 * np.log(2.0))).then_inc(start_gp, 1)
            nc.gpsimd.memset(epsc[:, 3:4], 1.0).then_inc(start_gp, 1)
            gp.sem_inc(GP.sem, GP.total)
            for s in (*raw_full, rows_full, cache_full, stored):
                gp.sem_inc(s.sem, s.total)
            with gp.Fori(0, DEPTH) as l:
                at = in_layer(l)
                for m, n in enumerate(SPLIT):
                    gp.wait_ge(*at(AC, "high", n))
                    load = LOADS[n]
                    for (low, w), (high, _) in zip(pieces(load, wl[m % SPL], raw[n % RAW]), pieces(load, wh[m % SPL], raw[n % RAW])):
                        nc.gpsimd.tensor_tensor(low, w, high.bitcast(F), ALU.subtract).then_inc(*GP.step())
                    GP.also("low", n)

        @block.tensor
        def _(pe):
            def prologue():
                tok = ybuf[:, :, :].rearrange("p c t -> p (c t)").rearrange("p (a d) -> p a d", d=D)
                pe.wait_ge(start_load, 16 * 10)
                nc.tensor.transpose(ps[7][:, 0:2 * C], rows_b[0:2 * C, :], ident[0:2 * C, 0:2 * C]).then_inc(start_pe, 2)
                for c in range(C):
                    if c == 7:
                        pe.wait_ge(start_ac, 1)
                    for a in range(3):
                        ins = nc.tensor.transpose(ps[c][:, a * P:a * P + P], tok[:, a, c * P:c * P + P], ident[:, :])
                    ins.then_inc(start_pe, 1)

            prologue()
            pe.wait_ge(start_gp, 5)
            pe.wait_ge(start_ve, C)
            pe.wait_ge(start_ac, 1)
            pe.sem_inc(PE.sem, PE.total)
            with pe.Fori(0, DEPTH) as l:
                at = in_layer(l)

                def banks_free(job):
                    for (s, *label), prev in reads_before(job):
                        pe.wait_ge(*at(s, *label, prev=prev))

                def split_job(job, high, low, ready=None, groups=None, then=None):
                    banks_free(job)
                    loads = of_job(job)
                    k = 0
                    total = sum(LOADS[n].kc for n in loads)
                    for n in loads:
                        load = LOADS[n]
                        s = SIDX[n] % SPL
                        pe.wait_ge(*at(GP, "low", n))
                        view = [w[:, 0:load.kc * load.cols].rearrange("p (k n) -> p k n", n=load.cols) for w in (wh[s], wl[s])]
                        for kk in range(load.kc):
                            if ready is not None:
                                pe.wait_ge(*at(*ready, k))
                            gs = groups or [slice(g * P, g * P + P) for g in range(load.cols // P)]
                            for g, cols in enumerate(gs):
                                o = bank(job, g)[:, 0:T]
                                nc.tensor.matmul(o, view[0][:, kk, cols], high[:, k, :], start=k == 0, stop=False)
                                nc.tensor.matmul(o, view[0][:, kk, cols], low[:, k, :], start=False, stop=False)
                                ins = nc.tensor.matmul(o, view[1][:, kk, cols], high[:, k, :], start=False,
                                                       stop=k == total - 1)
                                if k == total - 1:
                                    ins.then_inc(*PE.step(job, g))
                                elif kk == load.kc - 1 and g == len(gs) - 1:
                                    ins.then_inc(*PE.step())
                            k += 1
                        PE.also("used", n)
                        if then is not None:
                            then(n)

                def mod_job(job):
                    banks_free(job)
                    for i, n in enumerate(of_job(job)):
                        pe.wait_ge(*at(raw_full[n % RAW], "load", n))
                        view = raw[n % RAW][:, :].rearrange("p (k n) -> p k n", n=512)
                        o = bank(job, i // 2)
                        for kk in range(4):
                            k = 4 * (i % 2) + kk
                            for g in range(4):
                                ins = nc.tensor.matmul(o[:, 2 * g:2 * g + 2], view[:, kk, g * P:g * P + P], cs[:, :, k],
                                                       start=k == 0 and g == 0, stop=k == C - 1, skip_group_check=True)
                        ins.then_inc(*PE.step("used", n))
                        if i % 2:
                            PE.also(job, i // 2)

                def stat(job, b, c, count, sqlabel):
                    pe.wait_ge(*at(AC, *sqlabel, c))
                    return nc.tensor.matmul(bank(job, b)[:, 0:T], ones[:, :], sq[c % 4][:, :], start=c == 0, stop=c == count - 1)

                banks_free("par")
                pe.wait_ge(*at(rows_full, "all"))
                nc.tensor.transpose(bank("par", 0)[:, 0:NA], rows_a[:, :], ident[0:NA, 0:NA]).then_inc(*PE.step("par", 0))
                nc.tensor.transpose(bank("par", 1)[:, 0:NB], rows_b[:, :], ident[0:NB, 0:NB]).then_inc(*PE.step("par", 1))
                mod_job("mod01")
                banks_free("st_pre1")
                for c in range(C):
                    stat("st_pre1", 0, c, C, ("sq", "pre1")).then_inc(*PE.step("st", "pre1", c))
                split_job("lx0", hh, hl, ready=(VE, "h", "pre1"))
                split_job("lx1", hh, hl)

                def gates(b):
                    (n,) = of_job(f"gates{b}")
                    s = SIDX[n] % SPL
                    pe.wait_ge(*at(GP, "low", n))
                    for j in range(4):
                        c = 4 * b + j
                        banks_free(f"gate{c}")
                        pe.wait_ge(*at(VE, "xc_low", c))
                        for q in range(4):
                            cols = slice(512 * q + P * j, 512 * q + P * j + P)
                            o = bank(f"gate{c}", q)[:, 0:T]
                            nc.tensor.matmul(o, wh[s][:, cols], xch[:, c % 2, :], start=True, stop=False)
                            nc.tensor.matmul(o, wh[s][:, cols], xcl[:, c % 2, :], start=False, stop=False)
                            nc.tensor.matmul(o, wl[s][:, cols], xch[:, c % 2, :], start=False, stop=True
                                             ).then_inc(*PE.step("gate", c, q))
                    PE.also("used", n)

                gates(0)
                split_job("gg0", hh, hl)
                split_job("gg1", hh, hl)
                gates(1)
                split_job("qk", hh, hl)
                split_job("kr", hh, hl, groups=[slice(0, P), slice(160 - P, 160)])
                split_job("m2a", hh, hl)
                banks_free("st_qkv")
                for c in range(QC):
                    pe.wait_ge(*at(AC, "sqq", c))
                    nc.tensor.matmul(bank("st_qkv", 0)[:, 0:T], ones[:, :], sq[c][:, :], start=c == 0, stop=c == QC - 1
                                     ).then_inc(*PE.step("stq", c))
                for c in range(KC):
                    pe.wait_ge(*at(AC, "sqq", QC + c))
                    nc.tensor.matmul(bank("st_qkv", 1)[:, 0:T], ones[:, :], (sq[3], t[1])[c][:, :], start=c == 0,
                                     stop=c == KC - 1).then_inc(*PE.step("stq", QC + c))
                split_job("m2b", hh, hl)
                banks_free("krot")
                tail = slice(P - ROPE, P)
                nc.tensor.matmul(bank("krot", 0)[:, 0:T], rep[tail, :], qkv[tail, 5, :], start=True, stop=True)
                nc.tensor.matmul(bank("krot", 1)[:, 0:TS], reprot[tail, :], qkv[tail, 5, TP:T], start=True, stop=True
                                 ).then_inc(*PE.step("krot"))
                split_job("m1a", hh, hl)
                banks_free("cache")
                pe.wait_ge(*at(cache_full, "all"))
                for k in range(KC):
                    nc.tensor.transpose(bank("cache", 0)[:, k * P:k * P + P], cache_c[:, k * P:k * P + P], ident[:, :])
                nc.tensor.transpose(bank("cache", 1)[:, 0:P], cache_k[:, :, :].rearrange("p q r -> p (q r)"), ident[:, :]
                                    ).then_inc(*PE.step("cache"))
                split_job("m1b", hh, hl)
                banks_free("outs")
                pe.wait_ge(*at(VE, "states"))
                pe.wait_ge(*at(VE, "ckv_full", KC - 1))
                for k in range(KC):
                    nc.tensor.transpose(bank("outs", 0)[:, k * P:k * P + P], qkv[:, QC + k, 0:TP], ident[:, :])
                nc.tensor.transpose(bank("outs", 1)[:, 0:P], qkv[:, QC + KC, 0:TP], ident[:, :])
                nc.tensor.transpose(bank("outs", 2)[0:2 * C, 0:P], hst[:, :, :].rearrange("p d c -> p (d c)"), ident[:, :]
                                    ).then_inc(*PE.step("outs"))
                for j in range(2):
                    job = f"qn{j}"
                    (n,) = of_job(job)
                    s = SIDX[n] % SPL
                    banks_free(job)
                    pe.wait_ge(*at(GP, "low", n))
                    views = [w[:, 0:QC * 4 * QK].rearrange("p (k n) -> p k n", k=QC) for w in (wh[s], wl[s])]
                    for k in range(QC):
                        pe.wait_ge(*at(VE, "qn", k))
                        for g in range(3):
                            w2 = [v[:, k, g * P:g * P + P] for v in views]
                            o = bank(job, g)[:, 0:T]
                            nc.tensor.matmul(o, w2[0], qnh[:, k, :], start=k == 0, stop=False)
                            nc.tensor.matmul(o, w2[0], qnl[:, k, :], start=False, stop=False)
                            ins = nc.tensor.matmul(o, w2[1], qnh[:, k, :], start=False, stop=k == QC - 1)
                            if k == QC - 1:
                                ins.then_inc(*PE.step("qn", 3 * j + g))
                    PE.also("used", n)
                loads = of_job("kv")
                banks_free("kn")
                pe.wait_ge(*at(VE, "ckv_cache"))
                for k, n in enumerate(loads):
                    s = SIDX[n] % SPL
                    pe.wait_ge(*at(GP, "low", n))
                    pe.wait_ge(*at(VE, "ckv", k))
                    for g in range(4):
                        w2 = [w[:, g * P:g * P + P] for w in (wh[s], wl[s])]
                        o = bank("kn", g)[:, :]
                        nc.tensor.matmul(o, w2[0], ch[:, k, :], start=k == 0, stop=False)
                        nc.tensor.matmul(o, w2[0], cl[:, k, :], start=False, stop=False)
                        ins = nc.tensor.matmul(o, w2[1], ch[:, k, :], start=False, stop=k == KC - 1)
                        if k == KC - 1:
                            ins.then_inc(*PE.step("kn", g))
                banks_free("vv")
                for g in range(4):
                    for k, n in enumerate(loads):
                        s = SIDX[n] % SPL
                        wvh, wvl = (w[:, HEADS * NOPE:HEADS * (NOPE + VD)] for w in (wh[s], wl[s]))
                        o = bank("vv", g)[:, :]
                        tk = slice(g * P, g * P + P)
                        nc.tensor.matmul(o, ch[:, k, tk], wvh, start=k == 0, stop=False)
                        nc.tensor.matmul(o, cl[:, k, tk], wvh, start=False, stop=False)
                        ins = nc.tensor.matmul(o, ch[:, k, tk], wvl, start=False, stop=k == KC - 1)
                    ins.then_inc(*PE.step("vv", g))
                for n in loads:
                    PE.also("used", n)
                banks_free("qrot")
                for j in range(2):
                    pe.wait_ge(*at(AC, "qn", 3 * j + 2))
                    nc.tensor.matmul(bank("qrot", j)[:, 0:TS], rot[:, :], qr[:, j, TP:T], start=True, stop=True
                                     ).then_inc(*PE.step("qrot", j))
                split_job("ol0", hh, hl, ready=(VE, "lru_low"))
                split_job("ol1", hh, hl)

                banks_free("attnA")
                banks_free("attnB")
                pe.wait_ge(*at(VE, "qrot"))
                pe.wait_ge(*at(AC, "vv", 3))

                def scores(s):
                    h, q = divmod(s, 3)
                    if s >= 2:
                        pe.wait_ge(*at(AC, "exp", s - 2))
                    keys = slice(0, TP) if q == 0 else slice(TP, TK)
                    qs = slice(q * P, q * P + P)
                    o = bank("attnA", s % 2)[:, 0:keys.stop - keys.start]
                    half, quad = slice(64 * (h % 2), 64 * (h % 2) + 64), slice(32 * (h % 4), 32 * (h % 4) + 32)
                    nc.tensor.matmul(o, qt[half, h // 2, qs], kt[half, h // 2, keys], start=True, stop=False)
                    nc.tensor.matmul(o, qr[quad, h // 4, qs], kr[quad, keys], start=False, stop=True
                                     ).then_inc(*PE.step("scores", s))

                def turn(s):
                    n = 1 if s % 3 == 0 else 3
                    if s >= 2:
                        pe.wait_ge(*at(AC, "pt", s - 2))
                    pe.wait_ge(*at(VE, "probs", s))
                    for k in range(n):
                        ins = nc.tensor.transpose(bank("attnA", 2 + s % 2)[:, k * P:k * P + P],
                                                  sq[s % 2][:, k * P:k * P + P], ident[:, :])
                    ins.then_inc(*PE.step("turn", s))

                def values(s):
                    h, q = divmod(s, 3)
                    tiles = (0,) if q == 0 else (1, 2, 3)
                    if h % 2 == 0 and h >= 4 and q == 0:
                        pe.wait_ge(*at(VE, "o_low", h // 2 - 2))
                    pe.wait_ge(*at(AC, "pt", s))
                    half = slice(64 * (h % 2), 64 * (h % 2) + 64)
                    o = bank("attnB", (h // 2) % 2)[half, q * P:q * P + P]
                    for j, k in enumerate(tiles):
                        ins = nc.tensor.matmul(o, vv[:, k, h * VD:h * VD + VD], sq[2 + s % 2][:, j * P:j * P + P],
                                               start=j == 0, stop=j == len(tiles) - 1)
                    ins.then_inc(*PE.step("values", s))

                scores(0)
                for s in range(24):
                    if s + 1 < 24:
                        scores(s + 1)
                    turn(s)
                    if s >= 1:
                        values(s - 1)
                values(23)
                split_job("om0", oh, ol, ready=(VE, "o_low"))
                split_job("om1", oh, ol)
                mod_job("mod2")
                split_job("wo0", hh, hl, ready=(VE, "mix_low"))

                def ysquares(which, chunks):
                    for c in chunks:
                        if c == 0:
                            banks_free(f"st_{which}")
                        stat(f"st_{which}", 0, c, C, ("ysq", which)).then_inc(*PE.step("st", which, c))

                first = of_job("wo1")[0]
                split_job("wo1", hh, hl, then=lambda n: ysquares("post1", range(4)) if n == first else None)
                ysquares("post1", range(4, C))
                mod_job("mod34")
                banks_free("st_pre2")
                for c in range(C):
                    stat("st_pre2", 0, c, C, ("sq", "pre2")).then_inc(*PE.step("st", "pre2", c))
                for j in range(FC // 2):
                    if j == 6:
                        mod_job("mod5")
                    split_job(f"fi{j}", hh, hl, ready=(VE, "h", "pre2") if j == 0 else None)
                split_job("fo0", hidh, hidl, ready=(VE, "hid_low"))
                first2 = of_job("fo1")[0]
                split_job("fo1", hidh, hidl, then=lambda n: ysquares("post2", range(4)) if n == first2 else None)
                ysquares("post2", range(4, C))

            pe.wait_ge(VE.sem, DEPTH * VE.total + VE.value("x", "post2", C - 1))
            for a in range(3):
                for c in range(C):
                    ins = nc.tensor.transpose(ps[2 * a + c // 4][:, (c % 4) * P:(c % 4) * P + P], x[:, c, a * P:a * P + P],
                                              ident[:, :])
                    if c % 4 == 3:
                        ins.then_inc(end_pe, 1)

        @block.scalar
        def _(ac):
            ac.wait_ge(start_pe, 2)
            nc.scalar.activation(cs[:, :, :].rearrange("p g c -> p (g c)"), ps[7][:, 0:2 * C], ACT.Silu).then_inc(start_ac, 1)
            ac.wait_ge(start_gp, 5)
            ac.wait_ge(start_ve, C)
            ac.sem_inc(AC.sem, AC.total)
            with ac.Fori(0, DEPTH) as l:
                at = in_layer(l)
                made = [0]

                def highs(job, ahead=2):
                    upto = SIDX[of_job(job)[-1]] + ahead
                    while made[0] <= min(upto, len(SPLIT) - 1):
                        m = made[0]
                        n = SPLIT[m]
                        ac.wait_ge(*at(raw_full[n % RAW], "load", n))
                        ac.wait_ge(*at(PE, "used", SPLIT[m - SPL], prev=m < SPL))
                        for high, w in pieces(LOADS[n], wh[m % SPL], raw[n % RAW]):
                            nc.scalar.activation(high, w, ACT.Copy).then_inc(*AC.step())
                        AC.also("high", n)
                        made[0] += 1

                def squares(which, of, label, prev=False):
                    for c in range(C):
                        ac.wait_ge(*at(VE, *label, c, prev=prev))
                        if c >= 4:
                            ac.wait_ge(*at(PE, "st", which, c - 4))
                        nc.scalar.activation(sq[c % 4][:, :], of[:, c, :], ACT.Square).then_inc(*AC.step("sq", which, c))

                def inverse_root(which, src, n):
                    nc.scalar.activation(rstd[:, :], src[:, 0:T], ACT.Ln, scale=1.0 / n, bias=epsc[:, 0:1]
                                         ).then_inc(*AC.step("rs", which))
                    ac.wait_ge(*last(l, AC))
                    nc.scalar.activation(rstd[:, :], rstd[:, :], ACT.Exp, scale=-0.5).then_inc(*AC.step("rstd", which))

                def make_high(dst, src, label, *out):
                    ac.wait_ge(*label)
                    nc.scalar.activation(dst, src, ACT.Copy).then_inc(*AC.step(*out))

                highs("lx0", ahead=0)
                ac.wait_ge(*at(VE, "abslam"))
                nc.scalar.activation(lam[0][:, :], lam[1][:, :], ACT.Exp, scale=-1.0).then_inc(*AC.step("explam"))
                ac.wait_ge(*at(VE, "onelam"))
                nc.scalar.activation(lam[1][:, :], lam[2][:, :], ACT.Ln).then_inc(*AC.step("lnlam"))
                squares("pre1", x, ("x", "post2"), prev=True)
                ac.wait_ge(*at(PE, "st", "pre1", C - 1))
                ac.wait_ge(*at(VE, "x", "post2", C - 1, prev=True))
                inverse_root("pre1", bank("st_pre1", 0), D)
                for c in range(C):
                    make_high(hh[:, c, :], t[c % 2][:, :], at(VE, "hfull", "pre1", c), "hh", "pre1", c)

                highs("lx0")
                for c in range(C):
                    if c == 4:
                        highs("lx1")
                    ac.wait_ge(*at(PE, f"lx{c // 4}", c % 4))
                    nc.scalar.activation(xc[:, c, :], bank(f"lx{c // 4}", c % 4)[:, 0:T], ACT.Identity,
                                         scale=par_col("conv_w", 2 * C + c), bias=par_col("conv_b", c)
                                         ).then_inc(*AC.step("conv", c))
                    if c == 3:
                        for n in range(2):
                            make_high(xch[:, n, :], xc[:, n, :], at(VE, "conv", n), "xc_high", n)

                def lru_gates(b):
                    highs(f"gates{b}")
                    for j in range(4):
                        c = 4 * b + j
                        if c >= 2:
                            ac.wait_ge(*at(PE, "gate", c - 2, 3))
                            make_high(xch[:, c % 2, :], xc[:, c, :], at(VE, "conv", c), "xc_high", c)
                        if b == 1 and j == 0:
                            ac.wait_ge(*at(VE, "scan", 3))
                        for q in range(4):
                            ac.wait_ge(*at(PE, "gate", c, q))
                            dst = (r_ if q < 2 else i_)[:, q % 2, j, :]
                            nc.scalar.activation(dst, bank(f"gate{c}", q)[:, 0:T], ACT.Sigmoid,
                                                 bias=par_col("b_rg" if q < 2 else "b_ig", C * (q % 2) + c)
                                                 ).then_inc(*AC.step())
                        AC.also("gate", c)
                        ac.wait_ge(*last(l, AC))
                        for d in range(2):
                            nc.scalar.activation(tau[:, d, j, :], r_[:, d, j, :], ACT.Tanh,
                                                 scale=decay[:, C * d + c:C * d + c + 1]).then_inc(*AC.step())
                        AC.also("tau", c)

                def lru_coefficients(b):
                    ac.wait_ge(*last(l, AC))

                    def root(e):
                        d, j = e
                        ac.wait_ge(*at(VE, "lnroot", 4 * b + j, d))
                        nc.scalar.activation(tau[:, d, j, :], tau[:, d, j, :], ACT.Exp, scale=0.5, bias=epsc[:, 2:3]
                                             ).then_inc(*AC.step("root", 4 * b + j, d))

                    order = [(d, j) for j in range(4) for d in range(2)]
                    for e, (d, j) in enumerate(order):
                        c = 4 * b + j
                        if e >= 4:
                            ac.wait_ge(*at(VE, "lnroot", 4 * b + order[e - 4][1], order[e - 4][0]))
                        nc.scalar.activation(sq[e % 4][:, :], tau[:, d, j, :], ACT.Ln, bias=epsc[:, 1:2]).then_inc(*AC.step())
                        nc.scalar.activation(r_[:, d, j, :], r_[:, d, j, :], ACT.Exp,
                                             scale=ndecay[:, C * d + c:C * d + c + 1]).then_inc(*AC.step())
                        nc.scalar.activation(tau[:, d, j, :], tau[:, d, j, :], ACT.Ln, bias=epsc[:, 3:4]
                                             ).then_inc(*AC.step("lns", c, d))
                        if e >= 1:
                            root(order[e - 1])
                        if e == 4:
                            highs(("gg0", "qk")[b])
                    root(order[-1])

                lru_gates(0)
                lru_coefficients(0)
                for c in range(C):
                    if c % 4 == 0:
                        highs(f"gg{c // 4}")
                    ac.wait_ge(*at(PE, f"gg{c // 4}", c % 4))
                    nc.scalar.activation(ybuf[:, c, :], bank(f"gg{c // 4}", c % 4)[:, 0:T], ACT.Gelu_apprx_tanh
                                         ).then_inc(*AC.step("gelu", c))
                lru_gates(1)
                highs("qk")
                lru_coefficients(1)
                for c in range(6):
                    job, b = ("qk", c) if c < 4 else ("kr", c - 4)
                    if c == 4:
                        highs("kr")
                    ac.wait_ge(*at(PE, job, b))
                    if c < 5:
                        nc.scalar.activation((*sq, t[1])[c][:, :], bank(job, b)[:, 0:T], ACT.Square).then_inc(*AC.step("sqq", c))
                    nc.scalar.activation(qkv[:, c, :], bank(job, b)[:, 0:T], ACT.Copy).then_inc(*AC.step("qkv", c))
                ac.wait_ge(*at(VE, "scan", 7))

                def merge(job, dst, c0, label):
                    highs(job)
                    for b in range(4):
                        ac.wait_ge(*at(PE, job, b))
                        nc.scalar.activation(dst[:, c0 + b, :], bank(job, b)[:, 0:T], ACT.Sigmoid
                                             ).then_inc(*AC.step(label, c0 + b))

                merge("m2a", m2, 0, "m2")
                ac.wait_ge(*at(PE, "stq", QC - 1))
                inverse_root("q", bank("st_qkv", 0), QL)
                ac.wait_ge(*at(PE, "stq", QC + KC - 1))
                ac.wait_ge(*at(VE, "qfull"))
                inverse_root("kv", bank("st_qkv", 1), KVL)
                for k in range(QC):
                    make_high(qnh[:, k, :], qkv[:, k, :], at(VE, "qfull_c", k), "qn_high", k)
                for k in range(KC):
                    make_high(ch[:, k, 0:T], qkv[:, QC + k, :], at(VE, "ckv_full", k), "ckv_high", k)
                merge("m2b", m2, 4, "m2")
                merge("m1a", m1, 0, "m1")
                ac.wait_ge(*at(PE, "cache"))
                for k in range(KC):
                    nc.scalar.activation(ch[:, k, T:TK], bank("cache", 0)[:, k * P:k * P + P], ACT.Copy).then_inc(*AC.step())
                AC.also("cache_high")
                merge("m1b", m1, 4, "m1")
                for c in range(C):
                    make_high(hh[:, c, :], t[c % 2][:, :], at(VE, "lru_full", c), "lru_high", c)
                ac.wait_ge(*at(PE, "outs"))
                nc.scalar.activation(out_c[:, :], bank("outs", 0)[:, 0:KVL], ACT.Copy).then_inc(*AC.step())
                nc.scalar.activation(out_k[:, :], bank("outs", 1)[:, P - ROPE:P], ACT.Copy).then_inc(*AC.step())
                nc.scalar.activation(out_h[:, :], bank("outs", 2)[0:2 * C, 0:P], ACT.Copy).then_inc(*AC.step("outs"))
                highs("qn1")
                ac.wait_ge(*at(VE, "ckv", KC - 1))
                for j in range(2):
                    for g in range(3):
                        ac.wait_ge(*at(PE, "qn", 3 * j + g))
                        dst = qt[:, 2 * j + g, :] if g < 2 else qr[:, j, :]
                        nc.scalar.activation(dst, bank(f"qn{j}", g)[:, 0:T], ACT.Copy, scale=SCALE
                                             ).then_inc(*AC.step("qn", 3 * j + g))
                for g in range(4):
                    ac.wait_ge(*at(PE, "kn", g))
                    nc.scalar.activation(kt[:, g, :], bank("kn", g)[:, :], ACT.Copy).then_inc(*AC.step("kn", g))
                highs("kv")
                for g in range(4):
                    ac.wait_ge(*at(PE, "vv", g))
                    nc.scalar.activation(vv[:, g, :], bank("vv", g)[:, :], ACT.Copy).then_inc(*AC.step("vv", g))
                highs("ol1")

                def turned(s):
                    n = 1 if s % 3 == 0 else 3
                    ac.wait_ge(*at(PE, "turn", s))
                    if s >= 2:
                        ac.wait_ge(*at(PE, "values", s - 2))
                    nc.scalar.activation(sq[2 + s % 2][:, 0:n * P], bank("attnA", 2 + s % 2)[:, 0:n * P], ACT.Copy
                                         ).then_inc(*AC.step("pt", s))

                def out_high(g):
                    ac.wait_ge(*at(PE, "values", 6 * g + 5))
                    nc.scalar.activation(oh[:, g, :], bank("attnB", g % 2)[:, 0:T], ACT.Copy).then_inc(*AC.step("o_high", g))

                for s in range(24):
                    n = TP if s % 3 == 0 else TK - TP
                    ac.wait_ge(*at(VE, "max", s))
                    if s >= 2:
                        ac.wait_ge(*at(PE, "turn", s - 2))
                        ac.wait_ge(*at(VE, "probs", s - 2))
                    nc.scalar.activation(sq[s % 2][:, 0:n], bank("attnA", s % 2)[:, 0:n], ACT.Exp, bias=negmax[:, s % 2:s % 2 + 1],
                                         accum_out=psums[:, s % 2:s % 2 + 1]).then_inc(*AC.step("exp", s))
                    if s >= 1:
                        turned(s - 1)
                    if s >= 8 and (s - 8) % 6 == 0:
                        out_high((s - 8) // 6)
                turned(23)
                out_high(3)
                highs("om1")
                for c in range(C):
                    make_high(hh[:, c, :], ybuf[:, c, :], at(VE, "mix", c), "mix_high", c)

                def y_out(jobs2, which):
                    for c in range(C):
                        job = jobs2[c // 4]
                        if c % 4 == 0:
                            highs(job)
                        ac.wait_ge(*at(PE, job, c % 4))
                        nc.scalar.activation(ybuf[:, c, :], bank(job, c % 4)[:, 0:T], ACT.Copy).then_inc(*AC.step("y", which, c))
                        if c >= 4:
                            ac.wait_ge(*at(PE, "st", which, c - 4))
                        nc.scalar.activation(sq[c % 4][:, :], bank(job, c % 4)[:, 0:T], ACT.Square
                                             ).then_inc(*AC.step("ysq", which, c))
                    ac.wait_ge(*at(PE, "st", which, C - 1))
                    inverse_root(which, bank(f"st_{which}", 0), D)

                y_out(("wo0", "wo1"), "post1")
                squares("pre2", x, ("x", "post1"))
                ac.wait_ge(*at(PE, "st", "pre2", C - 1))
                inverse_root("pre2", bank("st_pre2", 0), D)
                for c in range(C):
                    make_high(hh[:, c, :], t[c % 2][:, :], at(VE, "hfull", "pre2", c), "hh", "pre2", c)
                for j in range(FC // 2):
                    highs(f"fi{j}")
                    for g in range(2):
                        c = 2 * j + g
                        ac.wait_ge(*at(PE, f"fi{j}", g))
                        if c >= 4:
                            ac.wait_ge(*at(VE, "hid", c - 4))
                        nc.scalar.activation(sq[c % 4][:, :], bank(f"fi{j}", g)[:, 0:T], ACT.Silu).then_inc(*AC.step("silu", c))
                    for g in range(2):
                        c = 2 * j + g
                        if c == 0:
                            ac.wait_ge(*at(PE, "om1", 3))
                        make_high(hidh[:, c, :], t[c % 2][:, :], at(VE, "hid", c), "hid_high", c)
                y_out(("fo0", "fo1"), "post2")

        @block.vector
        def _(ve):
            for c in range(C):
                ve.wait_ge(start_pe, 3 + c)
                nc.vector.tensor_copy(x[:, c, :], ps[c][:, 0:T]).then_inc(start_ve, 1)
            ve.wait_ge(start_load, 16 * 10)
            ve.wait_ge(start_ac, 1)
            ve.wait_ge(start_gp, 5)
            ve.wait_ge(start_ve, C)
            ve.sem_inc(VE.sem, VE.total)
            with ve.Fori(0, DEPTH) as l:
                at = in_layer(l)

                def own():
                    ve.wait_ge(*last(l, VE))

                def add_bias(job, ranges):
                    for b, r in enumerate(ranges):
                        ve.wait_ge(*at(PE, job, b))
                        o = bank(job, b)[:, 0:8].rearrange("p (g c) -> p g c", c=2)
                        bias = par[:, 4 * r:4 * r + 4].rearrange("p (g a) -> p g a", a=1).to_broadcast([P, 4, 2])
                        nc.vector.tensor_tensor(mod[:, 4 * r:4 * r + 4, :], o, bias, ALU.add).then_inc(*VE.step("mod", r))

                def vec2(name):
                    return par_cols(name).rearrange("p (g a) -> p g a", a=1).to_broadcast([P, C, 2])

                def gain(dst, m, name, one, label):
                    own()
                    nc.vector.scalar_tensor_tensor(out=dst[:, :, :], in0=mod[:, m * C:m * C + C, :], scalar=one, in1=vec2(name),
                                                   op0=ALU.add, op1=ALU.mult).then_inc(*VE.step(*label))

                def normalise(which, dst_scale, shift):
                    ve.wait_ge(*at(AC, "rstd", which))

                    def low(c):
                        ve.wait_ge(*at(AC, "hh", which, c))
                        nc.vector.tensor_tensor(hl[:, c, :], t[c % 2][:, :], hh[:, c, :].bitcast(F), ALU.subtract
                                                ).then_inc(*VE.step("h", which, c))

                    for c in range(C):
                        if c >= 2:
                            own()
                        nc.vector.tensor_tensor(t[c % 2][:, :], x[:, c, :], rstd[:, :], ALU.mult).then_inc(*VE.step())
                        own()
                        for g, toks in GROUPS:
                            nc.vector.tensor_scalar(t[c % 2][:, toks], t[c % 2][:, toks], dst_scale[:, c, g:g + 1],
                                                    mod[:, shift * C + c, g:g + 1], ALU.mult, ALU.add).then_inc(*VE.step())
                        VE.also("hfull", which, c)
                        if c >= 1:
                            low(c - 1)
                    low(C - 1)

                def residual(which, gains):
                    ve.wait_ge(*at(AC, "rstd", which))
                    nc.vector.tensor_tensor(t[0][:, :], ybuf[:, 0, :], rstd[:, :], ALU.mult).then_inc(*VE.step())
                    for c in range(C):
                        if c + 1 < C:
                            if c >= 1:
                                own()
                            nc.vector.tensor_tensor(t[(c + 1) % 2][:, :], ybuf[:, c + 1, :], rstd[:, :], ALU.mult
                                                    ).then_inc(*VE.step())
                        own()
                        for g, toks in GROUPS:
                            nc.vector.scalar_tensor_tensor(out=x[:, c, toks], in0=t[c % 2][:, toks], scalar=gains[:, c, g:g + 1],
                                                           in1=x[:, c, toks], op0=ALU.mult, op1=ALU.add).then_inc(*VE.step())
                        VE.also("x", which, c)

                ve.wait_ge(*at(PE, "par", 0))
                nc.vector.tensor_copy(par[:, 0:NA], bank("par", 0)[:, 0:NA]).then_inc(*VE.step("par", 0))
                ve.wait_ge(*at(PE, "par", 1))
                nc.vector.tensor_copy(par[:, NA:NA + NB], bank("par", 1)[:, 0:NB]).then_inc(*VE.step("par", 1))
                own()
                nc.vector.tensor_scalar(lam[3][:, :], par_cols("lru_lambda"), -1.0, None, ALU.mult).then_inc(*VE.step())
                own()
                nc.vector.tensor_tensor(lam[1][:, :], lam[3][:, :], par_cols("lru_lambda"), ALU.max).then_inc(*VE.step("abslam"))
                ve.wait_ge(*at(AC, "explam"))
                nc.vector.tensor_scalar(lam[2][:, :], lam[0][:, :], 1.0, None, ALU.add).then_inc(*VE.step("onelam"))
                ve.wait_ge(*at(AC, "lnlam"))
                own()
                nc.vector.tensor_scalar(lam[2][:, :], lam[2][:, :], -1.0, TINY, ALU.add, ALU.add).then_inc(*VE.step())
                nc.vector.tensor_scalar(lam[1][:, :], lam[1][:, :], TINY, None, ALU.add).then_inc(*VE.step())
                own()
                nc.vector.reciprocal(lam[2][:, :], lam[2][:, :]).then_inc(*VE.step())
                nc.vector.tensor_tensor(lam[0][:, :], lam[0][:, :], lam[1][:, :], ALU.mult).then_inc(*VE.step())
                own()
                nc.vector.tensor_tensor(lam[0][:, :], lam[0][:, :], lam[2][:, :], ALU.mult).then_inc(*VE.step())
                own()
                nc.vector.scalar_tensor_tensor(out=lam[3][:, :], in0=lam[3][:, :], scalar=0.0, in1=lam[0][:, :],
                                               op0=ALU.max, op1=ALU.add).then_inc(*VE.step())
                own()
                nc.vector.tensor_scalar(decay[:, :], lam[3][:, :], 8.0, None, ALU.mult).then_inc(*VE.step())
                nc.vector.tensor_scalar(ndecay[:, :], lam[3][:, :], -8.0, None, ALU.mult).then_inc(*VE.step("decay"))
                add_bias("mod01", range(4))
                gain(scale1, 1, "g_pre_mix", 1.0, ("scale1",))
                normalise("pre1", scale1, 0)

                def xc_low(c):
                    ve.wait_ge(*at(AC, "xc_high", c))
                    nc.vector.tensor_tensor(xcl[:, c % 2, :], xc[:, c, :], xch[:, c % 2, :].bitcast(F), ALU.subtract
                                            ).then_inc(*VE.step("xc_low", c))

                for c in range(C):
                    ve.wait_ge(*at(AC, "conv", c))
                    src = bank(f"lx{c // 4}", c % 4)
                    for i, (tap, off) in enumerate(((0, -2), (1, -1), (3, 1))):
                        for g, toks in GROUPS:
                            a, b = toks.start, toks.stop
                            dst = slice(a - min(off, 0), b - max(off, 0))
                            frm = slice(dst.start + off, dst.stop + off)
                            if i:
                                ve.wait_ge(VE.sem, l * VE.total + VE.count - 1 + VE.total)
                            nc.vector.scalar_tensor_tensor(out=xc[:, c, dst], in0=src[:, frm], scalar=par_col("conv_w", tap * C + c),
                                                           in1=xc[:, c, dst], op0=ALU.mult, op1=ALU.add).then_inc(*VE.step())
                    VE.also("conv", c)
                    if c == 3:
                        xc_low(0)
                        xc_low(1)

                def scans(c, j):
                    b = c // 4
                    for d in range(2):
                        ve.wait_ge(*at(AC, "root", c, d))
                        nc.vector.tensor_tensor(i_[:, d, j, :], i_[:, d, j, :], tau[:, d, j, :], ALU.mult).then_inc(*VE.step())
                    own()
                    for d in range(2):
                        nc.vector.tensor_tensor(i_[:, d, j, :], i_[:, d, j, :], xc[:, c, :], ALU.mult).then_inc(*VE.step())
                    own()
                    for g, toks in GROUPS:
                        init = 0.0 if g == 0 else par_col("state_lru_fwd", c)
                        nc.vector.tensor_tensor_scan(lruh[:, c, toks], r_[:, 0, j, toks], i_[:, 0, j, toks], init,
                                                     ALU.mult, ALU.add).then_inc(*VE.step())
                    for g, toks in GROUPS:
                        init = 0.0 if g == 0 else par_col("state_lru_bwd", c)
                        nc.vector.tensor_tensor_scan(tau[:, 1, j, toks][:, ::-1], r_[:, 1, j, toks][:, ::-1],
                                                     i_[:, 1, j, toks][:, ::-1], init, ALU.mult, ALU.add).then_inc(*VE.step())
                    own()
                    nc.vector.tensor_copy(hst[:, 0, c:c + 1], lruh[:, c, TP - 1:TP]).then_inc(*VE.step())
                    nc.vector.tensor_copy(hst[:, 1, c:c + 1], tau[:, 1, j, 0:1]).then_inc(*VE.step())
                    own()
                    nc.vector.tensor_tensor(lruh[:, c, :], lruh[:, c, :], tau[:, 1, j, :], ALU.add).then_inc(*VE.step("scan", c))

                def recurrence(b):
                    for j in range(4):
                        c = 4 * b + j
                        if c >= 2:
                            xc_low(c)
                    def lnroot(c, j, d, e):
                        ve.wait_ge(*at(AC, "lns", c, d))
                        nc.vector.tensor_tensor(tau[:, d, j, :], sq[e % 4][:, :], tau[:, d, j, :], ALU.subtract
                                                ).then_inc(*VE.step("lnroot", c, d))
                    for j in range(4):
                        for d in range(2):
                            lnroot(4 * b + j, j, d, 2 * j + d)
                        if j >= 1:
                            scans(4 * b + j - 1, j - 1)
                    scans(4 * b + 3, 3)

                recurrence(0)
                recurrence(1)
                VE.also("states")
                ve.wait_ge(*at(AC, "rstd", "q"))
                for k in range(QC):
                    nc.vector.scalar_tensor_tensor(out=qkv[:, k, :], in0=qkv[:, k, :], scalar=par_col("g_q", k), in1=rstd[:, :],
                                                   op0=ALU.mult, op1=ALU.mult).then_inc(*VE.step("qfull_c", k))
                VE.also("qfull")
                ve.wait_ge(*at(AC, "rstd", "kv"))
                for k in range(KC):
                    nc.vector.scalar_tensor_tensor(out=qkv[:, QC + k, :], in0=qkv[:, QC + k, :], scalar=par_col("g_kv", k),
                                                   in1=rstd[:, :], op0=ALU.mult, op1=ALU.mult).then_inc(*VE.step("ckv_full", k))
                for k in range(QC):
                    ve.wait_ge(*at(AC, "qn_high", k))
                    nc.vector.tensor_tensor(qnl[:, k, :], qkv[:, k, :], qnh[:, k, :].bitcast(F), ALU.subtract
                                            ).then_inc(*VE.step("qn", k))
                for k in range(KC):
                    ve.wait_ge(*at(AC, "ckv_high", k))
                    nc.vector.tensor_tensor(cl[:, k, 0:T], qkv[:, QC + k, :], ch[:, k, 0:T].bitcast(F), ALU.subtract
                                            ).then_inc(*VE.step("ckv", k))
                ve.wait_ge(*at(PE, "krot"))
                nc.vector.tensor_copy(kr[:, 0:TP], bank("krot", 0)[:, 0:TP]).then_inc(*VE.step())
                nc.vector.tensor_tensor(kr[:, TP:T], bank("krot", 0)[:, TP:T], cos[:, :], ALU.mult).then_inc(*VE.step())
                nc.vector.tensor_tensor(t[0][:, 0:TS], bank("krot", 1)[:, 0:TS], sin[:, :], ALU.mult).then_inc(*VE.step("krot"))
                own()
                nc.vector.tensor_tensor(kr[:, TP:T], kr[:, TP:T], t[0][:, 0:TS], ALU.add).then_inc(*VE.step())
                ve.wait_ge(*at(AC, "cache_high"))
                for k in range(KC):
                    nc.vector.tensor_tensor(cl[:, k, T:TK], bank("cache", 0)[:, k * P:k * P + P], ch[:, k, T:TK].bitcast(F),
                                            ALU.subtract).then_inc(*VE.step())
                VE.also("ckv_cache")
                nc.vector.tensor_copy(kr[:, T:TK], bank("cache", 1)[:, 0:P]).then_inc(*VE.step("cache"))
                ve.wait_ge(*at(PE, "m1b", 3))

                def lru_low(c):
                    ve.wait_ge(*at(AC, "lru_high", c))
                    nc.vector.tensor_tensor(hl[:, c, :], t[c % 2][:, :], hh[:, c, :].bitcast(F), ALU.subtract
                                            ).then_inc(*VE.step("lru_low", c))

                for c in range(C):
                    own()
                    nc.vector.tensor_tensor(t[c % 2][:, :], lruh[:, c, :], ybuf[:, c, :], ALU.mult).then_inc(*VE.step("lru_full", c))
                    if c >= 1:
                        lru_low(c - 1)
                lru_low(C - 1)
                for j in range(2):
                    ve.wait_ge(*at(PE, "qrot", j))
                    own()
                    nc.vector.tensor_tensor(t[j][:, 0:TS], bank("qrot", j)[:, 0:TS], sin[:, :], ALU.mult).then_inc(*VE.step())
                    nc.vector.tensor_tensor(qr[:, j, TP:T], qr[:, j, TP:T], cos[:, :], ALU.mult).then_inc(*VE.step())
                    own()
                    nc.vector.tensor_tensor(qr[:, j, TP:T], qr[:, j, TP:T], t[j][:, 0:TS], ALU.add).then_inc(*VE.step())
                VE.also("qrot")
                for c in range(C):
                    ve.wait_ge(*at(PE, f"ol{c // 4}", c % 4))
                    nc.vector.tensor_tensor(ybuf[:, c, :], bank(f"ol{c // 4}", c % 4)[:, 0:T], m2[:, c, :], ALU.mult
                                            ).then_inc(*VE.step("mix_lru", c))

                def divide(s):
                    n = TP if s % 3 == 0 else TK - TP
                    ve.wait_ge(*at(AC, "exp", s))
                    nc.vector.reciprocal(prec[:, s % 2:s % 2 + 1], psums[:, s % 2:s % 2 + 1]).then_inc(*VE.step())
                    own()
                    nc.vector.tensor_scalar(sq[s % 2][:, 0:n], sq[s % 2][:, 0:n], prec[:, s % 2:s % 2 + 1], None, ALU.mult
                                            ).then_inc(*VE.step("probs", s))

                def out_low(g):
                    ve.wait_ge(*at(AC, "o_high", g))
                    nc.vector.tensor_tensor(ol[:, g, :], bank("attnB", g % 2)[:, 0:T], oh[:, g, :].bitcast(F), ALU.subtract
                                            ).then_inc(*VE.step("o_low", g))

                for s in range(24):
                    n = TP if s % 3 == 0 else TK - TP
                    ve.wait_ge(*at(PE, "scores", s))
                    nc.vector.tensor_reduce(negmax[:, s % 2:s % 2 + 1], bank("attnA", s % 2)[:, 0:n], AX.X, ALU.max, negate=True
                                            ).then_inc(*VE.step("max", s))
                    if s >= 1:
                        divide(s - 1)
                    if s >= 9 and (s - 9) % 6 == 0:
                        out_low((s - 9) // 6)
                divide(23)
                out_low(3)

                def mix_low(c):
                    ve.wait_ge(*at(AC, "mix_high", c))
                    nc.vector.tensor_tensor(hl[:, c, :], ybuf[:, c, :], hh[:, c, :].bitcast(F), ALU.subtract
                                            ).then_inc(*VE.step("mix_low", c))

                for c in range(C):
                    ve.wait_ge(*at(PE, f"om{c // 4}", c % 4))
                    if c >= 2:
                        own()
                    nc.vector.tensor_tensor(t[c % 2][:, :], bank(f"om{c // 4}", c % 4)[:, 0:T], m1[:, c, :], ALU.mult
                                            ).then_inc(*VE.step())
                    own()
                    nc.vector.tensor_tensor(ybuf[:, c, :], ybuf[:, c, :], t[c % 2][:, :], ALU.add).then_inc(*VE.step("mix", c))
                    if c >= 1:
                        mix_low(c - 1)
                mix_low(C - 1)
                add_bias("mod2", (4, 5))
                gain(gain1, 2, "g_post_mix", 0.0, ("gain1",))
                own()
                residual("post1", gain1)
                add_bias("mod34", (6, 7, 8, 9))
                gain(scale2, 4, "g_pre_ffn", 1.0, ("scale2",))
                own()
                normalise("pre2", scale2, 3)

                def hid_low(c):
                    ve.wait_ge(*at(AC, "hid_high", c))
                    nc.vector.tensor_tensor(hidl[:, c, :], t[c % 2][:, :], hidh[:, c, :].bitcast(F), ALU.subtract
                                            ).then_inc(*VE.step("hid_low", c))

                for j in range(FC // 2):
                    if j == 6:
                        add_bias("mod5", (10, 11))
                        gain(gain2, 5, "g_post_ffn", 0.0, ("gain2",))
                    for g in range(2):
                        c = 2 * j + g
                        ve.wait_ge(*at(AC, "silu", c))
                        ve.wait_ge(*at(PE, f"fi{j}", 2 + g))
                        own()
                        nc.vector.tensor_tensor(t[c % 2][:, :], bank(f"fi{j}", 2 + g)[:, 0:T], sq[c % 4][:, :], ALU.mult
                                                ).then_inc(*VE.step("hid", c))
                    for g in range(2):
                        c = 2 * j + g
                        if c == 18:
                            ve.wait_ge(*at(stored, "all"))
                        hid_low(c)
                residual("post2", gain2)

            for a in range(6):
                ve.wait_ge(end_pe, a + 1)
                tok = ybuf[:, :, :].rearrange("p c t -> p (c t)")
                nc.vector.tensor_copy(tok[:, a * 512:a * 512 + 512], ps[a][:, :]).then_inc(end_ve, 1)

    return {n: (s.labels, s.count) for n, s in new_plan.items()}


_INS = ["x_prompt", "x_sample", "cache_ckv", "cache_krope", "state_lru_fwd", "state_lru_bwd", "c", "c_ctx", "w_mod", "b_mod",
        "g_pre_mix", "g_post_mix", "g_pre_ffn", "g_post_ffn", "w_in", "g_q", "w_q_up", "g_kv", "w_kv_up", "w_o_mla",
        "conv_w", "conv_b", "w_rg", "b_rg", "w_ig", "b_ig", "lru_lambda", "w_o_lru", "w_out", "w_ffn_in", "w_ffn_out"]
_OUTS = [("y_prompt", (1, TP, D)), ("y_sample", (1, TS, D)), ("new_ckv", (1, DEPTH, TP, KVL)),
         ("new_krope", (1, DEPTH, TP, ROPE)), ("new_lru_fwd", (1, DEPTH, LRU)), ("new_lru_bwd", (1, DEPTH, LRU))]


def constants():
    n = ROPE // 4
    inv = np.float32(10000.0) ** (-np.arange(n, dtype=np.float32) / np.float32(n))
    tok = np.arange(TS)
    row, col = (tok // GRID_W).astype(np.float32), (tok % GRID_W).astype(np.float32)
    ang = np.concatenate([row[:, None] * inv, col[:, None] * inv], axis=-1).astype(np.float32)
    ang = np.tile(ang.T, (2 * P // ROPE, 1))
    half = ROPE // 2
    turn = np.zeros((ROPE, ROPE), np.float32)
    for m in range(half):
        turn[m + half, m] = -1.0
        turn[m, m + half] = 1.0
    k = P // ROPE
    return {"ident": np.eye(P, dtype=np.float32), "rot": np.kron(np.eye(k, dtype=np.float32), turn),
            "rep": np.tile(np.eye(ROPE, dtype=np.float32), (k, k)), "reprot": np.tile(turn, (k, k)),
            "cos": np.cos(ang).astype(np.float32), "sin": np.sin(ang).astype(np.float32)}


def tensors(nc, arrays):
    A = {n: nc.dram_tensor(f"in_{n}", a.shape, F, kind="ExternalInput").ap() for n, a in arrays.items()}
    A.update({n: nc.dram_tensor(f"out_{n}", shape, F, kind="ExternalOutput").ap() for n, shape in _OUTS})
    return A


def kernel(**inputs):
    import concourse.bacc as _bacc
    from concourse.bass_utils import run_bass_kernel_spmd as _run

    arrays = {n: np.ascontiguousarray(inputs[n]) for n in _INS}
    arrays.update(constants())
    plan = {}
    for _ in range(2):
        nc = _bacc.Bacc("TRN2", target_bir_lowering=False, num_devices=1)
        plan = program(nc, tensors(nc, arrays), plan)
    r = _run(nc, [{f"in_{n}": a for n, a in arrays.items()}], core_ids=[0])
    return tuple(r.results[0][f"out_{n}"] for n, _ in _OUTS)
```

```python
from contextlib import ExitStack

import numpy as np

import concourse.bass as bass
from concourse import mybir

P = 128
D = 1024
DEPTH = 2
PAST = 128
HEADS = 8
NOPE, ROPE, VD = 64, 32, 64
QK = NOPE + ROPE
QL, KVL = 384, 256
LRU = 1024
FF = 2816
NMOD = 6
GRID_W = 64
EPS = 1e-6
TP, TS = 128, 256
T = TP + TS
TK = T + PAST
C = D // P
FC = FF // P
QC, KC = QL // P, KVL // P
OFF_KV = QL
OFF_KR = OFF_KV + KVL
OFF_LX = OFF_KR + ROPE
OFF_LG = OFF_LX + LRU
OFF_MG = OFF_LG + LRU
SCALE = float(QK) ** -0.5
TINY = 1e-30

F = mybir.dt.float32
FR = mybir.dt.float32r
ALU = mybir.AluOpType
ACT = mybir.ActivationFunctionType
AX = mybir.AxisListType
EXP_LN = "natural_log_exp_and_others"

GROUPS = ((0, slice(0, TP)), (1, slice(TP, T)))

ROWS_A = {}
ROWS_B = {}
for _rows, _names in ((ROWS_A, (("b_mod", NMOD * C), ("g_pre_mix", C), ("g_post_mix", C), ("g_pre_ffn", C),
                                ("g_post_ffn", C), ("conv_w", 4 * C), ("conv_b", C))),
                      (ROWS_B, (("b_rg", 2 * C), ("b_ig", 2 * C), ("lru_lambda", 2 * C), ("state_lru_fwd", C),
                                ("state_lru_bwd", C), ("g_q", QC), ("g_kv", KC)))):
    _at = 0
    for _n, _k in _names:
        _rows[_n] = (_at, _k)
        _at += _k
NA = sum(k for _, k in ROWS_A.values())
NB = sum(k for _, k in ROWS_B.values())


MODS = ((4, "lx0", "lx1"), (5, "gg0", "kr"), (6, "qk", "m2a"), (7, "m2b", "m1a"), (8, "m1b", "ol0"), (9, "wo0", "wo1"),
        (10, "fi0", "fi1"), (11, "fi2", "fi3"), (0, "fi4", "fi5"), (1, "fi6", "fi7"), (2, "fi8", "fi9"), (3, "fi10", "fo0"))
HOSTED = {host: r for r, host, _ in MODS}
FOLDED = {fold: r for r, _, fold in MODS}
NEXT = range(4)


class Load:

    def __init__(self, job, kc, cols, split, parts):
        self.job, self.kc, self.cols, self.split, self.parts = job, kc, cols, split, parts


def plan_loads():
    loads = []

    def mod(r, quarters):
        for i in quarters:
            loads.append(Load(("mod", r), 2, 512, False, [("rows", "w_mod", 2 * i, 2, r * 512, 512, 0)]))

    def w(job, name, c0, cols=512, chunks=(2, 2, 2, 2), second=None):
        k0 = 0
        for i, kc in enumerate(chunks):
            parts = [("rows", name, k0, kc, c0, cols, 0)]
            if second is not None:
                parts = [("rows", name, k0, kc, c0, cols // 2, 0), ("rows", name, k0, kc, second, cols // 2, cols // 2)]
            loads.append(Load(job, kc, cols, True, parts))
            if job in HOSTED and i in (0, 3):
                mod(HOSTED[job], (0, 1) if i == 0 else (2, 3))
            k0 += kc

    def gates(b):
        for name in ("w_rg", "w_ig"):
            loads.append(Load(f"gates{b}", 2, 512, True, [("gate", name, d, 4 * b, d * 512) for d in range(2)]))

    w("lx0", "w_in", OFF_LX)
    w("lx1", "w_in", OFF_LX + 512)
    gates(0)
    w("gg0", "w_in", OFF_LG)
    w("gg1", "w_in", OFF_LG + 512)
    gates(1)
    w("qk", "w_in", 0)
    w("kr", "w_in", 512, 160, (4, 2, 2))
    w("m2a", "w_in", OFF_MG + D)
    w("m2b", "w_in", OFF_MG + D + 512)
    w("m1a", "w_in", OFF_MG)
    w("m1b", "w_in", OFF_MG + 512)
    w("qn0", "w_q_up", 0, 4 * QK, (2, 1))
    w("qn1", "w_q_up", 4 * QK, 4 * QK, (2, 1))
    w("kv", "w_kv_up", 0, 1024, (1, 1))
    w("ol0", "w_o_lru", 0)
    w("ol1", "w_o_lru", 512)
    w("om0", "w_o_mla", 0, chunks=(2, 2))
    w("om1", "w_o_mla", 512, chunks=(2, 2))
    w("wo0", "w_out", 0)
    w("wo1", "w_out", 512)
    for j in range(FC // 2):
        w(f"fi{j}", "w_ffn_in", j * 256, second=FF + j * 256)
    w("fo0", "w_ffn_out", 0, chunks=(2,) * (FC // 2))
    w("fo1", "w_ffn_out", 512, chunks=(2,) * (FC // 2))
    return loads


LOADS = plan_loads()
RAW = 3
SPL = 5
MODR = 2
SPLIT = [n for n, x in enumerate(LOADS) if x.split]
MODL = [n for n, x in enumerate(LOADS) if not x.split]
SIDX = {n: i for i, n in enumerate(SPLIT)}
MIDX = {n: i for i, n in enumerate(MODL)}
assert len(SPLIT) % RAW == 0 and len(SPLIT) % SPL == 0 and len(MODL) % MODR == 0, (len(LOADS), len(SPLIT))


def of_job(job):
    return [n for n, x in enumerate(LOADS) if x.job == job]


def pieces(load, dst, src):
    size = load.kc * load.cols
    if load.job[:2] not in ("qn", "kv"):
        return [(dst[:, 0:size], src[:, 0:size])]
    first, head = NOPE, QK if load.job[:2] == "qn" else NOPE + VD
    h = load.cols // head
    d = dst[:, 0:size].rearrange("p (k n) -> p k n", n=load.cols)
    s = src[:, 0:size].rearrange("p (k h e) -> p k h e", k=load.kc, h=h)
    return [(d[:, :, 0:h * first].rearrange("p k (h e) -> p k h e", h=h), s[:, :, :, 0:first]),
            (d[:, :, h * first:].rearrange("p k (h e) -> p k h e", h=h), s[:, :, :, first:])]


class Steps:

    def __init__(self, sem, labels, total):
        self.sem, self.known, self.total = sem, labels, total
        self.count, self.labels = 0, {}

    def step(self, *label, by=1):
        self.count += by
        if label:
            assert label not in self.labels, label
            self.labels[label] = self.count
        return self.sem, by

    def value(self, *label):
        return self.known[label] if self.known else 1

    def also(self, *label):
        self.labels[label] = self.count


def program(nc, A, plan):
    new_plan = {}
    with ExitStack() as ctx:
        def sb(name, shape, dt=F):
            return ctx.enter_context(nc.sbuf_tensor(name, shape, dt))

        def sem(name):
            return ctx.enter_context(nc.semaphore(name))

        def steps(name):
            labels, total = plan.get(name, ({}, 1))
            s = Steps(sem(name), labels, total)
            new_plan[name] = s
            return s

        raw = [sb(f"raw{s}", [P, 1024]) for s in range(RAW)]
        wh = [sb(f"weight_high{s}", [P, 1024], FR) for s in range(SPL)]
        wl = [sb(f"weight_low{s}", [P, 1024], FR) for s in range(SPL)]
        modw = [sb(f"mod_weight{s}", [P, 1024]) for s in range(MODR)]
        x = sb("x", [P, C, T])
        hh = sb("act_high", [P, C, T], FR)
        hl = sb("act_low", [P, C, T], FR)
        REGION = 2 * FC * T * 4
        arena_at = -(-nc.sbuf_base // 32) * 32
        sb("arena", [P, REGION // 4])
        ybuf = sb("ybuf", [P, C, T])
        qkv = sb("qkv", [P, 6, T])
        ident = sb("ident", [P, P])
        ones = sb("ones", [P, P])
        rot = sb("rot", [P, P])
        rep = sb("rep", [P, P])
        reprot = sb("reprot", [P, P])
        cos = sb("cos", [P, TS])
        sin = sb("sin", [P, TS])
        rows_a = sb("rows_a", [NA, P])
        rows_b = sb("rows_b", [NB, P])
        cache_c = sb("cache_c", [P, KVL])
        cache_k = sb("cache_k", [P, 4, ROPE])
        par = sb("par", [P, NA + NB])
        mod = sb("mod", [P, NMOD * C, 2])
        scale1 = sb("scale1", [P, C, 2])
        scale2 = sb("scale2", [P, C, 2])
        gain1 = sb("gain1", [P, C, 2])
        gain2 = sb("gain2", [P, C, 2])
        cs = sb("cs", [P, C, 32])
        partial = sb("mod_partial", [P, 512])
        fold = sb("mod_fold", [P, 2])
        lam = [sb(f"lam{i}", [P, 2 * C]) for i in range(6)]
        decay, ndecay = lam[4], lam[5]
        hst = sb("hst", [P, 2, C])
        epsc = sb("epsc", [P, 4])
        sq = [sb(f"sq{i}", [P, T]) for i in range(4)]
        t = [sb(f"t{i}", [P, T]) for i in range(2)]
        rstd = sb("rstd", [P, T])
        negmax = sb("negmax", [P, 2])
        psums = sb("psums", [P, 2])
        prec = sb("prec", [P, 2])

        def region(name, at, shape, dt=F):
            return nc.alloc_sbuf_tensor_at(name, shape, dt, offset=arena_at + at)

        TB = T * 4
        hidh = region("hid_high", 0, [P, FC, T], FR)
        hidl = region("hid_low", FC * TB, [P, FC, T], FR)
        first_mod = region("first_mod", 0, [P, len(NEXT), C, 512])
        xc = region("xc", 0, [P, C, T])
        xch = region("xc_high", C * TB, [P, 2, T], FR)
        xcl = region("xc_low", (C + 2) * TB, [P, 2, T], FR)
        r_ = region("lru_r", 12 * TB, [P, 2, 4, T])
        i_ = region("lru_i", 20 * TB, [P, 2, 4, T])
        tau = region("lru_tau", 28 * TB, [P, 2, 4, T])
        lruh = region("lru_h", 36 * TB, [P, C, T])
        m2 = region("merge_lru", 12 * TB, [P, C, T])
        m1 = region("merge_mla", 20 * TB, [P, C, T])
        qnh = region("qn_high", 0, [P, QC, T], FR)
        qnl = region("qn_low", QC * TB, [P, QC, T], FR)
        ch = region("ckv_high", 2 * QC * TB, [P, KC, TK], FR)
        cl = region("ckv_low", 2 * QC * TB + KC * TK * 4, [P, KC, TK], FR)
        oh = region("o_high", 0, [P, 4, T], FR)
        ol = region("o_low", 4 * TB, [P, 4, T], FR)
        kt = region("k_nope", 28 * TB, [P, 4, TK])
        kr = region("k_rope", 28 * TB + 4 * TK * 4, [P, TK])
        vv = region("v", 36 * TB, [P, 4, HEADS * VD])
        out_c = region("out_ckv", 36 * TB + 8192, [P, KVL])
        out_k = region("out_krope", 36 * TB + 8192 + 1024, [P, ROPE])
        out_h = region("out_state", 36 * TB + 8192 + 1152, [2 * C, P])
        qt = qkv[:, 0:4, :]
        qr = qkv[:, 4:6, :]

        ps = [ctx.enter_context(nc.psum_tensor(f"bank{i}", [P, 512], F)) for i in range(8)]

        tensor_done = steps("tensor_done")
        scalar_done = steps("scalar_done")
        vector_done = steps("vector_done")
        gpsimd_done = steps("gpsimd_done")
        raw_full = [steps(f"raw_full{s}") for s in range(RAW)]
        mod_full = [steps(f"mod_full{s}") for s in range(MODR)]
        rows_full = steps("rows_full")
        cache_full = steps("cache_full")
        stored = steps("stored")
        PE, AC, VE, GP = tensor_done, scalar_done, vector_done, gpsimd_done
        sync_passed = sem("sync_passed")
        start_load = sem("start_load")
        start_mod = sem("start_mod")
        start_pe = sem("start_pe")
        start_ve = sem("start_ve")
        start_ac = sem("start_ac")
        start_gp = sem("start_gp")
        end_pe = sem("end_pe")
        end_ve = sem("end_ve")
        end_store = sem("end_store")

        def in_layer(l):
            def at(s, *label, prev=False):
                return s.sem, l * s.total + s.value(*label) + (0 if prev else s.total)
            return at

        def last(l, s):
            return s.sem, l * s.total + s.count + s.total

        def par_col(name, i):
            rows, off = (ROWS_A, 0) if name in ROWS_A else (ROWS_B, NA)
            return par[:, off + rows[name][0] + i:off + rows[name][0] + i + 1]

        def par_cols(name):
            rows, off = (ROWS_A, 0) if name in ROWS_A else (ROWS_B, NA)
            return par[:, off + rows[name][0]:off + rows[name][0] + rows[name][1]]

        jobs = [("par", [(VE, "par", 1)]), ("st_pre1", [(AC, "rs", "pre1")]),
                ("lx0", [(VE, "conv", 3)]), ("lx1", [(VE, "conv", 7)])]
        jobs += [(f"gate{n}", [(AC, "gate", n)]) for n in range(4)]
        jobs += [("gg0", [(AC, "gelu", 3)]), ("gg1", [(AC, "gelu", 7)])]
        jobs += [(f"gate{n}", [(AC, "gate", n)]) for n in range(4, 8)]
        jobs += [("qk", [(AC, "qkv", 3)]), ("kr", [(AC, "qkv", 5)]), ("m2a", [(AC, "m2", 3)]),
                 ("st_qkv", [(AC, "rs", "kv")]), ("m2b", [(AC, "m2", 7)]), ("krot", [(VE, "krot")]),
                 ("m1a", [(AC, "m1", 3)]), ("cache", [(VE, "cache")]), ("m1b", [(AC, "m1", 7)]),
                 ("outs", [(AC, "outs")]),
                 ("qn0", [(AC, "qn", 2)]), ("qn1", [(AC, "qn", 5)]), ("kn", [(AC, "kn", 3)]), ("vv", [(AC, "vv", 3)]),
                 ("qrot", [(VE, "qrot")]),
                 ("attn", [(AC, "pt", 23), (VE, "o_low", 3)]), ("ol0", [(VE, "mix_lru", 3)]), ("none", []),
                 ("ol1", [(VE, "mix_lru", 7)]),
                 ("om0", [(VE, "mix", 3)]), ("om1", [(VE, "mix", 7)]),
                 ("wo0", [(AC, "ysq", "post1", 3)]), ("wo1", [(AC, "ysq", "post1", 7)]), ("st_post1", [(AC, "rs", "post1")]),
                 ("st_pre2", [(AC, "rs", "pre2")])]
        for j in range(FC // 2):
            jobs.append((f"fi{j}", [(AC, "silu", 2 * j + 1), (VE, "hid", 2 * j + 1)]))
        jobs += [("fo0", [(AC, "ysq", "post2", 3)]), ("fo1", [(AC, "ysq", "post2", 7)]), ("st_post2", [(AC, "rs", "post2")])]
        for name, reads in jobs:
            if name in HOSTED:
                reads.append((VE, "partial", HOSTED[name]))
            if name in FOLDED:
                reads.append((VE, "mod", FOLDED[name]))
        names = [n for n, _ in jobs]
        if len(jobs) % 2:
            jobs.insert(names.index("attn"), ("none", []))
            names = [n for n, _ in jobs]
        set_of = {n: i % 2 for i, (n, _) in enumerate(jobs)}

        def bank(job, b):
            return ps[4 * set_of[job] + b]

        def reads_before(job):
            i = names.index(job)
            k = i - 2
            while not jobs[k][1]:
                k -= 2
            return [(r, k < 0) for r in jobs[k][1]]

        block = ctx.enter_context(nc.Block())

        @block.sync
        def _(sp):
            consts = ((ident, "ident"), (rot, "rot"), (rep, "rep"), (reprot, "reprot"), (cos, "cos"), (sin, "sin"), (fold, "fold"))
            for buf, name in consts:
                sp.dma_start(buf[:, :], A[name]).then_inc(start_load, 16)
            sp.dma_start(rows_b[0:C, :], A["c_ctx"].rearrange("(n p) -> n p", p=P)).then_inc(start_load, 16)
            sp.dma_start(rows_b[C:2 * C, :], A["c"].rearrange("b (n p) -> (b n) p", p=P)).then_inc(start_load, 16)
            tok = ybuf[:, :, :].rearrange("p c t -> p (c t)").rearrange("p (a d) -> p a d", d=D)
            sp.dma_start(tok[:, 0, :], A["x_prompt"].rearrange("b t d -> (b t) d")).then_inc(start_load, 16)
            sp.dma_start(tok[:, 1:3, :], A["x_sample"].rearrange("b (a p) d -> p (b a) d", p=P)).then_inc(start_load, 16)
            for r in NEXT:
                sp.dma_start(first_mod[:, r, :, :], A["w_mod"][0:1, :, r * 512:r * 512 + 512].rearrange("a (k p) n -> p (a k) n", p=P)
                             ).then_inc(start_mod, 16)

            with sp.Fori(0, DEPTH) as l:
                at = in_layer(l)

                def vector_rows():
                    sp.wait_ge(*at(PE, "par", 1, prev=True))
                    sp.sem_inc(sync_passed, 1)
                    sp.wait_ge(start_pe, 2)
                    for dst, rows in ((rows_a, ROWS_A), (rows_b, ROWS_B)):
                        for name, (r0, k) in rows.items():
                            src = A[name]
                            if name.startswith("state"):
                                src = src[0:1, bass.ds(l, 1), :].rearrange("b a (n p) -> (b a n) p", p=P)
                            elif len(src.shape) == 3:
                                src = src[bass.ds(l, 1), :, :].rearrange("a w (n p) -> (a w n) p", p=P)
                            else:
                                src = src[bass.ds(l, 1), :].rearrange("a (n p) -> (a n) p", p=P)
                            sp.dma_start(dst[r0:r0 + k, :], src).then_inc(*rows_full.step(by=16))
                    rows_full.also("all")

                def cache_rows():
                    sp.wait_ge(*at(PE, "cache", prev=True))
                    sp.sem_inc(sync_passed, 1)
                    sp.dma_start(cache_c[:, :], A["cache_ckv"][0:1, bass.ds(l, 1), :, :].rearrange("b a t d -> (b a t) d")
                                 ).then_inc(*cache_full.step(by=16))
                    for q in range(4):
                        sp.dma_start(cache_k[:, q, :], A["cache_krope"][0:1, bass.ds(l, 1), :, :].rearrange(
                            "b a t d -> (b a t) d")).then_inc(*cache_full.step(by=16))
                    cache_full.also("all")

                def stores():
                    sp.wait_ge(*at(AC, "outs"))
                    sp.sem_inc(sync_passed, 1)
                    sp.dma_start(A["new_ckv"][0:1, bass.ds(l, 1), :, :].rearrange("b a t d -> (b a t) d"), out_c[:, :]
                                 ).then_inc(*stored.step(by=16))
                    sp.dma_start(A["new_krope"][0:1, bass.ds(l, 1), :, :].rearrange("b a t d -> (b a t) d"), out_k[:, :]
                                 ).then_inc(*stored.step(by=16))
                    for d, name in enumerate(("new_lru_fwd", "new_lru_bwd")):
                        sp.dma_start(A[name][0:1, bass.ds(l, 1), :].rearrange("b a (n p) -> (b a n) p", p=P),
                                     out_h[C * d:C * d + C, :]).then_inc(*stored.step(by=16))
                    stored.also("all")

                for n, load in enumerate(LOADS):
                    if n == 2:
                        vector_rows()
                    if n == of_job("gg0")[0]:
                        cache_rows()
                    if n == of_job("fi2")[0]:
                        stores()
                    if load.split:
                        m = SIDX[n]
                        slot, full = raw[m % RAW], raw_full[m % RAW]
                        sp.wait_ge(*at(GP, "low", SPLIT[m - RAW], prev=m < RAW))
                        sp.sem_inc(sync_passed, 1)
                    else:
                        m = MIDX[n]
                        slot, full = modw[m % MODR], mod_full[m % MODR]
                        sp.wait_ge(*at(PE, "used", MODL[m - MODR], prev=m < MODR))
                        sp.sem_inc(sync_passed, 1)
                    layer = l if load.split or load.job[1] not in NEXT else (l + 1) % DEPTH
                    for part in load.parts:
                        if part[0] == "rows":
                            _, name, k0, kc, c0, cols, o = part
                            dst = slot[:, 0:load.kc * load.cols].rearrange("p (k n) -> p k n", n=load.cols)
                            src = A[name][bass.ds(layer, 1), k0 * P:(k0 + kc) * P, c0:c0 + cols]
                            sp.dma_start(dst[:, :, o:o + cols], src.rearrange("a (k p) n -> p (a k) n", p=P)
                                         ).then_inc(*full.step(by=16))
                        else:
                            _, name, d, n0, o = part
                            dst = slot[:, o:o + 512].rearrange("p (n e) -> p n e", e=P)
                            src = A[name][bass.ds(l, 1), d, n0:n0 + 4, :, :]
                            sp.dma_start(dst, src.rearrange("a n k e -> k (a n) e")).then_inc(*full.step(by=16))
                    full.also("load", n)

            sp.wait_ge(end_ve, 6)
            tok = ybuf[:, :, :].rearrange("p c t -> p (c t)").rearrange("p (a d) -> p a d", d=D)
            sp.dma_start(A["y_prompt"].rearrange("b t d -> (b t) d"), tok[:, 0, :]).then_inc(end_store, 16)
            sp.dma_start(A["y_sample"].rearrange("b (a p) d -> p (b a) d", p=P), tok[:, 1:3, :]).then_inc(end_store, 16)
            sp.wait_ge(end_store, 32)
            sp.wait_ge(stored.sem, DEPTH * stored.total + stored.total)

        @block.gpsimd
        def _(gp):
            nc.gpsimd.memset(ones[:, :], 1.0).then_inc(start_gp, 1)
            nc.gpsimd.memset(cs[:, :, :], 0.0).then_inc(start_gp, 1)
            nc.gpsimd.memset(epsc[:, 0:1], EPS).then_inc(start_gp, 1)
            nc.gpsimd.memset(epsc[:, 1:2], TINY).then_inc(start_gp, 1)
            nc.gpsimd.memset(epsc[:, 2:3], float(0.5 * np.log(2.0))).then_inc(start_gp, 1)
            nc.gpsimd.memset(epsc[:, 3:4], 1.0).then_inc(start_gp, 1)
            gp.sem_inc(GP.sem, GP.total)
            for s in (*raw_full, *mod_full, rows_full, cache_full, stored):
                gp.sem_inc(s.sem, s.total)
            with gp.Fori(0, DEPTH) as l:
                at = in_layer(l)
                for m, n in enumerate(SPLIT):
                    gp.wait_ge(*at(AC, "high", n))
                    load = LOADS[n]
                    for (low, w), (high, _) in zip(pieces(load, wl[m % SPL], raw[m % RAW]), pieces(load, wh[m % SPL], raw[m % RAW])):
                        nc.gpsimd.tensor_tensor(low, w, high.bitcast(F), ALU.subtract).then_inc(*GP.step())
                    GP.also("low", n)

        @block.tensor
        def _(pe):
            def prologue():
                tok = ybuf[:, :, :].rearrange("p c t -> p (c t)").rearrange("p (a d) -> p a d", d=D)
                pe.wait_ge(start_load, 16 * 11)
                nc.tensor.transpose(ps[7][:, 0:2 * C], rows_b[0:2 * C, :], ident[0:2 * C, 0:2 * C]).then_inc(start_pe, 2)
                for c in range(C):
                    if c == 7:
                        pe.wait_ge(start_ac, 1)
                    for a in range(3):
                        ins = nc.tensor.transpose(ps[c][:, a * P:a * P + P], tok[:, a, c * P:c * P + P], ident[:, :])
                    ins.then_inc(start_pe, 1)
                pe.wait_ge(start_mod, 16 * len(NEXT))
                pe.wait_ge(start_ve, C)
                for k in range(C):
                    for r in NEXT:
                        q = (k + r) % 4
                        ins = nc.tensor.matmul(ps[r][32 * q:32 * q + 32, :], cs[:, k, :], first_mod[:, r, k, :], start=k < 4,
                                               stop=k >= 4, skip_group_check=True)
                ins.then_inc(start_pe, 1)
                for r in NEXT:
                    pe.wait_ge(start_ve, C + 1 + r)
                    for g in range(4):
                        ins = nc.tensor.matmul(ps[4][:, 8 * r + 2 * g:8 * r + 2 * g + 2],
                                               tok_flat[:, 512 * r + P * g:512 * r + P * g + P], fold[:, :],
                                               start=r == 0 and g == 0, stop=True, skip_group_check=True)
                ins.then_inc(start_pe, 1)

            tok_flat = ybuf[:, :, :].rearrange("p c t -> p (c t)")
            prologue()
            pe.wait_ge(start_gp, 6)
            pe.wait_ge(start_ve, C + 5)
            pe.wait_ge(start_ac, 1)
            pe.sem_inc(PE.sem, PE.total)
            with pe.Fori(0, DEPTH) as l:
                at = in_layer(l)

                def banks_free(job):
                    for (s, *label), prev in reads_before(job):
                        pe.wait_ge(*at(s, *label, prev=prev))

                def split_job(job, high, low, ready=None, groups=None, after=None, between=None):
                    banks_free(job)
                    loads = of_job(job)
                    k = 0
                    total = sum(LOADS[n].kc for n in loads)
                    for i, n in enumerate(loads):
                        load = LOADS[n]
                        s = SIDX[n] % SPL
                        pe.wait_ge(*at(GP, "low", n))
                        view = [w[:, 0:load.kc * load.cols].rearrange("p (k n) -> p k n", n=load.cols) for w in (wh[s], wl[s])]
                        for kk in range(load.kc):
                            if ready is not None:
                                pe.wait_ge(*at(*ready, k))
                            gs = groups or [slice(g * P, g * P + P) for g in range(load.cols // P)]
                            for g, cols in enumerate(gs):
                                o = bank(job, g)[:, 0:T]
                                nc.tensor.matmul(o, view[0][:, kk, cols], high[:, k, :], start=k == 0, stop=False)
                                nc.tensor.matmul(o, view[0][:, kk, cols], low[:, k, :], start=False, stop=False)
                                ins = nc.tensor.matmul(o, view[1][:, kk, cols], high[:, k, :], start=False,
                                                       stop=k == total - 1)
                                if k == total - 1:
                                    ins.then_inc(*PE.step(job, g))
                                elif kk == load.kc - 1 and g == len(gs) - 1:
                                    ins.then_inc(*PE.step())
                                if kk == load.kc - 1 and g == len(gs) - 1:
                                    PE.also("used", n)
                                if between is not None:
                                    between(len(gs) * k + g, len(gs) * total)
                            k += 1
                        if job in HOSTED and i in (0, 2):
                            mod_products(HOSTED[job], job, (0, 1) if i == 0 else (2, 3))
                        if job in FOLDED and i == len(loads) - 2:
                            mod_fold(FOLDED[job], job)
                        if after is not None and i in after:
                            after[i]()

                def mod_products(r, job, quarters):
                    for i in quarters:
                        n = of_job(("mod", r))[i]
                        pe.wait_ge(*at(mod_full[MIDX[n] % MODR], "load", n))
                        for kk in range(2):
                            k = 2 * i + kk
                            for b in range(4):
                                q = (k + b) % 4
                                ins = nc.tensor.matmul(bank(job, b)[32 * q:32 * q + 32, T:512], cs[:, k, :],
                                                       modw[MIDX[n] % MODR][:, 512 * kk + P * b:512 * kk + P * b + P],
                                                       start=False, stop=k >= 4, skip_group_check=True)
                        ins.then_inc(*PE.step("used", n))

                def mod_fold(r, job):
                    pe.wait_ge(*at(VE, "partial", r))
                    for g in range(4):
                        ins = nc.tensor.matmul(bank(job, 0)[:, T + 2 * g:T + 2 * g + 2], partial[:, P * g:P * g + P], fold[:, :],
                                               start=False, stop=True, skip_group_check=True)
                    ins.then_inc(*PE.step("fold", r))

                def stat(job, b, c, count, sqlabel):
                    pe.wait_ge(*at(AC, *sqlabel, c))
                    return nc.tensor.matmul(bank(job, b)[:, 0:T], ones[:, :], sq[c % 4][:, :], start=c == 0, stop=c == count - 1)

                banks_free("par")
                pe.wait_ge(*at(rows_full, "all"))
                nc.tensor.transpose(bank("par", 0)[:, 0:NA], rows_a[:, :], ident[0:NA, 0:NA]).then_inc(*PE.step("par", 0))
                nc.tensor.transpose(bank("par", 1)[:, 0:NB], rows_b[:, :], ident[0:NB, 0:NB]).then_inc(*PE.step("par", 1))
                banks_free("st_pre1")
                for c in range(C):
                    stat("st_pre1", 0, c, C, ("sq", "pre1")).then_inc(*PE.step("st", "pre1", c))
                split_job("lx0", hh, hl, ready=(VE, "h", "pre1"))
                split_job("lx1", hh, hl)

                def gates(b):
                    loads = of_job(f"gates{b}")
                    pe.wait_ge(*at(GP, "low", loads[1]))
                    for j in range(4):
                        c = 4 * b + j
                        banks_free(f"gate{c}")
                        pe.wait_ge(*at(VE, "xc_low", c))
                        for q in range(4):
                            s = SIDX[loads[q // 2]] % SPL
                            cols = slice(512 * (q % 2) + P * j, 512 * (q % 2) + P * j + P)
                            o = bank(f"gate{c}", q)[:, 0:T]
                            nc.tensor.matmul(o, wh[s][:, cols], xch[:, c % 2, :], start=True, stop=False)
                            nc.tensor.matmul(o, wh[s][:, cols], xcl[:, c % 2, :], start=False, stop=False)
                            nc.tensor.matmul(o, wl[s][:, cols], xch[:, c % 2, :], start=False, stop=True
                                             ).then_inc(*PE.step("gate", c, q))
                    for n in loads:
                        PE.also("used", n)

                gates(0)
                split_job("gg0", hh, hl)
                split_job("gg1", hh, hl)
                gates(1)
                split_job("qk", hh, hl)
                split_job("kr", hh, hl, groups=[slice(0, P), slice(160 - P, 160)])
                split_job("m2a", hh, hl)
                banks_free("st_qkv")
                for c in range(QC):
                    pe.wait_ge(*at(AC, "sqq", c))
                    nc.tensor.matmul(bank("st_qkv", 0)[:, 0:T], ones[:, :], sq[c][:, :], start=c == 0, stop=c == QC - 1
                                     ).then_inc(*PE.step("stq", c))
                for c in range(KC):
                    pe.wait_ge(*at(AC, "sqq", QC + c))
                    nc.tensor.matmul(bank("st_qkv", 1)[:, 0:T], ones[:, :], (sq[3], t[1])[c][:, :], start=c == 0,
                                     stop=c == KC - 1).then_inc(*PE.step("stq", QC + c))
                split_job("m2b", hh, hl)
                banks_free("krot")
                tail = slice(P - ROPE, P)
                nc.tensor.matmul(bank("krot", 0)[:, 0:T], rep[tail, :], qkv[tail, 5, :], start=True, stop=True)
                nc.tensor.matmul(bank("krot", 1)[:, 0:TS], reprot[tail, :], qkv[tail, 5, TP:T], start=True, stop=True
                                 ).then_inc(*PE.step("krot"))
                split_job("m1a", hh, hl)
                banks_free("cache")
                pe.wait_ge(*at(cache_full, "all"))
                for k in range(KC):
                    nc.tensor.transpose(bank("cache", 0)[:, k * P:k * P + P], cache_c[:, k * P:k * P + P], ident[:, :])
                nc.tensor.transpose(bank("cache", 1)[:, 0:P], cache_k[:, :, :].rearrange("p q r -> p (q r)"), ident[:, :]
                                    ).then_inc(*PE.step("cache"))
                split_job("m1b", hh, hl)
                banks_free("outs")
                pe.wait_ge(*at(VE, "states"))
                pe.wait_ge(*at(VE, "ckv_full", KC - 1))
                for k in range(KC):
                    nc.tensor.transpose(bank("outs", 0)[:, k * P:k * P + P], qkv[:, QC + k, 0:TP], ident[:, :])
                nc.tensor.transpose(bank("outs", 1)[:, 0:P], qkv[:, QC + KC, 0:TP], ident[:, :])
                nc.tensor.transpose(bank("outs", 2)[0:2 * C, 0:P], hst[:, :, :].rearrange("p d c -> p (d c)"), ident[:, :]
                                    ).then_inc(*PE.step("outs"))
                for j in range(2):
                    job = f"qn{j}"
                    loads = of_job(job)
                    banks_free(job)
                    for k in range(QC):
                        n, kk = (loads[0], k) if k < 2 else (loads[1], 0)
                        s = SIDX[n] % SPL
                        pe.wait_ge(*at(GP, "low", n))
                        pe.wait_ge(*at(VE, "qn", k))
                        for g in range(3):
                            w2 = [w[:, kk * 4 * QK + g * P:kk * 4 * QK + g * P + P] for w in (wh[s], wl[s])]
                            o = bank(job, g)[:, 0:T]
                            nc.tensor.matmul(o, w2[0], qnh[:, k, :], start=k == 0, stop=False)
                            nc.tensor.matmul(o, w2[0], qnl[:, k, :], start=False, stop=False)
                            ins = nc.tensor.matmul(o, w2[1], qnh[:, k, :], start=False, stop=k == QC - 1)
                            if k == QC - 1:
                                ins.then_inc(*PE.step("qn", 3 * j + g))
                            elif k == 1 and g == 2:
                                ins.then_inc(*PE.step("used", n))
                    PE.also("used", n)
                loads = of_job("kv")
                banks_free("kn")
                pe.wait_ge(*at(VE, "ckv_cache"))
                for k, n in enumerate(loads):
                    s = SIDX[n] % SPL
                    pe.wait_ge(*at(GP, "low", n))
                    pe.wait_ge(*at(VE, "ckv", k))
                    for g in range(4):
                        w2 = [w[:, g * P:g * P + P] for w in (wh[s], wl[s])]
                        o = bank("kn", g)[:, :]
                        nc.tensor.matmul(o, w2[0], ch[:, k, :], start=k == 0, stop=False)
                        nc.tensor.matmul(o, w2[0], cl[:, k, :], start=False, stop=False)
                        ins = nc.tensor.matmul(o, w2[1], ch[:, k, :], start=False, stop=k == KC - 1)
                        if k == KC - 1:
                            ins.then_inc(*PE.step("kn", g))
                banks_free("vv")
                for g in range(4):
                    for k, n in enumerate(loads):
                        s = SIDX[n] % SPL
                        wvh, wvl = (w[:, HEADS * NOPE:HEADS * (NOPE + VD)] for w in (wh[s], wl[s]))
                        o = bank("vv", g)[:, :]
                        tk = slice(g * P, g * P + P)
                        nc.tensor.matmul(o, ch[:, k, tk], wvh, start=k == 0, stop=False)
                        nc.tensor.matmul(o, cl[:, k, tk], wvh, start=False, stop=False)
                        ins = nc.tensor.matmul(o, ch[:, k, tk], wvl, start=False, stop=k == KC - 1)
                    ins.then_inc(*PE.step("vv", g))
                for n in loads:
                    PE.also("used", n)
                banks_free("qrot")
                for j in range(2):
                    pe.wait_ge(*at(AC, "qn", 3 * j + 2))
                    nc.tensor.matmul(bank("qrot", j)[:, 0:TS], rot[:, :], qr[:, j, TP:T], start=True, stop=True
                                     ).then_inc(*PE.step("qrot", j))
                banks_free("attn")
                pe.wait_ge(*at(VE, "qrot"))
                pe.wait_ge(*at(AC, "vv", 3))

                def scores(s):
                    h, q = divmod(s, 3)
                    if s >= 2:
                        pe.wait_ge(*at(AC, "exp", s - 2))
                    keys = slice(0, TP) if q == 0 else slice(TP, TK)
                    qs = slice(q * P, q * P + P)
                    o = bank("attn", s % 2)[:, 0:keys.stop - keys.start]
                    half, quad = slice(64 * (h % 2), 64 * (h % 2) + 64), slice(32 * (h % 4), 32 * (h % 4) + 32)
                    nc.tensor.matmul(o, qt[half, h // 2, qs], kt[half, h // 2, keys], start=True, stop=False)
                    nc.tensor.matmul(o, qr[quad, h // 4, qs], kr[quad, keys], start=False, stop=True
                                     ).then_inc(*PE.step("scores", s))

                def turn(s):
                    n = 1 if s % 3 == 0 else 3
                    if s >= 1:
                        pe.wait_ge(*at(AC, "pt", s - 1))
                    pe.wait_ge(*at(VE, "probs", s))
                    for k in range(n):
                        ins = nc.tensor.transpose(bank("attn", 2)[:, k * P:k * P + P],
                                                  sq[s % 2][:, k * P:k * P + P], ident[:, :])
                    ins.then_inc(*PE.step("turn", s))

                def values(s):
                    h, q = divmod(s, 3)
                    tiles = (0,) if q == 0 else (1, 2, 3)
                    if h % 2 == 0 and h >= 2 and q == 0:
                        pe.wait_ge(*at(VE, "o_low", h // 2 - 1))
                    pe.wait_ge(*at(AC, "pt", s))
                    half = slice(64 * (h % 2), 64 * (h % 2) + 64)
                    o = bank("attn", 3)[half, q * P:q * P + P]
                    for j, k in enumerate(tiles):
                        ins = nc.tensor.matmul(o, vv[:, k, h * VD:h * VD + VD], sq[2 + s % 2][:, j * P:j * P + P],
                                               start=j == 0, stop=j == len(tiles) - 1)
                    ins.then_inc(*PE.step("values", s))

                def attention_step(s):
                    if s + 2 < 24:
                        scores(s + 2)
                    turn(s)
                    if s >= 1:
                        values(s - 1)

                def attention_steps(first):
                    def between(i, count):
                        if (i + 1) * 11 // count > i * 11 // count:
                            attention_step(first + i * 11 // count)
                    return between

                scores(0)
                scores(1)
                split_job("ol0", hh, hl, ready=(VE, "lru_low"), between=attention_steps(0))
                attention_step(11)
                attention_step(12)
                split_job("ol1", hh, hl, between=attention_steps(13))
                values(23)
                split_job("om0", oh, ol, ready=(VE, "o_low"))
                split_job("om1", oh, ol)
                split_job("wo0", hh, hl, ready=(VE, "mix_low"))

                def ysquares(which, chunks):
                    for c in chunks:
                        if c == 0:
                            banks_free(f"st_{which}")
                        stat(f"st_{which}", 0, c, C, ("ysq", which)).then_inc(*PE.step("st", which, c))

                split_job("wo1", hh, hl, after={1: lambda: ysquares("post1", range(4))})
                ysquares("post1", range(4, C))
                banks_free("st_pre2")
                for c in range(C):
                    stat("st_pre2", 0, c, C, ("sq", "pre2")).then_inc(*PE.step("st", "pre2", c))
                for j in range(FC // 2):
                    split_job(f"fi{j}", hh, hl, ready=(VE, "h", "pre2") if j == 0 else None)
                split_job("fo0", hidh, hidl, ready=(VE, "hid_low"))
                split_job("fo1", hidh, hidl, after={2: lambda: ysquares("post2", range(4))})
                ysquares("post2", range(4, C))

            pe.wait_ge(VE.sem, DEPTH * VE.total + VE.value("x", "post2", C - 1))
            for a in range(3):
                for c in range(C):
                    ins = nc.tensor.transpose(ps[2 * a + c // 4][:, (c % 4) * P:(c % 4) * P + P], x[:, c, a * P:a * P + P],
                                              ident[:, :])
                    if c % 4 == 3:
                        ins.then_inc(end_pe, 1)

        @block.scalar
        def _(ac):
            ac.wait_ge(start_pe, 2)
            ac.wait_ge(start_gp, 6)
            nc.scalar.activation(cs[:, :, 0:2], ps[7][:, 0:2 * C].rearrange("p (g c) -> p c g", g=2), ACT.Silu
                                 ).then_inc(start_ac, 1)
            ac.wait_ge(start_gp, 6)
            ac.wait_ge(start_ve, C + 5)
            ac.sem_inc(AC.sem, AC.total)
            with ac.Fori(0, DEPTH) as l:
                at = in_layer(l)
                made = [0]

                def highs(job, ahead=2):
                    upto = SIDX[of_job(job)[-1]] + ahead
                    while made[0] <= min(upto, len(SPLIT) - 1):
                        m = made[0]
                        n = SPLIT[m]
                        ac.wait_ge(*at(raw_full[m % RAW], "load", n))
                        ac.wait_ge(*at(PE, "used", SPLIT[m - SPL], prev=m < SPL))
                        for high, w in pieces(LOADS[n], wh[m % SPL], raw[m % RAW]):
                            nc.scalar.activation(high, w, ACT.Copy).then_inc(*AC.step())
                        AC.also("high", n)
                        made[0] += 1

                def squares(which, of, label, prev=False):
                    for c in range(C):
                        ac.wait_ge(*at(VE, *label, c, prev=prev))
                        if c >= 4:
                            ac.wait_ge(*at(PE, "st", which, c - 4))
                        nc.scalar.activation(sq[c % 4][:, :], of[:, c, :], ACT.Square).then_inc(*AC.step("sq", which, c))

                def inverse_root(which, src, n):
                    nc.scalar.activation(rstd[:, :], src[:, 0:T], ACT.Ln, scale=1.0 / n, bias=epsc[:, 0:1]
                                         ).then_inc(*AC.step("rs", which))
                    ac.wait_ge(*last(l, AC))
                    nc.scalar.activation(rstd[:, :], rstd[:, :], ACT.Exp, scale=-0.5).then_inc(*AC.step("rstd", which))

                def make_high(dst, src, label, *out):
                    ac.wait_ge(*label)
                    nc.scalar.activation(dst, src, ACT.Copy).then_inc(*AC.step(*out))

                highs("lx0", ahead=0)
                nc.scalar.preload_act_table_set(EXP_LN)
                ac.wait_ge(*at(VE, "abslam"))
                nc.scalar.activation(lam[0][:, :], lam[1][:, :], ACT.Exp, scale=-1.0).then_inc(*AC.step("explam"))
                ac.wait_ge(*at(VE, "onelam"))
                nc.scalar.activation(lam[1][:, :], lam[2][:, :], ACT.Ln).then_inc(*AC.step("lnlam"))
                squares("pre1", x, ("x", "post2"), prev=True)
                ac.wait_ge(*at(PE, "st", "pre1", C - 1))
                ac.wait_ge(*at(VE, "x", "post2", C - 1, prev=True))
                inverse_root("pre1", bank("st_pre1", 0), D)
                for c in range(C):
                    make_high(hh[:, c, :], t[c % 2][:, :], at(VE, "hfull", "pre1", c), "hh", "pre1", c)

                highs("lx0")
                for c in range(C):
                    if c == 4:
                        highs("lx1")
                    ac.wait_ge(*at(PE, f"lx{c // 4}", c % 4))
                    nc.scalar.activation(xc[:, c, :], bank(f"lx{c // 4}", c % 4)[:, 0:T], ACT.Identity,
                                         scale=par_col("conv_w", 2 * C + c), bias=par_col("conv_b", c)
                                         ).then_inc(*AC.step("conv", c))
                    if c == 3:
                        for n in range(2):
                            make_high(xch[:, n, :], xc[:, n, :], at(VE, "conv", n), "xc_high", n)

                def lru_gates(b):
                    highs(f"gates{b}")
                    for j in range(4):
                        c = 4 * b + j
                        if c >= 2:
                            ac.wait_ge(*at(PE, "gate", c - 2, 3))
                            make_high(xch[:, c % 2, :], xc[:, c, :], at(VE, "conv", c), "xc_high", c)
                        if b == 1 and j == 0:
                            ac.wait_ge(*at(VE, "scan", 3))
                        for q in range(4):
                            ac.wait_ge(*at(PE, "gate", c, q))
                            dst = (r_ if q < 2 else i_)[:, q % 2, j, :]
                            nc.scalar.activation(dst, bank(f"gate{c}", q)[:, 0:T], ACT.Sigmoid,
                                                 bias=par_col("b_rg" if q < 2 else "b_ig", C * (q % 2) + c)
                                                 ).then_inc(*AC.step())
                        AC.also("gate", c)
                        ac.wait_ge(*last(l, AC))
                        for d in range(2):
                            nc.scalar.activation(tau[:, d, j, :], r_[:, d, j, :], ACT.Tanh,
                                                 scale=decay[:, C * d + c:C * d + c + 1]).then_inc(*AC.step())
                        AC.also("tau", c)

                def lru_coefficients(b):
                    nc.scalar.preload_act_table_set(EXP_LN)
                    ac.wait_ge(*last(l, AC))

                    def root(e):
                        d, j = e
                        ac.wait_ge(*at(VE, "lnroot", 4 * b + j, d))
                        nc.scalar.activation(tau[:, d, j, :], tau[:, d, j, :], ACT.Exp, scale=0.5, bias=epsc[:, 2:3]
                                             ).then_inc(*AC.step("root", 4 * b + j, d))

                    order = [(d, j) for j in range(4) for d in range(2)]
                    for e, (d, j) in enumerate(order):
                        c = 4 * b + j
                        if e >= 4:
                            ac.wait_ge(*at(VE, "lnroot", 4 * b + order[e - 4][1], order[e - 4][0]))
                        nc.scalar.activation(sq[e % 4][:, :], tau[:, d, j, :], ACT.Ln, bias=epsc[:, 1:2]).then_inc(*AC.step())
                        nc.scalar.activation(r_[:, d, j, :], r_[:, d, j, :], ACT.Exp,
                                             scale=ndecay[:, C * d + c:C * d + c + 1]).then_inc(*AC.step())
                        nc.scalar.activation(tau[:, d, j, :], tau[:, d, j, :], ACT.Ln, bias=epsc[:, 3:4]
                                             ).then_inc(*AC.step("lns", c, d))
                        if e >= 1:
                            root(order[e - 1])
                        if e == 4:
                            highs(("gg0", "qk")[b])
                    root(order[-1])

                lru_gates(0)
                lru_coefficients(0)
                for c in range(C):
                    if c % 4 == 0:
                        highs(f"gg{c // 4}")
                    ac.wait_ge(*at(PE, f"gg{c // 4}", c % 4))
                    nc.scalar.activation(ybuf[:, c, :], bank(f"gg{c // 4}", c % 4)[:, 0:T], ACT.Gelu_apprx_tanh
                                         ).then_inc(*AC.step("gelu", c))
                lru_gates(1)
                highs("qk")
                lru_coefficients(1)
                for c in range(6):
                    job, b = ("qk", c) if c < 4 else ("kr", c - 4)
                    if c == 4:
                        highs("kr")
                    ac.wait_ge(*at(PE, job, b))
                    if c < 5:
                        nc.scalar.activation((*sq, t[1])[c][:, :], bank(job, b)[:, 0:T], ACT.Square).then_inc(*AC.step("sqq", c))
                    nc.scalar.activation(qkv[:, c, :], bank(job, b)[:, 0:T], ACT.Copy).then_inc(*AC.step("qkv", c))
                ac.wait_ge(*at(VE, "scan", 7))

                def merge(job, dst, c0, label):
                    highs(job)
                    for b in range(4):
                        ac.wait_ge(*at(PE, job, b))
                        nc.scalar.activation(dst[:, c0 + b, :], bank(job, b)[:, 0:T], ACT.Sigmoid
                                             ).then_inc(*AC.step(label, c0 + b))

                merge("m2a", m2, 0, "m2")
                nc.scalar.preload_act_table_set(EXP_LN)
                ac.wait_ge(*at(PE, "stq", QC - 1))
                inverse_root("q", bank("st_qkv", 0), QL)
                ac.wait_ge(*at(PE, "stq", QC + KC - 1))
                ac.wait_ge(*at(VE, "qfull"))
                inverse_root("kv", bank("st_qkv", 1), KVL)
                for k in range(QC):
                    make_high(qnh[:, k, :], qkv[:, k, :], at(VE, "qfull_c", k), "qn_high", k)
                for k in range(KC):
                    make_high(ch[:, k, 0:T], qkv[:, QC + k, :], at(VE, "ckv_full", k), "ckv_high", k)
                merge("m2b", m2, 4, "m2")
                merge("m1a", m1, 0, "m1")
                ac.wait_ge(*at(PE, "cache"))
                for k in range(KC):
                    nc.scalar.activation(ch[:, k, T:TK], bank("cache", 0)[:, k * P:k * P + P], ACT.Copy).then_inc(*AC.step())
                AC.also("cache_high")
                merge("m1b", m1, 4, "m1")
                for c in range(C):
                    make_high(hh[:, c, :], t[c % 2][:, :], at(VE, "lru_full", c), "lru_high", c)
                ac.wait_ge(*at(PE, "outs"))
                nc.scalar.activation(out_c[:, :], bank("outs", 0)[:, 0:KVL], ACT.Copy).then_inc(*AC.step())
                nc.scalar.activation(out_k[:, :], bank("outs", 1)[:, P - ROPE:P], ACT.Copy).then_inc(*AC.step())
                nc.scalar.activation(out_h[:, :], bank("outs", 2)[0:2 * C, 0:P], ACT.Copy).then_inc(*AC.step("outs"))
                highs("qn1")
                ac.wait_ge(*at(VE, "ckv", KC - 1))
                for j in range(2):
                    for g in range(3):
                        ac.wait_ge(*at(PE, "qn", 3 * j + g))
                        dst = qt[:, 2 * j + g, :] if g < 2 else qr[:, j, :]
                        nc.scalar.activation(dst, bank(f"qn{j}", g)[:, 0:T], ACT.Copy, scale=SCALE
                                             ).then_inc(*AC.step("qn", 3 * j + g))
                for g in range(4):
                    ac.wait_ge(*at(PE, "kn", g))
                    nc.scalar.activation(kt[:, g, :], bank("kn", g)[:, :], ACT.Copy).then_inc(*AC.step("kn", g))
                highs("kv")
                for g in range(4):
                    ac.wait_ge(*at(PE, "vv", g))
                    nc.scalar.activation(vv[:, g, :], bank("vv", g)[:, :], ACT.Copy).then_inc(*AC.step("vv", g))
                highs("ol0", ahead=0)

                def turned(s):
                    n = 1 if s % 3 == 0 else 3
                    ac.wait_ge(*at(PE, "turn", s))
                    if s >= 2:
                        ac.wait_ge(*at(PE, "values", s - 2))
                    nc.scalar.activation(sq[2 + s % 2][:, 0:n * P], bank("attn", 2)[:, 0:n * P], ACT.Copy
                                         ).then_inc(*AC.step("pt", s))

                def out_high(g):
                    ac.wait_ge(*at(PE, "values", 6 * g + 5))
                    nc.scalar.activation(oh[:, g, :], bank("attn", 3)[:, 0:T], ACT.Copy).then_inc(*AC.step("o_high", g))

                for s in range(24):
                    n = TP if s % 3 == 0 else TK - TP
                    ac.wait_ge(*at(VE, "max", s))
                    if s >= 2:
                        ac.wait_ge(*at(PE, "turn", s - 2))
                        ac.wait_ge(*at(VE, "probs", s - 2))
                    nc.scalar.activation(sq[s % 2][:, 0:n], bank("attn", s % 2)[:, 0:n], ACT.Exp, bias=negmax[:, s % 2:s % 2 + 1],
                                         accum_out=psums[:, s % 2:s % 2 + 1]).then_inc(*AC.step("exp", s))
                    if s >= 1:
                        turned(s - 1)
                    if s >= 7 and (s - 7) % 6 == 0:
                        out_high((s - 7) // 6)
                    if s % 3 == 1:
                        highs("ol0", ahead=1 + s // 3)
                turned(23)
                out_high(3)
                highs("om1")
                for c in range(C):
                    make_high(hh[:, c, :], ybuf[:, c, :], at(VE, "mix", c), "mix_high", c)

                def y_out(jobs2, which):
                    for c in range(C):
                        job = jobs2[c // 4]
                        if c % 4 == 0:
                            highs(job)
                        ac.wait_ge(*at(PE, job, c % 4))
                        nc.scalar.activation(ybuf[:, c, :], bank(job, c % 4)[:, 0:T], ACT.Copy).then_inc(*AC.step("y", which, c))
                        if c >= 4:
                            ac.wait_ge(*at(PE, "st", which, c - 4))
                        nc.scalar.activation(sq[c % 4][:, :], bank(job, c % 4)[:, 0:T], ACT.Square
                                             ).then_inc(*AC.step("ysq", which, c))
                    ac.wait_ge(*at(PE, "st", which, C - 1))
                    inverse_root(which, bank(f"st_{which}", 0), D)

                nc.scalar.preload_act_table_set(EXP_LN)
                y_out(("wo0", "wo1"), "post1")
                squares("pre2", x, ("x", "post1"))
                ac.wait_ge(*at(PE, "st", "pre2", C - 1))
                inverse_root("pre2", bank("st_pre2", 0), D)
                for c in range(C):
                    make_high(hh[:, c, :], t[c % 2][:, :], at(VE, "hfull", "pre2", c), "hh", "pre2", c)
                for j in range(FC // 2):
                    highs(f"fi{j}")
                    for g in range(2):
                        c = 2 * j + g
                        ac.wait_ge(*at(PE, f"fi{j}", g))
                        if c >= 4:
                            ac.wait_ge(*at(VE, "hid", c - 4))
                        nc.scalar.activation(sq[c % 4][:, :], bank(f"fi{j}", g)[:, 0:T], ACT.Silu).then_inc(*AC.step("silu", c))
                    for g in range(2):
                        c = 2 * j + g
                        if c == 0:
                            ac.wait_ge(*at(PE, "om1", 3))
                        make_high(hidh[:, c, :], t[c % 2][:, :], at(VE, "hid", c), "hid_high", c)
                nc.scalar.preload_act_table_set(EXP_LN)
                y_out(("fo0", "fo1"), "post2")

        @block.vector
        def _(ve):
            for c in range(C):
                ve.wait_ge(start_pe, 3 + c)
                nc.vector.tensor_copy(x[:, c, :], ps[c][:, 0:T]).then_inc(start_ve, 1)
            ve.wait_ge(start_load, 16 * 11)
            ve.wait_ge(start_ac, 1)
            ve.wait_ge(start_gp, 6)
            tok_flat = ybuf[:, :, :].rearrange("p c t -> p (c t)")
            ve.wait_ge(start_pe, 2 + C + 1)
            for r in NEXT:
                nc.vector.tensor_copy(tok_flat[:, 512 * r:512 * r + 512], ps[r][:, :]).then_inc(start_ve, 1)
            ve.wait_ge(start_pe, 2 + C + 2)
            nc.vector.tensor_copy(mod[:, 0:16, :], ps[4][:, 0:32].rearrange("p (g c) -> p g c", c=2)).then_inc(start_ve, 1)
            ve.wait_ge(start_ve, C + 5)
            ve.sem_inc(VE.sem, VE.total)
            with ve.Fori(0, DEPTH) as l:
                at = in_layer(l)

                def own():
                    ve.wait_ge(*last(l, VE))

                jobs_reads = dict(jobs)
                host_of = {r: host for r, host, _ in MODS}
                fold_of = {r: job for r, _, job in MODS}

                def scalar_reads(job):
                    for s, *label in jobs_reads[job]:
                        if s is AC:
                            ve.wait_ge(*at(s, *label))

                def mod_partial(r):
                    job = host_of[r]
                    ve.wait_ge(*at(PE, job, 3))
                    scalar_reads(job)
                    for b in range(4):
                        ins = nc.vector.tensor_copy(partial[:, P * b:P * b + P], bank(job, b)[:, T:512])
                        ins.then_inc(*VE.step(*(("partial", r) if b == 3 else ())))

                def mod_result(r):
                    job = fold_of[r]
                    ve.wait_ge(*at(PE, "fold", r))
                    ve.wait_ge(*at(PE, job, 0))
                    scalar_reads(job)
                    o = bank(job, 0)[:, T:T + 8].rearrange("p (g c) -> p g c", c=2)
                    if r in NEXT:
                        nc.vector.tensor_copy(mod[:, 4 * r:4 * r + 4, :], o).then_inc(*VE.step("mod", r))
                    else:
                        bias = par[:, 4 * r:4 * r + 4].rearrange("p (g a) -> p g a", a=1).to_broadcast([P, 4, 2])
                        nc.vector.tensor_tensor(mod[:, 4 * r:4 * r + 4, :], o, bias, ALU.add).then_inc(*VE.step("mod", r))

                def vec2(name):
                    return par_cols(name).rearrange("p (g a) -> p g a", a=1).to_broadcast([P, C, 2])

                def gain(dst, m, name, one, label):
                    own()
                    nc.vector.scalar_tensor_tensor(out=dst[:, :, :], in0=mod[:, m * C:m * C + C, :], scalar=one, in1=vec2(name),
                                                   op0=ALU.add, op1=ALU.mult).then_inc(*VE.step(*label))

                def normalise(which, dst_scale, shift):
                    ve.wait_ge(*at(AC, "rstd", which))

                    def low(c):
                        ve.wait_ge(*at(AC, "hh", which, c))
                        nc.vector.tensor_tensor(hl[:, c, :], t[c % 2][:, :], hh[:, c, :].bitcast(F), ALU.subtract
                                                ).then_inc(*VE.step("h", which, c))

                    for c in range(C):
                        if c >= 2:
                            own()
                        nc.vector.tensor_tensor(t[c % 2][:, :], x[:, c, :], rstd[:, :], ALU.mult).then_inc(*VE.step())
                        own()
                        for g, toks in GROUPS:
                            nc.vector.tensor_scalar(t[c % 2][:, toks], t[c % 2][:, toks], dst_scale[:, c, g:g + 1],
                                                    mod[:, shift * C + c, g:g + 1], ALU.mult, ALU.add).then_inc(*VE.step())
                        VE.also("hfull", which, c)
                        if c >= 1:
                            low(c - 1)
                    low(C - 1)

                def residual(which, gains):
                    ve.wait_ge(*at(AC, "rstd", which))
                    nc.vector.tensor_tensor(t[0][:, :], ybuf[:, 0, :], rstd[:, :], ALU.mult).then_inc(*VE.step())
                    for c in range(C):
                        if c + 1 < C:
                            if c >= 1:
                                own()
                            nc.vector.tensor_tensor(t[(c + 1) % 2][:, :], ybuf[:, c + 1, :], rstd[:, :], ALU.mult
                                                    ).then_inc(*VE.step())
                        own()
                        for g, toks in GROUPS:
                            nc.vector.scalar_tensor_tensor(out=x[:, c, toks], in0=t[c % 2][:, toks], scalar=gains[:, c, g:g + 1],
                                                           in1=x[:, c, toks], op0=ALU.mult, op1=ALU.add).then_inc(*VE.step())
                        VE.also("x", which, c)

                ve.wait_ge(*at(PE, "par", 0))
                nc.vector.tensor_copy(par[:, 0:NA], bank("par", 0)[:, 0:NA]).then_inc(*VE.step("par", 0))
                ve.wait_ge(*at(PE, "par", 1))
                nc.vector.tensor_copy(par[:, NA:NA + NB], bank("par", 1)[:, 0:NB]).then_inc(*VE.step("par", 1))
                own()
                nc.vector.tensor_scalar(lam[3][:, :], par_cols("lru_lambda"), -1.0, None, ALU.mult).then_inc(*VE.step())
                own()
                nc.vector.tensor_tensor(lam[1][:, :], lam[3][:, :], par_cols("lru_lambda"), ALU.max).then_inc(*VE.step("abslam"))
                ve.wait_ge(*at(AC, "explam"))
                nc.vector.tensor_scalar(lam[2][:, :], lam[0][:, :], 1.0, None, ALU.add).then_inc(*VE.step("onelam"))
                ve.wait_ge(*at(AC, "lnlam"))
                own()
                nc.vector.tensor_scalar(lam[2][:, :], lam[2][:, :], -1.0, TINY, ALU.add, ALU.add).then_inc(*VE.step())
                nc.vector.tensor_scalar(lam[1][:, :], lam[1][:, :], TINY, None, ALU.add).then_inc(*VE.step())
                own()
                nc.vector.reciprocal(lam[2][:, :], lam[2][:, :]).then_inc(*VE.step())
                nc.vector.tensor_tensor(lam[0][:, :], lam[0][:, :], lam[1][:, :], ALU.mult).then_inc(*VE.step())
                own()
                nc.vector.tensor_tensor(lam[0][:, :], lam[0][:, :], lam[2][:, :], ALU.mult).then_inc(*VE.step())
                own()
                nc.vector.scalar_tensor_tensor(out=lam[3][:, :], in0=lam[3][:, :], scalar=0.0, in1=lam[0][:, :],
                                               op0=ALU.max, op1=ALU.add).then_inc(*VE.step())
                own()
                nc.vector.tensor_scalar(decay[:, :], lam[3][:, :], 8.0, None, ALU.mult).then_inc(*VE.step())
                nc.vector.tensor_scalar(ndecay[:, :], lam[3][:, :], -8.0, None, ALU.mult).then_inc(*VE.step("decay"))
                first = par[:, 0:16].rearrange("p (g a) -> p g a", a=1).to_broadcast([P, 16, 2])
                nc.vector.tensor_tensor(mod[:, 0:16, :], mod[:, 0:16, :], first, ALU.add).then_inc(*VE.step())
                gain(scale1, 1, "g_pre_mix", 1.0, ("scale1",))
                normalise("pre1", scale1, 0)

                def xc_low(c):
                    ve.wait_ge(*at(AC, "xc_high", c))
                    nc.vector.tensor_tensor(xcl[:, c % 2, :], xc[:, c, :], xch[:, c % 2, :].bitcast(F), ALU.subtract
                                            ).then_inc(*VE.step("xc_low", c))

                for c in range(C):
                    ve.wait_ge(*at(AC, "conv", c))
                    src = bank(f"lx{c // 4}", c % 4)
                    for i, (tap, off) in enumerate(((0, -2), (1, -1), (3, 1))):
                        for g, toks in GROUPS:
                            a, b = toks.start, toks.stop
                            dst = slice(a - min(off, 0), b - max(off, 0))
                            frm = slice(dst.start + off, dst.stop + off)
                            if i:
                                ve.wait_ge(VE.sem, l * VE.total + VE.count - 1 + VE.total)
                            nc.vector.scalar_tensor_tensor(out=xc[:, c, dst], in0=src[:, frm], scalar=par_col("conv_w", tap * C + c),
                                                           in1=xc[:, c, dst], op0=ALU.mult, op1=ALU.add).then_inc(*VE.step())
                    VE.also("conv", c)
                    if c == 3:
                        xc_low(0)
                        xc_low(1)
                        mod_partial(4)

                def scans(c, j):
                    b = c // 4
                    for d in range(2):
                        ve.wait_ge(*at(AC, "root", c, d))
                        nc.vector.tensor_tensor(i_[:, d, j, :], i_[:, d, j, :], tau[:, d, j, :], ALU.mult).then_inc(*VE.step())
                    own()
                    for d in range(2):
                        nc.vector.tensor_tensor(i_[:, d, j, :], i_[:, d, j, :], xc[:, c, :], ALU.mult).then_inc(*VE.step())
                    own()
                    for g, toks in GROUPS:
                        init = 0.0 if g == 0 else par_col("state_lru_fwd", c)
                        nc.vector.tensor_tensor_scan(lruh[:, c, toks], r_[:, 0, j, toks], i_[:, 0, j, toks], init,
                                                     ALU.mult, ALU.add).then_inc(*VE.step())
                    for g, toks in GROUPS:
                        init = 0.0 if g == 0 else par_col("state_lru_bwd", c)
                        nc.vector.tensor_tensor_scan(tau[:, 1, j, toks][:, ::-1], r_[:, 1, j, toks][:, ::-1],
                                                     i_[:, 1, j, toks][:, ::-1], init, ALU.mult, ALU.add).then_inc(*VE.step())
                    own()
                    nc.vector.tensor_copy(hst[:, 0, c:c + 1], lruh[:, c, TP - 1:TP]).then_inc(*VE.step())
                    nc.vector.tensor_copy(hst[:, 1, c:c + 1], tau[:, 1, j, 0:1]).then_inc(*VE.step())
                    own()
                    nc.vector.tensor_tensor(lruh[:, c, :], lruh[:, c, :], tau[:, 1, j, :], ALU.add).then_inc(*VE.step("scan", c))

                def recurrence(b):
                    for j in range(4):
                        c = 4 * b + j
                        if c >= 2:
                            xc_low(c)
                    def lnroot(c, j, d, e):
                        ve.wait_ge(*at(AC, "lns", c, d))
                        nc.vector.tensor_tensor(tau[:, d, j, :], sq[e % 4][:, :], tau[:, d, j, :], ALU.subtract
                                                ).then_inc(*VE.step("lnroot", c, d))
                    for j in range(4):
                        for d in range(2):
                            lnroot(4 * b + j, j, d, 2 * j + d)
                        if j >= 1:
                            scans(4 * b + j - 1, j - 1)
                    scans(4 * b + 3, 3)

                mod_result(4)
                recurrence(0)
                mod_partial(5)
                recurrence(1)
                mod_result(5)
                mod_partial(6)
                VE.also("states")
                ve.wait_ge(*at(AC, "rstd", "q"))
                for k in range(QC):
                    nc.vector.scalar_tensor_tensor(out=qkv[:, k, :], in0=qkv[:, k, :], scalar=par_col("g_q", k), in1=rstd[:, :],
                                                   op0=ALU.mult, op1=ALU.mult).then_inc(*VE.step("qfull_c", k))
                VE.also("qfull")
                ve.wait_ge(*at(AC, "rstd", "kv"))
                for k in range(KC):
                    nc.vector.scalar_tensor_tensor(out=qkv[:, QC + k, :], in0=qkv[:, QC + k, :], scalar=par_col("g_kv", k),
                                                   in1=rstd[:, :], op0=ALU.mult, op1=ALU.mult).then_inc(*VE.step("ckv_full", k))
                for k in range(QC):
                    ve.wait_ge(*at(AC, "qn_high", k))
                    nc.vector.tensor_tensor(qnl[:, k, :], qkv[:, k, :], qnh[:, k, :].bitcast(F), ALU.subtract
                                            ).then_inc(*VE.step("qn", k))
                for k in range(KC):
                    ve.wait_ge(*at(AC, "ckv_high", k))
                    nc.vector.tensor_tensor(cl[:, k, 0:T], qkv[:, QC + k, :], ch[:, k, 0:T].bitcast(F), ALU.subtract
                                            ).then_inc(*VE.step("ckv", k))
                mod_result(6)
                mod_partial(7)
                ve.wait_ge(*at(PE, "krot"))
                nc.vector.tensor_copy(kr[:, 0:TP], bank("krot", 0)[:, 0:TP]).then_inc(*VE.step())
                nc.vector.tensor_tensor(kr[:, TP:T], bank("krot", 0)[:, TP:T], cos[:, :], ALU.mult).then_inc(*VE.step())
                nc.vector.tensor_tensor(t[0][:, 0:TS], bank("krot", 1)[:, 0:TS], sin[:, :], ALU.mult).then_inc(*VE.step("krot"))
                own()
                nc.vector.tensor_tensor(kr[:, TP:T], kr[:, TP:T], t[0][:, 0:TS], ALU.add).then_inc(*VE.step())
                ve.wait_ge(*at(AC, "cache_high"))
                for k in range(KC):
                    nc.vector.tensor_tensor(cl[:, k, T:TK], bank("cache", 0)[:, k * P:k * P + P], ch[:, k, T:TK].bitcast(F),
                                            ALU.subtract).then_inc(*VE.step())
                VE.also("ckv_cache")
                nc.vector.tensor_copy(kr[:, T:TK], bank("cache", 1)[:, 0:P]).then_inc(*VE.step("cache"))
                mod_result(7)
                ve.wait_ge(*at(PE, "m1b", 3))

                def lru_low(c):
                    ve.wait_ge(*at(AC, "lru_high", c))
                    nc.vector.tensor_tensor(hl[:, c, :], t[c % 2][:, :], hh[:, c, :].bitcast(F), ALU.subtract
                                            ).then_inc(*VE.step("lru_low", c))

                for c in range(C):
                    own()
                    nc.vector.tensor_tensor(t[c % 2][:, :], lruh[:, c, :], ybuf[:, c, :], ALU.mult).then_inc(*VE.step("lru_full", c))
                    if c >= 1:
                        lru_low(c - 1)
                lru_low(C - 1)
                mod_partial(8)
                for j in range(2):
                    ve.wait_ge(*at(PE, "qrot", j))
                    own()
                    nc.vector.tensor_tensor(t[j][:, 0:TS], bank("qrot", j)[:, 0:TS], sin[:, :], ALU.mult).then_inc(*VE.step())
                    nc.vector.tensor_tensor(qr[:, j, TP:T], qr[:, j, TP:T], cos[:, :], ALU.mult).then_inc(*VE.step())
                    own()
                    nc.vector.tensor_tensor(qr[:, j, TP:T], qr[:, j, TP:T], t[j][:, 0:TS], ALU.add).then_inc(*VE.step())
                VE.also("qrot")

                def mix_lru(b):
                    for c in range(4 * b, 4 * b + 4):
                        ve.wait_ge(*at(PE, f"ol{b}", c % 4))
                        nc.vector.tensor_tensor(ybuf[:, c, :], bank(f"ol{b}", c % 4)[:, 0:T], m2[:, c, :], ALU.mult
                                                ).then_inc(*VE.step("mix_lru", c))

                def divide(s):
                    n = TP if s % 3 == 0 else TK - TP
                    ve.wait_ge(*at(AC, "exp", s))
                    nc.vector.reciprocal(prec[:, s % 2:s % 2 + 1], psums[:, s % 2:s % 2 + 1]).then_inc(*VE.step())
                    own()
                    nc.vector.tensor_scalar(sq[s % 2][:, 0:n], sq[s % 2][:, 0:n], prec[:, s % 2:s % 2 + 1], None, ALU.mult
                                            ).then_inc(*VE.step("probs", s))

                def out_low(g):
                    ve.wait_ge(*at(AC, "o_high", g))
                    nc.vector.tensor_tensor(ol[:, g, :], bank("attn", 3)[:, 0:T], oh[:, g, :].bitcast(F), ALU.subtract
                                            ).then_inc(*VE.step("o_low", g))

                for s in range(24):
                    n = TP if s % 3 == 0 else TK - TP
                    ve.wait_ge(*at(PE, "scores", s))
                    nc.vector.tensor_reduce(negmax[:, s % 2:s % 2 + 1], bank("attn", s % 2)[:, 0:n], AX.X, ALU.max, negate=True
                                            ).then_inc(*VE.step("max", s))
                    if s >= 8 and (s - 8) % 6 == 0:
                        out_low((s - 8) // 6)
                    if s >= 1:
                        divide(s - 1)
                    if s == 12:
                        mix_lru(0)
                        mod_result(8)
                divide(23)
                out_low(3)
                mix_lru(1)

                def mix_low(c):
                    ve.wait_ge(*at(AC, "mix_high", c))
                    nc.vector.tensor_tensor(hl[:, c, :], ybuf[:, c, :], hh[:, c, :].bitcast(F), ALU.subtract
                                            ).then_inc(*VE.step("mix_low", c))

                for c in range(C):
                    ve.wait_ge(*at(PE, f"om{c // 4}", c % 4))
                    if c >= 2:
                        own()
                    nc.vector.tensor_tensor(t[c % 2][:, :], bank(f"om{c // 4}", c % 4)[:, 0:T], m1[:, c, :], ALU.mult
                                            ).then_inc(*VE.step())
                    own()
                    nc.vector.tensor_tensor(ybuf[:, c, :], ybuf[:, c, :], t[c % 2][:, :], ALU.add).then_inc(*VE.step("mix", c))
                    if c >= 1:
                        mix_low(c - 1)
                mix_low(C - 1)
                mod_partial(9)
                gain(gain1, 2, "g_post_mix", 0.0, ("gain1",))
                own()
                mod_result(9)
                residual("post1", gain1)
                gain(scale2, 4, "g_pre_ffn", 1.0, ("scale2",))
                own()
                normalise("pre2", scale2, 3)

                def hid_low(c):
                    ve.wait_ge(*at(AC, "hid_high", c))
                    nc.vector.tensor_tensor(hidl[:, c, :], t[c % 2][:, :], hidh[:, c, :].bitcast(F), ALU.subtract
                                            ).then_inc(*VE.step("hid_low", c))

                for j in range(FC // 2):
                    for g in range(2):
                        c = 2 * j + g
                        ve.wait_ge(*at(AC, "silu", c))
                        ve.wait_ge(*at(PE, f"fi{j}", 2 + g))
                        own()
                        nc.vector.tensor_tensor(t[c % 2][:, :], bank(f"fi{j}", 2 + g)[:, 0:T], sq[c % 4][:, :], ALU.mult
                                                ).then_inc(*VE.step("hid", c))
                    for g in range(2):
                        c = 2 * j + g
                        if c == 18:
                            ve.wait_ge(*at(stored, "all"))
                        hid_low(c)
                    if f"fi{j}" in HOSTED:
                        mod_partial(HOSTED[f"fi{j}"])
                    if f"fi{j}" in FOLDED:
                        mod_result(FOLDED[f"fi{j}"])
                    if j == 3:
                        gain(gain2, 5, "g_post_ffn", 0.0, ("gain2",))
                mod_result(FOLDED["fo0"])
                residual("post2", gain2)

            for a in range(6):
                ve.wait_ge(end_pe, a + 1)
                tok = ybuf[:, :, :].rearrange("p c t -> p (c t)")
                nc.vector.tensor_copy(tok[:, a * 512:a * 512 + 512], ps[a][:, :]).then_inc(end_ve, 1)

    return {n: (s.labels, s.count) for n, s in new_plan.items()}


_INS = ["x_prompt", "x_sample", "cache_ckv", "cache_krope", "state_lru_fwd", "state_lru_bwd", "c", "c_ctx", "w_mod", "b_mod",
        "g_pre_mix", "g_post_mix", "g_pre_ffn", "g_post_ffn", "w_in", "g_q", "w_q_up", "g_kv", "w_kv_up", "w_o_mla",
        "conv_w", "conv_b", "w_rg", "b_rg", "w_ig", "b_ig", "lru_lambda", "w_o_lru", "w_out", "w_ffn_in", "w_ffn_out"]
_OUTS = [("y_prompt", (1, TP, D)), ("y_sample", (1, TS, D)), ("new_ckv", (1, DEPTH, TP, KVL)),
         ("new_krope", (1, DEPTH, TP, ROPE)), ("new_lru_fwd", (1, DEPTH, LRU)), ("new_lru_bwd", (1, DEPTH, LRU))]


def constants():
    n = ROPE // 4
    inv = np.float32(10000.0) ** (-np.arange(n, dtype=np.float32) / np.float32(n))
    tok = np.arange(TS)
    row, col = (tok // GRID_W).astype(np.float32), (tok % GRID_W).astype(np.float32)
    ang = np.concatenate([row[:, None] * inv, col[:, None] * inv], axis=-1).astype(np.float32)
    ang = np.tile(ang.T, (2 * P // ROPE, 1))
    half = ROPE // 2
    turn = np.zeros((ROPE, ROPE), np.float32)
    for m in range(half):
        turn[m + half, m] = -1.0
        turn[m, m + half] = 1.0
    k = P // ROPE
    return {"ident": np.eye(P, dtype=np.float32), "rot": np.kron(np.eye(k, dtype=np.float32), turn),
            "rep": np.tile(np.eye(ROPE, dtype=np.float32), (k, k)), "reprot": np.tile(turn, (k, k)),
            "fold": np.tile(np.eye(32, 2, dtype=np.float32), (P // 32, 1)), "cos": np.cos(ang).astype(np.float32), "sin": np.sin(ang).astype(np.float32)}


def tensors(nc, arrays):
    A = {n: nc.dram_tensor(f"in_{n}", a.shape, F, kind="ExternalInput").ap() for n, a in arrays.items()}
    A.update({n: nc.dram_tensor(f"out_{n}", shape, F, kind="ExternalOutput").ap() for n, shape in _OUTS})
    return A


def kernel(**inputs):
    import concourse.bacc as _bacc
    from concourse.bass_utils import run_bass_kernel_spmd as _run

    arrays = {n: np.ascontiguousarray(inputs[n]) for n in _INS}
    arrays.update(constants())
    plan = {}
    for _ in range(2):
        nc = _bacc.Bacc("TRN2", target_bir_lowering=False, num_devices=1)
        plan = program(nc, tensors(nc, arrays), plan)
    r = _run(nc, [{f"in_{n}": a for n, a in arrays.items()}], core_ids=[0])
    return tuple(r.results[0][f"out_{n}"] for n, _ in _OUTS)
```

```python
from contextlib import ExitStack

import numpy as np

import concourse.bass as bass
from concourse import mybir

P = 128
D = 1024
DEPTH = 2
PAST = 128
HEADS = 8
NOPE, ROPE, VD = 64, 32, 64
QK = NOPE + ROPE
QL, KVL = 384, 256
LRU = 1024
FF = 2816
NMOD = 6
GRID_W = 64
EPS = 1e-6
TP, TS = 128, 256
T = TP + TS
TK = T + PAST
C = D // P
FC = FF // P
QC, KC = QL // P, KVL // P
OFF_KV = QL
OFF_KR = OFF_KV + KVL
OFF_LX = OFF_KR + ROPE
OFF_LG = OFF_LX + LRU
OFF_MG = OFF_LG + LRU
SCALE = float(QK) ** -0.5
TINY = 1e-30

F = mybir.dt.float32
FR = mybir.dt.float32r
ALU = mybir.AluOpType
ACT = mybir.ActivationFunctionType
AX = mybir.AxisListType
EXP_LN = "natural_log_exp_and_others"

GROUPS = ((0, slice(0, TP)), (1, slice(TP, T)))

ROWS_A = {}
ROWS_B = {}
for _rows, _names in ((ROWS_A, (("b_mod", NMOD * C), ("g_pre_mix", C), ("g_post_mix", C), ("g_pre_ffn", C),
                                ("g_post_ffn", C), ("conv_w", 4 * C), ("conv_b", C))),
                      (ROWS_B, (("b_rg", 2 * C), ("b_ig", 2 * C), ("lru_lambda", 2 * C), ("state_lru_fwd", C),
                                ("state_lru_bwd", C), ("g_q", QC), ("g_kv", KC)))):
    _at = 0
    for _n, _k in _names:
        _rows[_n] = (_at, _k)
        _at += _k
NA = sum(k for _, k in ROWS_A.values())
NB = sum(k for _, k in ROWS_B.values())


MODS = ((4, "lx0", "lx1"), (5, "gg0", "gate5"), (6, "m2a", "small"), (7, "m1a", "outs"), (8, "m1b", "ol0"), (9, "wo0", "wo1"),
        (10, "fi0", "fi1"), (11, "fi2", "fi3"), (0, "fi4", "fi5"), (1, "fi6", "fi7"), (2, "fi8", "fi9"), (3, "fi10", "fo0"))
HOSTED = {host: r for r, host, _ in MODS}
FOLDED = {fold: r for r, _, fold in MODS}
NEXT = range(4)
FOLD_BANK = {"small": 1, "outs": 3}


class Load:

    def __init__(self, job, kc, cols, split, parts):
        self.job, self.kc, self.cols, self.split, self.parts = job, kc, cols, split, parts


def plan_loads():
    loads = []

    def mod(r, quarters):
        for i in quarters:
            loads.append(Load(("mod", r), 2, 512, False, [("rows", "w_mod", 2 * i, 2, r * 512, 512, 0)]))

    def w(job, name, c0, cols=512, chunks=(2, 2, 2, 2), second=None, gates_after_first=None):
        k0 = 0
        for i, kc in enumerate(chunks):
            parts = [("rows", name, k0, kc, c0, cols, 0)]
            if second is not None:
                parts = [("rows", name, k0, kc, c0, cols // 2, 0), ("rows", name, k0, kc, second, cols // 2, cols // 2)]
            loads.append(Load(job, kc, cols, True, parts))
            if job in HOSTED and i in (0, 3):
                mod(HOSTED[job], (0, 1) if i == 0 else (2, 3))
            if i == 0 and gates_after_first is not None:
                gates(gates_after_first)
            k0 += kc

    def gates(b):
        for name in ("w_rg", "w_ig"):
            loads.append(Load(f"gates{b}", 2, 512, True, [("gate", name, d, 4 * b, d * 512) for d in range(2)]))

    w("lx0", "w_in", OFF_LX)
    w("lx1", "w_in", OFF_LX + 512)
    w("gg0", "w_in", OFF_LG, gates_after_first=0)
    w("gg1", "w_in", OFF_LG + 512)
    w("qk", "w_in", 0, gates_after_first=1)
    w("kr", "w_in", 512, 160, (4, 2, 2))
    w("m2a", "w_in", OFF_MG + D)
    w("m2b", "w_in", OFF_MG + D + 512)
    w("m1a", "w_in", OFF_MG)
    w("m1b", "w_in", OFF_MG + 512)
    w("qn0", "w_q_up", 0, 4 * QK, (2, 1))
    w("qn1", "w_q_up", 4 * QK, 4 * QK, (2, 1))
    w("kv", "w_kv_up", 0, 1024, (1, 1))
    w("ol0", "w_o_lru", 0)
    w("ol1", "w_o_lru", 512)
    w("om0", "w_o_mla", 0, chunks=(2, 2))
    w("om1", "w_o_mla", 512, chunks=(2, 2))
    w("wo0", "w_out", 0)
    w("wo1", "w_out", 512)
    for j in range(FC // 2):
        w(f"fi{j}", "w_ffn_in", j * 256, second=FF + j * 256)
    w("fo0", "w_ffn_out", 0, chunks=(2,) * (FC // 2))
    w("fo1", "w_ffn_out", 512, chunks=(2,) * (FC // 2))
    return loads


LOADS = plan_loads()
RAW = 3
SPL = 5
MODR = 2
SPLIT = [n for n, x in enumerate(LOADS) if x.split]
MODL = [n for n, x in enumerate(LOADS) if not x.split]
SIDX = {n: i for i, n in enumerate(SPLIT)}
MIDX = {n: i for i, n in enumerate(MODL)}
assert len(SPLIT) % RAW == 0 and len(SPLIT) % SPL == 0 and len(MODL) % MODR == 0, (len(LOADS), len(SPLIT))


INPUTS_AFTER = {("gg0", 3): (0, 1), ("gg1", 0): (2, 3), ("qk", 3): (4, 5), ("kr", 0): (6, 7)}


def of_job(job):
    return [n for n, x in enumerate(LOADS) if x.job == job]


def pieces(load, dst, src):
    size = load.kc * load.cols
    if load.job[:2] not in ("qn", "kv"):
        return [(dst[:, 0:size], src[:, 0:size])]
    first, head = NOPE, QK if load.job[:2] == "qn" else NOPE + VD
    h = load.cols // head
    d = dst[:, 0:size].rearrange("p (k n) -> p k n", n=load.cols)
    s = src[:, 0:size].rearrange("p (k h e) -> p k h e", k=load.kc, h=h)
    return [(d[:, :, 0:h * first].rearrange("p k (h e) -> p k h e", h=h), s[:, :, :, 0:first]),
            (d[:, :, h * first:].rearrange("p k (h e) -> p k h e", h=h), s[:, :, :, first:])]


class Steps:

    def __init__(self, sem, labels, total):
        self.sem, self.known, self.total = sem, labels, total
        self.count, self.labels = 0, {}

    def step(self, *label, by=1):
        self.count += by
        if label:
            assert label not in self.labels, label
            self.labels[label] = self.count
        return self.sem, by

    def value(self, *label):
        return self.known[label] if self.known else 1

    def also(self, *label):
        self.labels[label] = self.count


def program(nc, A, plan):
    new_plan = {}
    with ExitStack() as ctx:
        def sb(name, shape, dt=F):
            return ctx.enter_context(nc.sbuf_tensor(name, shape, dt))

        def sem(name):
            return ctx.enter_context(nc.semaphore(name))

        def steps(name):
            labels, total = plan.get(name, ({}, 1))
            s = Steps(sem(name), labels, total)
            new_plan[name] = s
            return s

        raw = [sb(f"raw{s}", [P, 1024]) for s in range(RAW)]
        wh = [sb(f"weight_high{s}", [P, 1024], FR) for s in range(SPL)]
        wl = [sb(f"weight_low{s}", [P, 1024], FR) for s in range(SPL)]
        modw = [sb(f"mod_weight{s}", [P, 1024]) for s in range(MODR)]
        x = sb("x", [P, C, T])
        hh = sb("act_high", [P, C, T], FR)
        hl = sb("act_low", [P, C, T], FR)
        REGION = 2 * FC * T * 4
        arena_at = -(-nc.sbuf_base // 32) * 32
        sb("arena", [P, REGION // 4])
        ybuf = sb("ybuf", [P, C, T])
        qkv = sb("qkv", [P, 6, T])
        ident = sb("ident", [P, P])
        ones = sb("ones", [P, P])
        rot = sb("rot", [P, P])
        rep = sb("rep", [P, P])
        reprot = sb("reprot", [P, P])
        cos = sb("cos", [P, TS])
        sin = sb("sin", [P, TS])
        rows_a = sb("rows_a", [NA, P])
        rows_b = sb("rows_b", [NB, P])
        cache_c = sb("cache_c", [P, KVL])
        cache_k = sb("cache_k", [P, 4, ROPE])
        par = sb("par", [P, NA + NB])
        mod = sb("mod", [P, NMOD * C, 2])
        scale1 = sb("scale1", [P, C, 2])
        scale2 = sb("scale2", [P, C, 2])
        gain1 = sb("gain1", [P, C, 2])
        gain2 = sb("gain2", [P, C, 2])
        cs = sb("cs", [P, C, 32])
        partial = sb("mod_partial", [P, 512])
        fold = sb("mod_fold", [P, 2])
        lam = [sb(f"lam{i}", [P, 2 * C]) for i in range(6)]
        decay, ndecay = lam[4], lam[5]
        hst = sb("hst", [P, 2, C])
        epsc = sb("epsc", [P, 2])
        sq = [sb(f"sq{i}", [P, T]) for i in range(4)]
        t = [sb(f"t{i}", [P, T]) for i in range(2)]
        rstd = sb("rstd", [P, T])
        negmax = sb("negmax", [P, 2])
        psums = sb("psums", [P, 2])
        prec = sb("prec", [P, 2])

        def region(name, at, shape, dt=F):
            return nc.alloc_sbuf_tensor_at(name, shape, dt, offset=arena_at + at)

        TB = T * 4
        hidh = region("hid_high", 0, [P, FC, T], FR)
        hidl = region("hid_low", FC * TB, [P, FC, T], FR)
        first_mod = region("first_mod", 0, [P, len(NEXT), C, 512])
        xc = region("xc", 0, [P, C, T])
        xch = region("xc_high", C * TB, [P, 2, T], FR)
        xcl = region("xc_low", (C + 2) * TB, [P, 2, T], FR)
        r_ = region("lru_r", 12 * TB, [P, 2, 4, T])
        i_ = region("lru_i", 20 * TB, [P, 2, 4, T])
        tau = region("lru_tau", 28 * TB, [P, 2, 4, T])
        lruh = region("lru_h", 36 * TB, [P, C, T])
        m2 = region("merge_lru", 12 * TB, [P, C, T])
        m1 = region("merge_mla", 20 * TB, [P, C, T])
        qnh = region("qn_high", 0, [P, QC, T], FR)
        qnl = region("qn_low", QC * TB, [P, QC, T], FR)
        ch = region("ckv_high", 2 * QC * TB, [P, KC, TK], FR)
        cl = region("ckv_low", 2 * QC * TB + KC * TK * 4, [P, KC, TK], FR)
        oh = region("o_high", 0, [P, 4, T], FR)
        ol = region("o_low", 4 * TB, [P, 4, T], FR)
        kt = region("k_nope", 28 * TB, [P, 4, TK])
        kr = region("k_rope", 28 * TB + 4 * TK * 4, [P, TK])
        vv = region("v", 36 * TB, [P, 4, HEADS * VD])
        out_at = 28 * TB + 5 * TK * 4
        out_c = region("out_ckv", out_at, [P, KVL])
        out_k = region("out_krope", out_at + KVL * 4, [P, ROPE])
        out_h = region("out_state", out_at + (KVL + ROPE) * 4, [2 * C, P])
        qt = qkv[:, 0:4, :]
        qr = qkv[:, 4:6, :]

        ps = [ctx.enter_context(nc.psum_tensor(f"bank{i}", [P, 512], F)) for i in range(8)]

        tensor_done = steps("tensor_done")
        scalar_done = steps("scalar_done")
        vector_done = steps("vector_done")
        gpsimd_done = steps("gpsimd_done")
        raw_full = [steps(f"raw_full{s}") for s in range(RAW)]
        mod_full = [steps(f"mod_full{s}") for s in range(MODR)]
        rows_full = steps("rows_full")
        cache_full = steps("cache_full")
        stored = steps("stored")
        PE, AC, VE, GP = tensor_done, scalar_done, vector_done, gpsimd_done
        sync_passed = sem("sync_passed")
        start_load = sem("start_load")
        start_mod = [sem(f"start_mod{r}") for r in NEXT]
        start_pe = sem("start_pe")
        start_ve = sem("start_ve")
        start_ac = sem("start_ac")
        start_gp = sem("start_gp")
        end_pe = sem("end_pe")
        end_ve = sem("end_ve")
        end_store = sem("end_store")

        def in_layer(l):
            def at(s, *label, prev=False):
                return s.sem, l * s.total + s.value(*label) + (0 if prev else s.total)
            return at

        def last(l, s):
            return s.sem, l * s.total + s.count + s.total

        def residual(engine, own_sem, at, own, which):
            chunks = [c for c in range(C) if adder(c) is own_sem]

            def product(c):
                engine.tensor_tensor(ybuf[:, c, :], ybuf[:, c, :], rstd[:, :], ALU.mult).then_inc(*own_sem.step("yn", which, c))

            product(chunks[0])
            for i, c in enumerate(chunks):
                if i + 1 < len(chunks):
                    product(chunks[i + 1])
                own(*at(own_sem, "yn", which, c))
                engine.tensor_tensor(x[:, c, :], x[:, c, :], ybuf[:, c, :], ALU.add).then_inc(*own_sem.step("x", which, c))

        def adder(c):
            return GP if c in (2, 4, 6) else VE

        def par_col(name, i):
            rows, off = (ROWS_A, 0) if name in ROWS_A else (ROWS_B, NA)
            return par[:, off + rows[name][0] + i:off + rows[name][0] + i + 1]

        def par_cols(name):
            rows, off = (ROWS_A, 0) if name in ROWS_A else (ROWS_B, NA)
            return par[:, off + rows[name][0]:off + rows[name][0] + rows[name][1]]

        jobs = [("par", [(VE, "par", 1)]), ("st_pre1", [(AC, "rs", "pre1")]),
                ("lx0", [(VE, "lx", 3)]), ("lx1", [(VE, "lx", 7)])]
        none = ("none", [])
        jobs += [("gg0", [(AC, "gate_input", 3)])]
        jobs += [x for n in range(0, 4) for x in ((f"gate{n}", [(AC, "gate", n)]), none)]
        jobs += [("gg1", [(AC, "gelu", 7)]), ("qk", [(AC, "qkv", 3)])]
        jobs += [x for n in range(4, 8) for x in ((f"gate{n}", [(AC, "gate", n)]), none)]
        jobs += [("kr", [(AC, "qkv", 5)]), ("m2a", [(AC, "m2", 3)]), ("st_qkv", [(AC, "rs", "kv")]), none,
                 ("m2b", [(AC, "m2", 7)]), ("m1a", [(AC, "m1", 3)]), ("small", [(VE, "krot"), (VE, "cache")]), none,
                 ("m1b", [(AC, "m1", 7)]), ("outs", [(AC, "outs")]), none,
                 ("qn0", [(AC, "qn", 2)]), ("qn1", [(AC, "qn", 5)]), ("kn", [(AC, "kn", 3)]), ("vv", [(AC, "vv", 3)]),
                 ("qrot", [(VE, "qrot")]),
                 ("attn", [(AC, "pt", 23), (VE, "o_low", 3)]), ("ol0", [(VE, "mix_lru", 3)]), none,
                 ("ol1", [(VE, "mix_lru", 7)]),
                 ("om0", [(VE, "mix", 3)]), ("om1", [(VE, "mix", 7)]),
                 ("wo0", [(VE, "y", "post1", 3)]), ("wo1", [(VE, "y", "post1", 7)]), ("st_post1", [(AC, "rs", "post1")]),
                 ("st_pre2", [(AC, "rs", "pre2")])]
        for j in range(FC // 2):
            jobs.append((f"fi{j}", [(AC, "silu", 2 * j + 1), (VE, "hid", 2 * j + 1)]))
        jobs += [("fo0", [(VE, "y", "post2", 3)]), ("fo1", [(VE, "y", "post2", 7)]), ("st_post2", [(AC, "rs", "post2")])]
        for name, reads in jobs:
            if name in HOSTED:
                reads.append((VE, "partial", HOSTED[name]))
            if name in FOLDED:
                reads.append((VE, "mod", FOLDED[name]))
        names = [n for n, _ in jobs]
        if len(jobs) % 2:
            jobs.insert(names.index("attn"), ("none", []))
            names = [n for n, _ in jobs]
        set_of = {n: i % 2 for i, (n, _) in enumerate(jobs)}

        def bank(job, b):
            return ps[4 * set_of[job] + b]

        def reads_before(job):
            i = names.index(job)
            k = i - 2
            while not jobs[k][1]:
                k -= 2
            return [(r, k < 0) for r in jobs[k][1]]

        block = ctx.enter_context(nc.Block())

        @block.sync
        def _(sp):
            consts = ((ident, "ident"), (rot, "rot"), (rep, "rep"), (reprot, "reprot"), (cos, "cos"), (sin, "sin"), (fold, "fold"))
            for buf, name in consts:
                sp.dma_start(buf[:, :], A[name]).then_inc(start_load, 16)
            sp.dma_start(rows_b[0:C, :], A["c_ctx"].rearrange("(n p) -> n p", p=P)).then_inc(start_load, 16)
            sp.dma_start(rows_b[C:2 * C, :], A["c"].rearrange("b (n p) -> (b n) p", p=P)).then_inc(start_load, 16)
            tok = ybuf[:, :, :].rearrange("p c t -> p (c t)").rearrange("p (a d) -> p a d", d=D)
            sp.dma_start(tok[:, 0, :], A["x_prompt"].rearrange("b t d -> (b t) d")).then_inc(start_load, 16)
            sp.dma_start(tok[:, 1:3, :], A["x_sample"].rearrange("b (a p) d -> p (b a) d", p=P)).then_inc(start_load, 16)
            for r in NEXT:
                sp.dma_start(first_mod[:, r, :, :], A["w_mod"][0:1, :, r * 512:r * 512 + 512].rearrange("a (k p) n -> p (a k) n", p=P)
                             ).then_inc(start_mod[r], 16)

            with sp.Fori(0, DEPTH) as l:
                at = in_layer(l)

                def vector_rows():
                    sp.wait_ge(*at(PE, "par", 1, prev=True))
                    sp.sem_inc(sync_passed, 1)
                    sp.wait_ge(start_pe, 2)
                    for dst, rows in ((rows_a, ROWS_A), (rows_b, ROWS_B)):
                        for name, (r0, k) in rows.items():
                            src = A[name]
                            if name.startswith("state"):
                                src = src[0:1, bass.ds(l, 1), :].rearrange("b a (n p) -> (b a n) p", p=P)
                            elif len(src.shape) == 3:
                                src = src[bass.ds(l, 1), :, :].rearrange("a w (n p) -> (a w n) p", p=P)
                            else:
                                src = src[bass.ds(l, 1), :].rearrange("a (n p) -> (a n) p", p=P)
                            sp.dma_start(dst[r0:r0 + k, :], src).then_inc(*rows_full.step(by=16))
                    rows_full.also("all")

                def cache_rows():
                    sp.wait_ge(*at(PE, "cache", prev=True))
                    sp.sem_inc(sync_passed, 1)
                    sp.dma_start(cache_c[:, :], A["cache_ckv"][0:1, bass.ds(l, 1), :, :].rearrange("b a t d -> (b a t) d")
                                 ).then_inc(*cache_full.step(by=16))
                    for q in range(4):
                        sp.dma_start(cache_k[:, q, :], A["cache_krope"][0:1, bass.ds(l, 1), :, :].rearrange(
                            "b a t d -> (b a t) d")).then_inc(*cache_full.step(by=16))
                    cache_full.also("all")

                def stores():
                    sp.wait_ge(*at(AC, "outs"))
                    sp.sem_inc(sync_passed, 1)
                    sp.dma_start(A["new_ckv"][0:1, bass.ds(l, 1), :, :].rearrange("b a t d -> (b a t) d"), out_c[:, :]
                                 ).then_inc(*stored.step(by=16))
                    sp.dma_start(A["new_krope"][0:1, bass.ds(l, 1), :, :].rearrange("b a t d -> (b a t) d"), out_k[:, :]
                                 ).then_inc(*stored.step(by=16))
                    for d, name in enumerate(("new_lru_fwd", "new_lru_bwd")):
                        sp.dma_start(A[name][0:1, bass.ds(l, 1), :].rearrange("b a (n p) -> (b a n) p", p=P),
                                     out_h[C * d:C * d + C, :]).then_inc(*stored.step(by=16))
                    stored.also("all")

                for n, load in enumerate(LOADS):
                    if n == 2:
                        vector_rows()
                    if n == of_job("gg0")[0]:
                        cache_rows()
                    if n == of_job("fi2")[0]:
                        stores()
                    if load.split:
                        m = SIDX[n]
                        slot, full = raw[m % RAW], raw_full[m % RAW]
                        sp.wait_ge(*at(GP, "low", SPLIT[m - RAW], prev=m < RAW))
                        sp.sem_inc(sync_passed, 1)
                    else:
                        m = MIDX[n]
                        slot, full = modw[m % MODR], mod_full[m % MODR]
                        sp.wait_ge(*at(PE, "used", MODL[m - MODR], prev=m < MODR))
                        sp.sem_inc(sync_passed, 1)
                    layer = l if load.split or load.job[1] not in NEXT else (l + 1) % DEPTH
                    for part in load.parts:
                        if part[0] == "rows":
                            _, name, k0, kc, c0, cols, o = part
                            dst = slot[:, 0:load.kc * load.cols].rearrange("p (k n) -> p k n", n=load.cols)
                            src = A[name][bass.ds(layer, 1), k0 * P:(k0 + kc) * P, c0:c0 + cols]
                            sp.dma_start(dst[:, :, o:o + cols], src.rearrange("a (k p) n -> p (a k) n", p=P)
                                         ).then_inc(*full.step(by=16))
                        else:
                            _, name, d, n0, o = part
                            dst = slot[:, o:o + 512].rearrange("p (n e) -> p n e", e=P)
                            src = A[name][bass.ds(l, 1), d, n0:n0 + 4, :, :]
                            sp.dma_start(dst, src.rearrange("a n k e -> k (a n) e")).then_inc(*full.step(by=16))
                    full.also("load", n)

            sp.wait_ge(end_ve, 6)
            tok = ybuf[:, :, :].rearrange("p c t -> p (c t)").rearrange("p (a d) -> p a d", d=D)
            sp.dma_start(A["y_prompt"].rearrange("b t d -> (b t) d"), tok[:, 0, :]).then_inc(end_store, 16)
            sp.dma_start(A["y_sample"].rearrange("b (a p) d -> p (b a) d", p=P), tok[:, 1:3, :]).then_inc(end_store, 16)
            sp.wait_ge(end_store, 32)
            sp.wait_ge(stored.sem, DEPTH * stored.total + stored.total)

        @block.gpsimd
        def _(gp):
            nc.gpsimd.memset(ones[:, :], 1.0).then_inc(start_gp, 1)
            nc.gpsimd.memset(cs[:, :, :], 0.0).then_inc(start_gp, 1)
            nc.gpsimd.memset(epsc[:, 0:1], EPS).then_inc(start_gp, 1)
            nc.gpsimd.memset(epsc[:, 1:2], TINY).then_inc(start_gp, 1)
            gp.sem_inc(GP.sem, GP.total)
            for s in (*raw_full, *mod_full, rows_full, cache_full, stored):
                gp.sem_inc(s.sem, s.total)
            with gp.Fori(0, DEPTH) as l:
                at = in_layer(l)

                def residual_share(which):
                    gp.wait_ge(*at(AC, "rstd", which))
                    gp.wait_ge(*at(VE, "y", which, C - 1))
                    residual(nc.gpsimd, GP, at, gp.wait_ge, which)

                for m, n in enumerate(SPLIT):
                    gp.wait_ge(*at(AC, "high", n))
                    load = LOADS[n]
                    for (low, w), (high, _) in zip(pieces(load, wl[m % SPL], raw[m % RAW]), pieces(load, wh[m % SPL], raw[m % RAW])):
                        nc.gpsimd.tensor_tensor(low, w, high.bitcast(F), ALU.subtract).then_inc(*GP.step())
                    GP.also("low", n)
                    if load.job == "fi0" and n == of_job("fi0")[1]:
                        residual_share("post1")
                    for c in INPUTS_AFTER.get((load.job, of_job(load.job).index(n)), ()):
                        gp.wait_ge(*at(AC, "gate", c))
                        gp.wait_ge(*at(VE, "conv", c))
                        for d in range(2):
                            nc.gpsimd.tensor_tensor(i_[:, d, c % 4, :], i_[:, d, c % 4, :], xc[:, c, :], ALU.mult
                                                    ).then_inc(*GP.step("gated", c, d))
                residual_share("post2")

        @block.tensor
        def _(pe):
            def prologue():
                tok = ybuf[:, :, :].rearrange("p c t -> p (c t)").rearrange("p (a d) -> p a d", d=D)
                pe.wait_ge(start_load, 16 * 11)
                nc.tensor.transpose(ps[7][:, 0:2 * C], rows_b[0:2 * C, :], ident[0:2 * C, 0:2 * C]).then_inc(start_pe, 2)
                for c in range(C):
                    if c == 7:
                        pe.wait_ge(start_ac, 1)
                    for a in range(3):
                        ins = nc.tensor.transpose(ps[c][:, a * P:a * P + P], tok[:, a, c * P:c * P + P], ident[:, :])
                    ins.then_inc(start_pe, 1)
                pe.wait_ge(start_ve, C)
                for r in NEXT:
                    pe.wait_ge(start_mod[r], 16)
                    for k in range(C):
                        q = (k + r) % 4
                        ins = nc.tensor.matmul(ps[r][32 * q:32 * q + 32, :], cs[:, k, :], first_mod[:, r, k, :], start=k < 4,
                                               stop=k >= 4, skip_group_check=True)
                    ins.then_inc(start_pe, 1)
                for r in NEXT:
                    pe.wait_ge(start_ve, C + 1 + r)
                    for g in range(4):
                        ins = nc.tensor.matmul(ps[4][:, 8 * r + 2 * g:8 * r + 2 * g + 2],
                                               tok_flat[:, 512 * r + P * g:512 * r + P * g + P], fold[:, :],
                                               start=r == 0 and g == 0, stop=True, skip_group_check=True)
                ins.then_inc(start_pe, 1)

            tok_flat = ybuf[:, :, :].rearrange("p c t -> p (c t)")
            pe.sem_inc(PE.sem, PE.total)
            prologue()
            pe.wait_ge(start_gp, 4)
            pe.wait_ge(start_ve, C + 5)
            pe.wait_ge(start_ac, 1)
            with pe.Fori(0, DEPTH) as l:
                at = in_layer(l)

                def banks_free(job):
                    for (s, *label), prev in reads_before(job):
                        pe.wait_ge(*at(s, *label, prev=prev))

                def split_job(job, high, low, ready=None, groups=None, after=None, between=None):
                    banks_free(job)
                    loads = of_job(job)
                    k = 0
                    total = sum(LOADS[n].kc for n in loads)
                    for i, n in enumerate(loads):
                        load = LOADS[n]
                        s = SIDX[n] % SPL
                        pe.wait_ge(*at(GP, "low", n))
                        view = [w[:, 0:load.kc * load.cols].rearrange("p (k n) -> p k n", n=load.cols) for w in (wh[s], wl[s])]
                        for kk in range(load.kc):
                            if ready is not None:
                                pe.wait_ge(*at(*ready, k))
                            gs = groups or [slice(g * P, g * P + P) for g in range(load.cols // P)]
                            for g, cols in enumerate(gs):
                                o = bank(job, g)[:, 0:T]
                                nc.tensor.matmul(o, view[0][:, kk, cols], high[:, k, :], start=k == 0, stop=False)
                                nc.tensor.matmul(o, view[0][:, kk, cols], low[:, k, :], start=False, stop=False)
                                ins = nc.tensor.matmul(o, view[1][:, kk, cols], high[:, k, :], start=False,
                                                       stop=k == total - 1)
                                if k == total - 1:
                                    ins.then_inc(*PE.step(job, g))
                                elif kk == load.kc - 1 and g == len(gs) - 1:
                                    ins.then_inc(*PE.step())
                                if kk == load.kc - 1 and g == len(gs) - 1:
                                    PE.also("used", n)
                                if between is not None:
                                    between(len(gs) * k + g, len(gs) * total)
                            k += 1
                        if job in HOSTED and i in (0, 2):
                            mod_products(HOSTED[job], job, (0, 1) if i == 0 else (2, 3))
                        if job in FOLDED and i == len(loads) - 2:
                            mod_fold(FOLDED[job], job)
                        if after is not None and i in after:
                            after[i]()

                def mod_products(r, job, quarters):
                    for i in quarters:
                        n = of_job(("mod", r))[i]
                        pe.wait_ge(*at(mod_full[MIDX[n] % MODR], "load", n))
                        for kk in range(2):
                            k = 2 * i + kk
                            for b in range(4):
                                q = (k + b) % 4
                                ins = nc.tensor.matmul(bank(job, b)[32 * q:32 * q + 32, T:512], cs[:, k, :],
                                                       modw[MIDX[n] % MODR][:, 512 * kk + P * b:512 * kk + P * b + P],
                                                       start=False, stop=k >= 4, skip_group_check=True)
                        ins.then_inc(*PE.step("used", n))

                def mod_fold(r, job):
                    pe.wait_ge(*at(VE, "partial", r))
                    b = FOLD_BANK.get(job, 0)
                    for g in range(4):
                        ins = nc.tensor.matmul(bank(job, b)[:, T + 2 * g:T + 2 * g + 2], partial[:, P * g:P * g + P], fold[:, :],
                                               start=g == 0 and b > 0, stop=True, skip_group_check=True)
                    ins.then_inc(*PE.step("fold", r))

                def stat(job, b, c, count, sqlabel):
                    pe.wait_ge(*at(AC, *sqlabel, c))
                    return nc.tensor.matmul(bank(job, b)[:, 0:T], ones[:, :], sq[c % 4][:, :], start=c == 0, stop=c == count - 1)

                banks_free("par")
                pe.wait_ge(*at(rows_full, "all"))
                nc.tensor.transpose(bank("par", 0)[:, 0:NA], rows_a[:, :], ident[0:NA, 0:NA]).then_inc(*PE.step("par", 0))
                nc.tensor.transpose(bank("par", 1)[:, 0:NB], rows_b[:, :], ident[0:NB, 0:NB]).then_inc(*PE.step("par", 1))
                banks_free("st_pre1")
                for c in range(C):
                    stat("st_pre1", 0, c, C, ("sq", "pre1")).then_inc(*PE.step("st", "pre1", c))
                split_job("lx0", hh, hl, ready=(VE, "h", "pre1"))
                split_job("lx1", hh, hl)

                def gate_block(c):
                    loads = of_job(f"gates{c // 4}")
                    j = c % 4
                    if j == 0:
                        pe.wait_ge(*at(GP, "low", loads[1]))
                    banks_free(f"gate{c}")
                    pe.wait_ge(*at(VE, "xc_low", c))
                    for q in range(4):
                        s = SIDX[loads[q // 2]] % SPL
                        cols = slice(512 * (q % 2) + P * j, 512 * (q % 2) + P * j + P)
                        o = bank(f"gate{c}", q)[:, 0:T]
                        nc.tensor.matmul(o, wh[s][:, cols], xch[:, c % 2, :], start=True, stop=False)
                        nc.tensor.matmul(o, wh[s][:, cols], xcl[:, c % 2, :], start=False, stop=False)
                        if q == 0 and f"gate{c}" in FOLDED:
                            mod_fold(FOLDED[f"gate{c}"], f"gate{c}")
                        nc.tensor.matmul(o, wl[s][:, cols], xch[:, c % 2, :], start=False, stop=True
                                         ).then_inc(*PE.step("gate", c, q))
                    if j == 3:
                        for n in loads:
                            PE.also("used", n)

                def gates_between(b):
                    def between(i, count):
                        if i % 6 == 5 and i // 6 < 4:
                            gate_block(4 * b + i // 6)
                    return between

                def once(at_product, do):
                    def between(i, count):
                        if i == at_product:
                            do()
                    return between

                def latent_norms():
                    banks_free("st_qkv")
                    for c in range(QC):
                        pe.wait_ge(*at(AC, "sqq", c))
                        nc.tensor.matmul(bank("st_qkv", 0)[:, 0:T], ones[:, :], sq[c][:, :], start=c == 0, stop=c == QC - 1
                                         ).then_inc(*PE.step("stq", c))
                    for c in range(KC):
                        pe.wait_ge(*at(AC, "sqq", QC + c))
                        nc.tensor.matmul(bank("st_qkv", 1)[:, 0:T], ones[:, :], (sq[3], t[1])[c][:, :], start=c == 0,
                                         stop=c == KC - 1).then_inc(*PE.step("stq", QC + c))

                def keys():
                    banks_free("small")
                    mod_fold(FOLDED["small"], "small")
                    pe.wait_ge(*at(cache_full, "all"))
                    for k in range(KC):
                        nc.tensor.transpose(bank("small", 0)[:, k * P:k * P + P], cache_c[:, k * P:k * P + P], ident[:, :])
                    nc.tensor.transpose(bank("small", 1)[:, 0:P], cache_k[:, :, :].rearrange("p q r -> p (q r)"), ident[:, :]
                                        ).then_inc(*PE.step("cache"))
                    tail = slice(P - ROPE, P)
                    nc.tensor.matmul(bank("small", 2)[:, 0:T], rep[tail, :], qkv[tail, 5, :], start=True, stop=True)
                    nc.tensor.matmul(bank("small", 3)[:, 0:TS], reprot[tail, :], qkv[tail, 5, TP:T], start=True, stop=True
                                     ).then_inc(*PE.step("krot"))

                def rows_out():
                    banks_free("outs")
                    pe.wait_ge(*at(VE, "states"))
                    pe.wait_ge(*at(VE, "ckv_full", KC - 1))
                    for k in range(KC):
                        nc.tensor.transpose(bank("outs", 0)[:, k * P:k * P + P], qkv[:, QC + k, 0:TP], ident[:, :])
                    nc.tensor.transpose(bank("outs", 1)[:, 0:P], qkv[:, QC + KC, 0:TP], ident[:, :])
                    nc.tensor.transpose(bank("outs", 2)[0:2 * C, 0:P], hst[:, :, :].rearrange("p d c -> p (d c)"), ident[:, :]
                                        ).then_inc(*PE.step("outs"))
                    mod_fold(FOLDED["outs"], "outs")

                split_job("gg0", hh, hl, between=gates_between(0))
                split_job("gg1", hh, hl)
                split_job("qk", hh, hl, between=gates_between(1))
                split_job("kr", hh, hl, groups=[slice(0, P), slice(160 - P, 160)])
                split_job("m2a", hh, hl, between=once(24, latent_norms))
                split_job("m2b", hh, hl)
                split_job("m1a", hh, hl, between=once(20, keys))
                split_job("m1b", hh, hl, between=once(20, rows_out))
                for j in range(2):
                    job = f"qn{j}"
                    loads = of_job(job)
                    banks_free(job)
                    for k in range(QC):
                        n, kk = (loads[0], k) if k < 2 else (loads[1], 0)
                        s = SIDX[n] % SPL
                        pe.wait_ge(*at(GP, "low", n))
                        pe.wait_ge(*at(VE, "qn", k))
                        for g in range(3):
                            w2 = [w[:, kk * 4 * QK + g * P:kk * 4 * QK + g * P + P] for w in (wh[s], wl[s])]
                            o = bank(job, g)[:, 0:T]
                            nc.tensor.matmul(o, w2[0], qnh[:, k, :], start=k == 0, stop=False)
                            nc.tensor.matmul(o, w2[0], qnl[:, k, :], start=False, stop=False)
                            ins = nc.tensor.matmul(o, w2[1], qnh[:, k, :], start=False, stop=k == QC - 1)
                            if k == QC - 1:
                                ins.then_inc(*PE.step("qn", 3 * j + g))
                            elif k == 1 and g == 2:
                                ins.then_inc(*PE.step("used", n))
                    PE.also("used", n)
                loads = of_job("kv")
                banks_free("kn")
                pe.wait_ge(*at(VE, "ckv_cache"))
                for k, n in enumerate(loads):
                    s = SIDX[n] % SPL
                    pe.wait_ge(*at(GP, "low", n))
                    pe.wait_ge(*at(VE, "ckv", k))
                    for g in range(4):
                        w2 = [w[:, g * P:g * P + P] for w in (wh[s], wl[s])]
                        o = bank("kn", g)[:, :]
                        nc.tensor.matmul(o, w2[0], ch[:, k, :], start=k == 0, stop=False)
                        nc.tensor.matmul(o, w2[0], cl[:, k, :], start=False, stop=False)
                        ins = nc.tensor.matmul(o, w2[1], ch[:, k, :], start=False, stop=k == KC - 1)
                        if k == KC - 1:
                            ins.then_inc(*PE.step("kn", g))
                banks_free("vv")
                for g in range(4):
                    for k, n in enumerate(loads):
                        s = SIDX[n] % SPL
                        wvh, wvl = (w[:, HEADS * NOPE:HEADS * (NOPE + VD)] for w in (wh[s], wl[s]))
                        o = bank("vv", g)[:, :]
                        tk = slice(g * P, g * P + P)
                        nc.tensor.matmul(o, ch[:, k, tk], wvh, start=k == 0, stop=False)
                        nc.tensor.matmul(o, cl[:, k, tk], wvh, start=False, stop=False)
                        ins = nc.tensor.matmul(o, ch[:, k, tk], wvl, start=False, stop=k == KC - 1)
                    ins.then_inc(*PE.step("vv", g))
                for n in loads:
                    PE.also("used", n)
                banks_free("qrot")
                for j in range(2):
                    pe.wait_ge(*at(AC, "qn", 3 * j + 2))
                    nc.tensor.matmul(bank("qrot", j)[:, 0:TS], rot[:, :], qr[:, j, TP:T], start=True, stop=True
                                     ).then_inc(*PE.step("qrot", j))
                def attention_begin():
                    banks_free("attn")
                    pe.wait_ge(*at(VE, "qrot"))
                    pe.wait_ge(*at(AC, "vv", 3))
                    scores(0)
                    scores(1)

                def scores(s):
                    h, q = divmod(s, 3)
                    if s >= 2:
                        pe.wait_ge(*at(AC, "exp", s - 2))
                    keys = slice(0, TP) if q == 0 else slice(TP, TK)
                    qs = slice(q * P, q * P + P)
                    o = bank("attn", s % 2)[:, 0:keys.stop - keys.start]
                    half, quad = slice(64 * (h % 2), 64 * (h % 2) + 64), slice(32 * (h % 4), 32 * (h % 4) + 32)
                    nc.tensor.matmul(o, qt[half, h // 2, qs], kt[half, h // 2, keys], start=True, stop=False)
                    nc.tensor.matmul(o, qr[quad, h // 4, qs], kr[quad, keys], start=False, stop=True
                                     ).then_inc(*PE.step("scores", s))

                def turn(s):
                    n = 1 if s % 3 == 0 else 3
                    if s >= 1:
                        pe.wait_ge(*at(AC, "pt", s - 1))
                    pe.wait_ge(*at(VE, "probs", s))
                    for k in range(n):
                        ins = nc.tensor.transpose(bank("attn", 2)[:, k * P:k * P + P],
                                                  sq[s % 2][:, k * P:k * P + P], ident[:, :])
                    ins.then_inc(*PE.step("turn", s))

                def values(s):
                    h, q = divmod(s, 3)
                    tiles = (0,) if q == 0 else (1, 2, 3)
                    if h % 2 == 0 and h >= 2 and q == 0:
                        pe.wait_ge(*at(VE, "o_low", h // 2 - 1))
                    pe.wait_ge(*at(AC, "pt", s))
                    half = slice(64 * (h % 2), 64 * (h % 2) + 64)
                    o = bank("attn", 3)[half, q * P:q * P + P]
                    for j, k in enumerate(tiles):
                        ins = nc.tensor.matmul(o, vv[:, k, h * VD:h * VD + VD], sq[2 + s % 2][:, j * P:j * P + P],
                                               start=j == 0, stop=j == len(tiles) - 1)
                    ins.then_inc(*PE.step("values", s))

                def attention_step(s):
                    if s + 2 < 24:
                        scores(s + 2)
                    turn(s)
                    if s >= 1:
                        values(s - 1)

                def attention_steps(first):
                    start = 0 if first else 4

                    def between(i, count):
                        if i == start - 1:
                            attention_begin()
                        if i >= start:
                            n, count = i - start, count - start
                            if (n + 1) * 11 // count > n * 11 // count:
                                attention_step(first + n * 11 // count)
                    return between

                split_job("ol0", hh, hl, ready=(VE, "lru_low"), between=attention_steps(0))
                attention_step(11)
                attention_step(12)
                split_job("ol1", hh, hl, between=attention_steps(13))
                values(23)
                split_job("om0", oh, ol, ready=(VE, "o_low"))
                split_job("om1", oh, ol)
                split_job("wo0", hh, hl, ready=(VE, "mix_low"))

                def ysquares(which, chunks):
                    for c in chunks:
                        if c == 0:
                            banks_free(f"st_{which}")
                        stat(f"st_{which}", 0, c, C, ("ysq", which)).then_inc(*PE.step("st", which, c))

                split_job("wo1", hh, hl, after={1: lambda: ysquares("post1", range(4))})
                ysquares("post1", range(4, C))
                banks_free("st_pre2")
                for c in range(C):
                    stat("st_pre2", 0, c, C, ("sq", "pre2")).then_inc(*PE.step("st", "pre2", c))
                for j in range(FC // 2):
                    split_job(f"fi{j}", hh, hl, ready=(VE, "h", "pre2") if j == 0 else None)
                split_job("fo0", hidh, hidl, ready=(VE, "hid_low"))
                split_job("fo1", hidh, hidl, after={2: lambda: ysquares("post2", range(4))})
                ysquares("post2", range(4, C))

            for s in (VE, GP):
                pe.wait_ge(s.sem, DEPTH * s.total + s.value("x", "post2", C - 1 if s is VE else C - 2))
            for a in range(3):
                for c in range(C):
                    ins = nc.tensor.transpose(ps[2 * a + c // 4][:, (c % 4) * P:(c % 4) * P + P], x[:, c, a * P:a * P + P],
                                              ident[:, :])
                    if c % 4 == 3:
                        ins.then_inc(end_pe, 1)

        @block.scalar
        def _(ac):
            ac.wait_ge(start_pe, 2)
            ac.wait_ge(start_gp, 4)
            nc.scalar.activation(cs[:, :, 0:2], ps[7][:, 0:2 * C].rearrange("p (g c) -> p c g", g=2), ACT.Silu
                                 ).then_inc(start_ac, 1)
            ac.sem_inc(AC.sem, AC.total)
            with ac.Fori(0, DEPTH) as l:
                at = in_layer(l)
                made = [0]

                def highs(job, ahead=2):
                    upto = SIDX[of_job(job)[-1]] + ahead
                    while made[0] <= min(upto, len(SPLIT) - 1):
                        m = made[0]
                        n = SPLIT[m]
                        ac.wait_ge(*at(raw_full[m % RAW], "load", n))
                        ac.wait_ge(*at(PE, "used", SPLIT[m - SPL], prev=m < SPL))
                        for high, w in pieces(LOADS[n], wh[m % SPL], raw[m % RAW]):
                            nc.scalar.activation(high, w, ACT.Copy).then_inc(*AC.step())
                        AC.also("high", n)
                        made[0] += 1

                def highs_to(job, unit):
                    highs(job, ahead=unit + 1 - len(of_job(job)))

                def squares(which, of, label, prev=False, between={}):
                    for c in range(C):
                        ac.wait_ge(*at(adder(c), *label, c, prev=prev))
                        if c >= 4:
                            ac.wait_ge(*at(PE, "st", which, c - 4))
                        nc.scalar.activation(sq[c % 4][:, :], of[:, c, :], ACT.Square).then_inc(*AC.step("sq", which, c))
                        if c in between:
                            highs_to("lx0", between[c])

                def inverse_root(which, src, n, dst=rstd):
                    nc.scalar.activation(dst[:, :], src[:, 0:T], ACT.Ln, scale=1.0 / n, bias=epsc[:, 0:1]
                                         ).then_inc(*AC.step("rs", which))
                    ac.wait_ge(*last(l, AC))
                    nc.scalar.activation(dst[:, :], dst[:, :], ACT.Exp, scale=-0.5).then_inc(*AC.step("rstd", which))

                def make_high(dst, src, label, *out):
                    ac.wait_ge(*label)
                    nc.scalar.activation(dst, src, ACT.Copy).then_inc(*AC.step(*out))

                nc.scalar.preload_act_table_set(EXP_LN)
                squares("pre1", x, ("x", "post2"), prev=True, between={3: 0})
                ac.wait_ge(*at(PE, "st", "pre1", C - 1))
                ac.wait_ge(*at(VE, "x", "post2", C - 1, prev=True))
                ac.wait_ge(*at(GP, "x", "post2", C - 2, prev=True))
                inverse_root("pre1", bank("st_pre1", 0), D)
                highs_to("lx0", 1)
                for c in range(C):
                    make_high(hh[:, c, :], t[c % 2][:, :], at(VE, "hfull", "pre1", c), "hh", "pre1", c)
                    if c in (2, 4):
                        highs_to("lx0", 1 + c // 2)

                ac.wait_ge(*at(VE, "abslam"))
                nc.scalar.activation(lam[0][:, :], lam[1][:, :], ACT.Exp, scale=-1.0).then_inc(*AC.step("explam"))
                highs("lx0", ahead=1)
                ac.wait_ge(*at(VE, "onelam"))
                nc.scalar.activation(lam[1][:, :], lam[2][:, :], ACT.Ln).then_inc(*AC.step("lnlam"))
                highs("lx0")
                for c in range(C):
                    if c == 4:
                        highs("lx1")
                    ac.wait_ge(*at(PE, f"lx{c // 4}", c % 4))
                    nc.scalar.activation(xc[:, c, :], bank(f"lx{c // 4}", c % 4)[:, 0:T], ACT.Identity,
                                         scale=par_col("conv_w", 2 * C + c), bias=par_col("conv_b", c)
                                         ).then_inc(*AC.step("conv", c))
                    if c == 3:
                        highs("lx1", ahead=0)
                        for n in range(2):
                            make_high(xch[:, n, :], xc[:, n, :], at(VE, "conv", n), "xc_high", n)

                def lru_gates(b):
                    job = ("gg0", "qk")[b]
                    for j in range(4):
                        c = 4 * b + j
                        if j < 3:
                            highs_to(job, j + 1)
                        if c >= 2:
                            ac.wait_ge(*at(PE, "gate", c - 2, 3))
                            make_high(xch[:, c % 2, :], xc[:, c, :], at(VE, "conv", c), "xc_high", c)
                        if b == 1 and j == 0:
                            ac.wait_ge(*at(VE, "scan", 3))
                        for q in range(4):
                            ac.wait_ge(*at(PE, "gate", c, q))
                            dst = (r_ if q < 2 else i_)[:, q % 2, j, :]
                            nc.scalar.activation(dst, bank(f"gate{c}", q)[:, 0:T], ACT.Sigmoid,
                                                 bias=par_col("b_rg" if q < 2 else "b_ig", C * (q % 2) + c)
                                                 ).then_inc(*AC.step())
                        AC.also("gate", c)
                        if j == 3:
                            highs_to(("gg1", "kr")[b], 0)
                        ac.wait_ge(*last(l, AC))
                        for d in range(2):
                            nc.scalar.activation(tau[:, d, j, :], r_[:, d, j, :], ACT.Tanh,
                                                 scale=decay[:, C * d + c:C * d + c + 1]).then_inc(*AC.step())
                        AC.also("tau", c)

                def lru_coefficients(b):
                    nc.scalar.preload_act_table_set(EXP_LN)
                    ac.wait_ge(*last(l, AC))
                    order = [(j, d) for j in range(4) for d in range(2)]
                    for e in range(len(order) + 2):
                        if e < len(order):
                            j, d = order[e]
                            c = 4 * b + j
                            nc.scalar.activation(r_[:, d, j, :], r_[:, d, j, :], ACT.Exp,
                                                 scale=ndecay[:, C * d + c:C * d + c + 1]).then_inc(*AC.step("a", c, d))
                        if 1 <= e <= len(order):
                            j, d = order[e - 1]
                            ac.wait_ge(*at(VE, "squared_root", 4 * b + j, d))
                            nc.scalar.activation(tau[:, d, j, :], tau[:, d, j, :], ACT.Ln, bias=epsc[:, 1:2]
                                                 ).then_inc(*AC.step("ln", 4 * b + j, d))
                        if e >= 2:
                            j, d = order[e - 2]
                            ac.wait_ge(*at(AC, "ln", 4 * b + j, d))
                            nc.scalar.activation(tau[:, d, j, :], tau[:, d, j, :], ACT.Exp, scale=0.5
                                                 ).then_inc(*AC.step("root", 4 * b + j, d))
                        if e % 2 and e < len(order):
                            highs_to(*((("gg1", 1), ("gg1", 2), ("gg1", 3), ("qk", 0)),
                                       (("kr", 1), ("kr", 2), ("m2a", 0), ("m2a", 1)))[b][e // 2])
                        for k in ({4: (0,), 5: (1,), 6: (2,), 7: (3,)}, {1: (0, 1), 2: (2,), 3: (3,)})[b].get(e, ()):
                            if b == 1:
                                latents(k)
                            else:
                                ac.wait_ge(*at(PE, "gg0", k))
                                nc.scalar.activation(ybuf[:, k, :], bank("gg0", k)[:, 0:T], ACT.Copy).then_inc(*AC.step("gate_input", k))

                def latents(c):
                    job, b = ("qk", c) if c < 4 else ("kr", c - 4)
                    ac.wait_ge(*at(PE, job, b))
                    if c < 5:
                        nc.scalar.activation((*sq, t[1])[c][:, :], bank(job, b)[:, 0:T], ACT.Square).then_inc(*AC.step("sqq", c))
                    nc.scalar.activation(qkv[:, c, :], bank(job, b)[:, 0:T], ACT.Copy).then_inc(*AC.step("qkv", c))

                lru_gates(0)
                lru_coefficients(0)
                for c in range(C):
                    if c == 4:
                        highs_to("qk", 0)
                    if c < 4:
                        ac.wait_ge(*at(AC, "gate_input", c))
                    else:
                        ac.wait_ge(*at(PE, "gg1", c % 4))
                    nc.scalar.activation(ybuf[:, c, :], ybuf[:, c, :] if c < 4 else bank("gg1", c % 4)[:, 0:T], ACT.Gelu_apprx_tanh
                                         ).then_inc(*AC.step("gelu", c))
                lru_gates(1)
                lru_coefficients(1)
                highs_to("m2a", 1)
                ac.wait_ge(*at(VE, "squared_root", C - 1, 1))
                latents(4)
                latents(5)
                highs_to("m2a", 2)

                def merge(job, dst, c0, label, ahead=2):
                    highs(job, ahead)
                    for b in range(4):
                        ac.wait_ge(*at(PE, job, b))
                        nc.scalar.activation(dst[:, c0 + b, :], bank(job, b)[:, 0:T], ACT.Sigmoid
                                             ).then_inc(*AC.step(label, c0 + b))

                highs("m2a")
                ac.wait_ge(*at(PE, "stq", QC - 1))
                inverse_root("q", bank("st_qkv", 0), QL)
                ac.wait_ge(*at(PE, "stq", QC + KC - 1))
                inverse_root("kv", bank("st_qkv", 1), KVL, sq[0])
                ac.wait_ge(*at(VE, "scan", 7))
                merge("m2a", m2, 0, "m2")
                highs("m2b", ahead=0)
                for k in range(QC):
                    make_high(qnh[:, k, :], qkv[:, k, :], at(VE, "qfull_c", k), "qn_high", k)
                for k in range(KC):
                    make_high(ch[:, k, 0:T], qkv[:, QC + k, :], at(VE, "ckv_full", k), "ckv_high", k)
                merge("m2b", m2, 4, "m2")
                merge("m1a", m1, 0, "m1", ahead=1)
                ac.wait_ge(*at(PE, "cache"))
                for k in range(KC):
                    nc.scalar.activation(ch[:, k, T:TK], bank("small", 0)[:, k * P:k * P + P], ACT.Copy).then_inc(*AC.step())
                AC.also("cache_high")
                highs("m1b")
                ac.wait_ge(*at(PE, "outs"))
                nc.scalar.activation(out_c[:, :], bank("outs", 0)[:, 0:KVL], ACT.Copy).then_inc(*AC.step())
                nc.scalar.activation(out_k[:, :], bank("outs", 1)[:, P - ROPE:P], ACT.Copy).then_inc(*AC.step())
                nc.scalar.activation(out_h[:, :], bank("outs", 2)[0:2 * C, 0:P], ACT.Copy).then_inc(*AC.step("outs"))
                merge("m1b", m1, 4, "m1")

                def lru_highs(chunks):
                    for c in chunks:
                        make_high(hh[:, c, :], t[c % 2][:, :], at(VE, "lru_full", c), "lru_high", c)

                highs("qn1")
                ac.wait_ge(*at(VE, "ckv", KC - 1))
                for j in range(2):
                    for g in range(3):
                        ac.wait_ge(*at(PE, "qn", 3 * j + g))
                        dst = qt[:, 2 * j + g, :] if g < 2 else qr[:, j, :]
                        nc.scalar.activation(dst, bank(f"qn{j}", g)[:, 0:T], ACT.Copy, scale=SCALE
                                             ).then_inc(*AC.step("qn", 3 * j + g))
                    lru_highs((range(0, 3), range(3, 6))[j])
                for g in range(4):
                    ac.wait_ge(*at(PE, "kn", g))
                    nc.scalar.activation(kt[:, g, :], bank("kn", g)[:, :], ACT.Copy).then_inc(*AC.step("kn", g))
                lru_highs(range(6, 8))
                highs_to("ol0", 0)
                for g in range(4):
                    ac.wait_ge(*at(PE, "vv", g))
                    nc.scalar.activation(vv[:, g, :], bank("vv", g)[:, :], ACT.Copy).then_inc(*AC.step("vv", g))
                highs("ol0", ahead=0)

                def turned(s):
                    n = 1 if s % 3 == 0 else 3
                    ac.wait_ge(*at(PE, "turn", s))
                    if s >= 2:
                        ac.wait_ge(*at(PE, "values", s - 2))
                    nc.scalar.activation(sq[2 + s % 2][:, 0:n * P], bank("attn", 2)[:, 0:n * P], ACT.Copy
                                         ).then_inc(*AC.step("pt", s))

                def out_high(g):
                    ac.wait_ge(*at(PE, "values", 6 * g + 5))
                    nc.scalar.activation(oh[:, g, :], bank("attn", 3)[:, 0:T], ACT.Copy).then_inc(*AC.step("o_high", g))

                for s in range(24):
                    n = TP if s % 3 == 0 else TK - TP
                    ac.wait_ge(*at(VE, "max", s))
                    if s >= 2:
                        ac.wait_ge(*at(PE, "turn", s - 2))
                        ac.wait_ge(*at(VE, "probs", s - 2))
                    nc.scalar.activation(sq[s % 2][:, 0:n], bank("attn", s % 2)[:, 0:n], ACT.Exp, bias=negmax[:, s % 2:s % 2 + 1],
                                         accum_out=psums[:, s % 2:s % 2 + 1]).then_inc(*AC.step("exp", s))
                    if s >= 1:
                        turned(s - 1)
                    if s >= 7 and (s - 7) % 6 == 0:
                        out_high((s - 7) // 6)
                    if s % 3 == 1:
                        highs("ol0", ahead=1 + s // 3)
                turned(23)
                out_high(3)
                highs("om1")
                for c in range(C):
                    make_high(hh[:, c, :], ybuf[:, c, :], at(VE, "mix", c), "mix_high", c)

                def y_out(jobs2, which):
                    for c in range(C):
                        job = jobs2[c // 4]
                        if c % 4 == 0:
                            highs(job)
                        ac.wait_ge(*at(PE, job, c % 4))
                        if c >= 4:
                            ac.wait_ge(*at(PE, "st", which, c - 4))
                        nc.scalar.activation(sq[c % 4][:, :], bank(job, c % 4)[:, 0:T], ACT.Square
                                             ).then_inc(*AC.step("ysq", which, c))
                    ac.wait_ge(*at(PE, "st", which, C - 1))
                    inverse_root(which, bank(f"st_{which}", 0), D)

                nc.scalar.preload_act_table_set(EXP_LN)
                y_out(("wo0", "wo1"), "post1")
                squares("pre2", x, ("x", "post1"))
                ac.wait_ge(*at(PE, "st", "pre2", C - 1))
                inverse_root("pre2", bank("st_pre2", 0), D)
                for c in range(C):
                    make_high(hh[:, c, :], t[c % 2][:, :], at(VE, "hfull", "pre2", c), "hh", "pre2", c)
                    if c in (2, 4):
                        highs_to("fi0", 1 + c // 2)
                for j in range(FC // 2):
                    highs(f"fi{j}")
                    for g in range(2):
                        c = 2 * j + g
                        ac.wait_ge(*at(PE, f"fi{j}", g))
                        if c >= 4:
                            ac.wait_ge(*at(VE, "hid", c - 4))
                        nc.scalar.activation(sq[c % 4][:, :], bank(f"fi{j}", g)[:, 0:T], ACT.Silu).then_inc(*AC.step("silu", c))
                    for g in range(2):
                        c = 2 * j + g
                        if c == 0:
                            ac.wait_ge(*at(PE, "om1", 3))
                        make_high(hidh[:, c, :], t[c % 2][:, :], at(VE, "hid", c), "hid_high", c)
                nc.scalar.preload_act_table_set(EXP_LN)
                y_out(("fo0", "fo1"), "post2")

        @block.vector
        def _(ve):
            for c in range(C):
                ve.wait_ge(start_pe, 3 + c)
                nc.vector.tensor_copy(x[:, c, :], ps[c][:, 0:T]).then_inc(start_ve, 1)
            ve.wait_ge(start_load, 16 * 11)
            ve.wait_ge(start_ac, 1)
            ve.wait_ge(start_gp, 4)
            tok_flat = ybuf[:, :, :].rearrange("p c t -> p (c t)")
            for r in NEXT:
                ve.wait_ge(start_pe, 2 + C + 1 + r)
                nc.vector.tensor_copy(tok_flat[:, 512 * r:512 * r + 512], ps[r][:, :]).then_inc(start_ve, 1)
            ve.wait_ge(start_pe, 2 + C + 5)
            nc.vector.tensor_copy(mod[:, 0:16, :], ps[4][:, 0:32].rearrange("p (g c) -> p g c", c=2)).then_inc(start_ve, 1)
            ve.wait_ge(start_ve, C + 5)
            ve.sem_inc(VE.sem, VE.total)
            with ve.Fori(0, DEPTH) as l:
                at = in_layer(l)

                def own():
                    ve.wait_ge(*last(l, VE))

                jobs_reads = dict(jobs)
                host_of = {r: host for r, host, _ in MODS}
                fold_of = {r: job for r, _, job in MODS}

                def scalar_reads(job):
                    for s, *label in jobs_reads[job]:
                        if s is AC:
                            ve.wait_ge(*at(s, *label))

                def mod_partial(r):
                    job = host_of[r]
                    ve.wait_ge(*at(PE, job, 3))
                    scalar_reads(job)
                    for b in range(4):
                        ins = nc.vector.tensor_copy(partial[:, P * b:P * b + P], bank(job, b)[:, T:512])
                        ins.then_inc(*VE.step(*(("partial", r) if b == 3 else ())))

                def mod_result(r):
                    job = fold_of[r]
                    ve.wait_ge(*at(PE, "fold", r))
                    if of_job(job):
                        ve.wait_ge(*at(PE, job, 0))
                    scalar_reads(job)
                    o = bank(job, FOLD_BANK.get(job, 0))[:, T:T + 8].rearrange("p (g c) -> p g c", c=2)
                    if r in NEXT:
                        nc.vector.tensor_copy(mod[:, 4 * r:4 * r + 4, :], o).then_inc(*VE.step("mod", r))
                    else:
                        bias = par[:, 4 * r:4 * r + 4].rearrange("p (g a) -> p g a", a=1).to_broadcast([P, 4, 2])
                        nc.vector.tensor_tensor(mod[:, 4 * r:4 * r + 4, :], o, bias, ALU.add).then_inc(*VE.step("mod", r))

                def vec2(name):
                    return par_cols(name).rearrange("p (g a) -> p g a", a=1).to_broadcast([P, C, 2])

                def gain(dst, m, name, one, label):
                    own()
                    nc.vector.scalar_tensor_tensor(out=dst[:, :, :], in0=mod[:, m * C:m * C + C, :], scalar=one, in1=vec2(name),
                                                   op0=ALU.add, op1=ALU.mult).then_inc(*VE.step(*label))

                def normalise(which, dst_scale, shift):
                    ve.wait_ge(*at(AC, "rstd", which))

                    def low(c):
                        ve.wait_ge(*at(AC, "hh", which, c))
                        nc.vector.tensor_tensor(hl[:, c, :], t[c % 2][:, :], hh[:, c, :].bitcast(F), ALU.subtract
                                                ).then_inc(*VE.step("h", which, c))

                    for c in range(C):
                        if c >= 2:
                            own()
                        nc.vector.tensor_tensor(t[c % 2][:, :], x[:, c, :], rstd[:, :], ALU.mult).then_inc(*VE.step())
                        own()
                        for g, toks in GROUPS:
                            nc.vector.tensor_scalar(t[c % 2][:, toks], t[c % 2][:, toks], dst_scale[:, c, g:g + 1],
                                                    mod[:, shift * C + c, g:g + 1], ALU.mult, ALU.add).then_inc(*VE.step())
                        VE.also("hfull", which, c)
                        if c >= 1:
                            low(c - 1)
                    low(C - 1)

                def y_out(job, which, gains, first):
                    for c in range(first, first + 4):
                        ve.wait_ge(*at(AC, "ysq", which, c))
                        for g, toks in GROUPS:
                            nc.vector.tensor_scalar(ybuf[:, c, toks], bank(job, c % 4)[:, toks], gains[:, c, g:g + 1], None, ALU.mult
                                                    ).then_inc(*VE.step())
                        VE.also("y", which, c)

                def residual_share(which):
                    ve.wait_ge(*at(AC, "rstd", which))
                    own()
                    residual(nc.vector, VE, at, ve.wait_ge, which)

                ve.wait_ge(*at(PE, "par", 0))
                nc.vector.tensor_copy(par[:, 0:NA], bank("par", 0)[:, 0:NA]).then_inc(*VE.step("par", 0))
                ve.wait_ge(*at(PE, "par", 1))
                nc.vector.tensor_copy(par[:, NA:NA + NB], bank("par", 1)[:, 0:NB]).then_inc(*VE.step("par", 1))
                own()
                first = par[:, 0:16].rearrange("p (g a) -> p g a", a=1).to_broadcast([P, 16, 2])
                nc.vector.tensor_tensor(mod[:, 0:16, :], mod[:, 0:16, :], first, ALU.add).then_inc(*VE.step())
                gain(scale1, 1, "g_pre_mix", 1.0, ("scale1",))
                normalise("pre1", scale1, 0)
                own()
                nc.vector.tensor_scalar(lam[3][:, :], par_cols("lru_lambda"), -1.0, None, ALU.mult).then_inc(*VE.step())
                own()
                nc.vector.tensor_tensor(lam[1][:, :], lam[3][:, :], par_cols("lru_lambda"), ALU.max).then_inc(*VE.step("abslam"))
                ve.wait_ge(*at(AC, "explam"))
                nc.vector.tensor_scalar(lam[2][:, :], lam[0][:, :], 1.0, None, ALU.add).then_inc(*VE.step("onelam"))
                ve.wait_ge(*at(AC, "lnlam"))
                own()
                nc.vector.tensor_scalar(lam[2][:, :], lam[2][:, :], -1.0, TINY, ALU.add, ALU.add).then_inc(*VE.step())
                nc.vector.tensor_scalar(lam[1][:, :], lam[1][:, :], TINY, None, ALU.add).then_inc(*VE.step())
                own()
                nc.vector.reciprocal(lam[2][:, :], lam[2][:, :]).then_inc(*VE.step())
                nc.vector.tensor_tensor(lam[0][:, :], lam[0][:, :], lam[1][:, :], ALU.mult).then_inc(*VE.step())
                own()
                nc.vector.tensor_tensor(lam[0][:, :], lam[0][:, :], lam[2][:, :], ALU.mult).then_inc(*VE.step())
                own()
                nc.vector.scalar_tensor_tensor(out=lam[3][:, :], in0=lam[3][:, :], scalar=0.0, in1=lam[0][:, :],
                                               op0=ALU.max, op1=ALU.add).then_inc(*VE.step())
                own()
                nc.vector.tensor_scalar(decay[:, :], lam[3][:, :], 8.0, None, ALU.mult).then_inc(*VE.step())
                nc.vector.tensor_scalar(ndecay[:, :], lam[3][:, :], -8.0, None, ALU.mult).then_inc(*VE.step("decay"))

                def xc_low(c):
                    ve.wait_ge(*at(AC, "xc_high", c))
                    nc.vector.tensor_tensor(xcl[:, c % 2, :], xc[:, c, :], xch[:, c % 2, :].bitcast(F), ALU.subtract
                                            ).then_inc(*VE.step("xc_low", c))

                for c in range(C):
                    if c % 4 == 0:
                        for k in range(c, c + 4):
                            ve.wait_ge(*at(AC, "conv", k))
                            nc.vector.tensor_copy(lruh[:, k, :], bank(f"lx{k // 4}", k % 4)[:, 0:T]).then_inc(*VE.step("lx", k))
                        if c == 4:
                            mod_result(4)
                    for i, (tap, off) in enumerate(((0, -2), (1, -1), (3, 1))):
                        for g, toks in GROUPS:
                            a, b = toks.start, toks.stop
                            dst = slice(a - min(off, 0), b - max(off, 0))
                            frm = slice(dst.start + off, dst.stop + off)
                            ve.wait_ge(VE.sem, l * VE.total + VE.count - (1 if i else 0) + VE.total)
                            nc.vector.scalar_tensor_tensor(out=xc[:, c, dst], in0=lruh[:, c, frm], scalar=par_col("conv_w", tap * C + c),
                                                           in1=xc[:, c, dst], op0=ALU.mult, op1=ALU.add).then_inc(*VE.step())
                    VE.also("conv", c)
                    if c == 3:
                        xc_low(0)
                        xc_low(1)
                        mod_partial(4)

                def scans(c, j):
                    b = c // 4
                    for d in range(2):
                        ve.wait_ge(*at(GP, "gated", c, d))
                        ve.wait_ge(*at(AC, "root", c, d))
                        nc.vector.tensor_tensor(i_[:, d, j, :], i_[:, d, j, :], tau[:, d, j, :], ALU.mult).then_inc(*VE.step())
                    own()
                    for g, toks in GROUPS:
                        init = 0.0 if g == 0 else par_col("state_lru_fwd", c)
                        nc.vector.tensor_tensor_scan(lruh[:, c, toks], r_[:, 0, j, toks], i_[:, 0, j, toks], init,
                                                     ALU.mult, ALU.add).then_inc(*VE.step())
                    for g, toks in GROUPS:
                        init = 0.0 if g == 0 else par_col("state_lru_bwd", c)
                        nc.vector.tensor_tensor_scan(tau[:, 1, j, toks][:, ::-1], r_[:, 1, j, toks][:, ::-1],
                                                     i_[:, 1, j, toks][:, ::-1], init, ALU.mult, ALU.add).then_inc(*VE.step())
                    own()
                    nc.vector.tensor_copy(hst[:, 0, c:c + 1], lruh[:, c, TP - 1:TP]).then_inc(*VE.step())
                    nc.vector.tensor_copy(hst[:, 1, c:c + 1], tau[:, 1, j, 0:1]).then_inc(*VE.step())
                    own()
                    nc.vector.tensor_tensor(lruh[:, c, :], lruh[:, c, :], tau[:, 1, j, :], ALU.add).then_inc(*VE.step("scan", c))

                def recurrence(b):
                    for j in range(4):
                        c = 4 * b + j
                        if c == 6:
                            mod_result(5)
                        if c >= 2:
                            xc_low(c)

                    def squared_root(c, j, d, e):
                        ve.wait_ge(*at(AC, "a", c, d))
                        nc.vector.tensor_tensor(t[e % 2][:, :], r_[:, d, j, :], r_[:, d, j, :], ALU.mult).then_inc(*VE.step())
                        own()
                        nc.vector.scalar_tensor_tensor(out=tau[:, d, j, :], in0=t[e % 2][:, :], scalar=1.0, in1=tau[:, d, j, :],
                                                       op0=ALU.add, op1=ALU.mult).then_inc(*VE.step("squared_root", c, d))

                    for j in range(4):
                        for d in range(2):
                            squared_root(4 * b + j, j, d, 2 * j + d)
                        if b == 0 and j == 3:
                            mod_partial(5)
                        if j >= 1:
                            scans(4 * b + j - 1, j - 1)
                    scans(4 * b + 3, 3)

                recurrence(0)
                recurrence(1)
                VE.also("states")
                ve.wait_ge(*at(AC, "rstd", "q"))
                for k in range(QC):
                    nc.vector.scalar_tensor_tensor(out=qkv[:, k, :], in0=qkv[:, k, :], scalar=par_col("g_q", k), in1=rstd[:, :],
                                                   op0=ALU.mult, op1=ALU.mult).then_inc(*VE.step("qfull_c", k))
                VE.also("qfull")
                ve.wait_ge(*at(AC, "rstd", "kv"))
                for k in range(KC):
                    nc.vector.scalar_tensor_tensor(out=qkv[:, QC + k, :], in0=qkv[:, QC + k, :], scalar=par_col("g_kv", k),
                                                   in1=sq[0][:, :], op0=ALU.mult, op1=ALU.mult).then_inc(*VE.step("ckv_full", k))
                for k in range(QC):
                    ve.wait_ge(*at(AC, "qn_high", k))
                    nc.vector.tensor_tensor(qnl[:, k, :], qkv[:, k, :], qnh[:, k, :].bitcast(F), ALU.subtract
                                            ).then_inc(*VE.step("qn", k))
                for k in range(KC):
                    ve.wait_ge(*at(AC, "ckv_high", k))
                    nc.vector.tensor_tensor(cl[:, k, 0:T], qkv[:, QC + k, :], ch[:, k, 0:T].bitcast(F), ALU.subtract
                                            ).then_inc(*VE.step("ckv", k))
                mod_partial(6)
                ve.wait_ge(*at(PE, "krot"))
                nc.vector.tensor_copy(kr[:, 0:TP], bank("small", 2)[:, 0:TP]).then_inc(*VE.step())
                nc.vector.tensor_tensor(kr[:, TP:T], bank("small", 2)[:, TP:T], cos[:, :], ALU.mult).then_inc(*VE.step())
                nc.vector.tensor_tensor(t[0][:, 0:TS], bank("small", 3)[:, 0:TS], sin[:, :], ALU.mult).then_inc(*VE.step("krot"))
                own()
                nc.vector.tensor_tensor(kr[:, TP:T], kr[:, TP:T], t[0][:, 0:TS], ALU.add).then_inc(*VE.step())
                ve.wait_ge(*at(AC, "cache_high"))
                for k in range(KC):
                    nc.vector.tensor_tensor(cl[:, k, T:TK], bank("small", 0)[:, k * P:k * P + P], ch[:, k, T:TK].bitcast(F),
                                            ALU.subtract).then_inc(*VE.step())
                VE.also("ckv_cache")
                nc.vector.tensor_copy(kr[:, T:TK], bank("small", 1)[:, 0:P]).then_inc(*VE.step("cache"))
                mod_result(6)
                mod_partial(7)
                mod_result(7)
                mod_partial(8)
                ve.wait_ge(*at(PE, "m1b", 3))

                def lru_low(c):
                    ve.wait_ge(*at(AC, "lru_high", c))
                    nc.vector.tensor_tensor(hl[:, c, :], t[c % 2][:, :], hh[:, c, :].bitcast(F), ALU.subtract
                                            ).then_inc(*VE.step("lru_low", c))

                for c in range(C):
                    own()
                    nc.vector.tensor_tensor(t[c % 2][:, :], lruh[:, c, :], ybuf[:, c, :], ALU.mult).then_inc(*VE.step("lru_full", c))
                    if c >= 1:
                        lru_low(c - 1)
                lru_low(C - 1)
                for j in range(2):
                    ve.wait_ge(*at(PE, "qrot", j))
                    own()
                    nc.vector.tensor_tensor(t[j][:, 0:TS], bank("qrot", j)[:, 0:TS], sin[:, :], ALU.mult).then_inc(*VE.step())
                    nc.vector.tensor_tensor(qr[:, j, TP:T], qr[:, j, TP:T], cos[:, :], ALU.mult).then_inc(*VE.step())
                    own()
                    nc.vector.tensor_tensor(qr[:, j, TP:T], qr[:, j, TP:T], t[j][:, 0:TS], ALU.add).then_inc(*VE.step())
                VE.also("qrot")

                def mix_lru(b):
                    for c in range(4 * b, 4 * b + 4):
                        ve.wait_ge(*at(PE, f"ol{b}", c % 4))
                        nc.vector.tensor_tensor(ybuf[:, c, :], bank(f"ol{b}", c % 4)[:, 0:T], m2[:, c, :], ALU.mult
                                                ).then_inc(*VE.step("mix_lru", c))

                def divide(s):
                    n = TP if s % 3 == 0 else TK - TP
                    ve.wait_ge(*at(AC, "exp", s))
                    nc.vector.reciprocal(prec[:, s % 2:s % 2 + 1], psums[:, s % 2:s % 2 + 1]).then_inc(*VE.step())
                    own()
                    nc.vector.tensor_scalar(sq[s % 2][:, 0:n], sq[s % 2][:, 0:n], prec[:, s % 2:s % 2 + 1], None, ALU.mult
                                            ).then_inc(*VE.step("probs", s))

                def out_low(g):
                    ve.wait_ge(*at(AC, "o_high", g))
                    nc.vector.tensor_tensor(ol[:, g, :], bank("attn", 3)[:, 0:T], oh[:, g, :].bitcast(F), ALU.subtract
                                            ).then_inc(*VE.step("o_low", g))

                for s in range(24):
                    n = TP if s % 3 == 0 else TK - TP
                    ve.wait_ge(*at(PE, "scores", s))
                    nc.vector.tensor_reduce(negmax[:, s % 2:s % 2 + 1], bank("attn", s % 2)[:, 0:n], AX.X, ALU.max, negate=True
                                            ).then_inc(*VE.step("max", s))
                    if s >= 8 and (s - 8) % 6 == 0:
                        out_low((s - 8) // 6)
                    if s >= 1:
                        divide(s - 1)
                    if s == 12:
                        mix_lru(0)
                        mod_result(8)
                divide(23)
                out_low(3)
                mix_lru(1)

                def mix_low(c):
                    ve.wait_ge(*at(AC, "mix_high", c))
                    nc.vector.tensor_tensor(hl[:, c, :], ybuf[:, c, :], hh[:, c, :].bitcast(F), ALU.subtract
                                            ).then_inc(*VE.step("mix_low", c))

                for c in range(C):
                    ve.wait_ge(*at(PE, f"om{c // 4}", c % 4))
                    if c >= 2:
                        own()
                    nc.vector.tensor_tensor(t[c % 2][:, :], bank(f"om{c // 4}", c % 4)[:, 0:T], m1[:, c, :], ALU.mult
                                            ).then_inc(*VE.step())
                    own()
                    nc.vector.tensor_tensor(ybuf[:, c, :], ybuf[:, c, :], t[c % 2][:, :], ALU.add).then_inc(*VE.step("mix", c))
                    if c >= 1:
                        mix_low(c - 1)
                mix_low(C - 1)
                gain(gain1, 2, "g_post_mix", 0.0, ("gain1",))
                own()
                y_out("wo0", "post1", gain1, 0)
                mod_partial(9)
                y_out("wo1", "post1", gain1, 4)
                mod_result(9)
                residual_share("post1")
                gain(scale2, 4, "g_pre_ffn", 1.0, ("scale2",))
                own()
                normalise("pre2", scale2, 3)

                def hid_low(c):
                    ve.wait_ge(*at(AC, "hid_high", c))
                    nc.vector.tensor_tensor(hidl[:, c, :], t[c % 2][:, :], hidh[:, c, :].bitcast(F), ALU.subtract
                                            ).then_inc(*VE.step("hid_low", c))

                for j in range(FC // 2):
                    for g in range(2):
                        c = 2 * j + g
                        ve.wait_ge(*at(AC, "silu", c))
                        ve.wait_ge(*at(PE, f"fi{j}", 2 + g))
                        own()
                        nc.vector.tensor_tensor(t[c % 2][:, :], bank(f"fi{j}", 2 + g)[:, 0:T], sq[c % 4][:, :], ALU.mult
                                                ).then_inc(*VE.step("hid", c))
                    for g in range(2):
                        c = 2 * j + g
                        if c == out_at // TB - FC:
                            ve.wait_ge(*at(stored, "all"))
                        hid_low(c)
                    if f"fi{j}" in HOSTED:
                        mod_partial(HOSTED[f"fi{j}"])
                    if f"fi{j}" in FOLDED:
                        mod_result(FOLDED[f"fi{j}"])
                    if j == 3:
                        gain(gain2, 5, "g_post_ffn", 0.0, ("gain2",))
                own()
                y_out("fo0", "post2", gain2, 0)
                mod_result(FOLDED["fo0"])
                y_out("fo1", "post2", gain2, 4)
                residual_share("post2")

            for a in range(6):
                ve.wait_ge(end_pe, a + 1)
                tok = ybuf[:, :, :].rearrange("p c t -> p (c t)")
                nc.vector.tensor_copy(tok[:, a * 512:a * 512 + 512], ps[a][:, :]).then_inc(end_ve, 1)

    return {n: (s.labels, s.count) for n, s in new_plan.items()}


_INS = ["x_prompt", "x_sample", "cache_ckv", "cache_krope", "state_lru_fwd", "state_lru_bwd", "c", "c_ctx", "w_mod", "b_mod",
        "g_pre_mix", "g_post_mix", "g_pre_ffn", "g_post_ffn", "w_in", "g_q", "w_q_up", "g_kv", "w_kv_up", "w_o_mla",
        "conv_w", "conv_b", "w_rg", "b_rg", "w_ig", "b_ig", "lru_lambda", "w_o_lru", "w_out", "w_ffn_in", "w_ffn_out"]
_OUTS = [("y_prompt", (1, TP, D)), ("y_sample", (1, TS, D)), ("new_ckv", (1, DEPTH, TP, KVL)),
         ("new_krope", (1, DEPTH, TP, ROPE)), ("new_lru_fwd", (1, DEPTH, LRU)), ("new_lru_bwd", (1, DEPTH, LRU))]


def constants():
    n = ROPE // 4
    inv = np.float32(10000.0) ** (-np.arange(n, dtype=np.float32) / np.float32(n))
    tok = np.arange(TS)
    row, col = (tok // GRID_W).astype(np.float32), (tok % GRID_W).astype(np.float32)
    ang = np.concatenate([row[:, None] * inv, col[:, None] * inv], axis=-1).astype(np.float32)
    ang = np.tile(ang.T, (2 * P // ROPE, 1))
    half = ROPE // 2
    turn = np.zeros((ROPE, ROPE), np.float32)
    for m in range(half):
        turn[m + half, m] = -1.0
        turn[m, m + half] = 1.0
    k = P // ROPE
    return {"ident": np.eye(P, dtype=np.float32), "rot": np.kron(np.eye(k, dtype=np.float32), turn),
            "rep": np.tile(np.eye(ROPE, dtype=np.float32), (k, k)), "reprot": np.tile(turn, (k, k)),
            "fold": np.tile(np.eye(32, 2, dtype=np.float32), (P // 32, 1)), "cos": np.cos(ang).astype(np.float32), "sin": np.sin(ang).astype(np.float32)}


def tensors(nc, arrays):
    A = {n: nc.dram_tensor(f"in_{n}", a.shape, F, kind="ExternalInput").ap() for n, a in arrays.items()}
    A.update({n: nc.dram_tensor(f"out_{n}", shape, F, kind="ExternalOutput").ap() for n, shape in _OUTS})
    return A


def kernel(**inputs):
    import concourse.bacc as _bacc
    from concourse.bass_utils import run_bass_kernel_spmd as _run

    arrays = {n: np.ascontiguousarray(inputs[n]) for n in _INS}
    arrays.update(constants())
    plan = {}
    for _ in range(2):
        nc = _bacc.Bacc("TRN2", target_bir_lowering=False, num_devices=1)
        plan = program(nc, tensors(nc, arrays), plan)
    r = _run(nc, [{f"in_{n}": a for n, a in arrays.items()}], core_ids=[0])
    return tuple(r.results[0][f"out_{n}"] for n, _ in _OUTS)
```
